# Optimizing a Trainium2 kernel written in Bass

```python
import math
import jax
import jax.numpy as jnp
from jax import lax
import numpy as np
import jax, jax.numpy as jnp

D_MODEL = 1024
BATCH = 1
SEQ = 256
DEPTH = 2

GRID_W = 64
CTX_LEN = 256
EPS = 1e-6

MLSTM_HEADS = 8
MLSTM_DQK = 64
MLSTM_DV = 64
MLSTM_CONV = 3
MLSTM_CHUNK = 64
DIFF_HEADS = 4
DIFF_DQK = 64
DIFF_DV = 128
ROPE_BASE = 10000.0
Q_BLOCK = 128
CONV_WIDTH = 31
D_FF = 2816
N_EXPERTS = 8
TOP_K = 2
D_FF_EXPERT = 2816
MOE_BLOCK = 128

MQK = MLSTM_HEADS * MLSTM_DQK
MV = MLSTM_HEADS * MLSTM_DV
MG = 4 * MLSTM_HEADS
DQK = DIFF_HEADS * 2 * DIFF_DQK
DVW = DIFF_HEADS * DIFF_DV
OFF_MQ = 0
OFF_MK = OFF_MQ + MQK
OFF_MV = OFF_MK + MQK
OFF_MO = OFF_MV + MV
OFF_MG = OFF_MO + MV
OFF_DQ = OFF_MG + MG
OFF_DK = OFF_DQ + DQK
OFF_DV = OFF_DK + DQK
IN0_WIDTH = OFF_DV + DVW
MIX0_WIDTH = MV + DVW


F32 = jnp.float32

def rmsnorm(x, g):
    xf = x.astype(F32)
    y = xf * lax.rsqrt(jnp.mean(xf * xf, axis=-1, keepdims=True) + EPS)
    return (y * g.astype(F32)).astype(x.dtype)

def layernorm(x, g, b):
    xf = x.astype(F32)
    mu = jnp.mean(xf, axis=-1, keepdims=True)
    var = jnp.mean(jnp.square(xf - mu), axis=-1, keepdims=True)
    return ((xf - mu) * lax.rsqrt(var + EPS) * g.astype(F32) + b.astype(F32)).astype(x.dtype)

def adaln(cond, w, b):
    return jax.nn.silu(cond) @ w + b

def modulate(x, g, shift, scale):
    return rmsnorm(x, g) * (1 + scale) + shift

def depthwise_conv(x, w):
    k = w.shape[0]
    return lax.conv_general_dilated(
        x, w[:, None, :].astype(x.dtype), window_strides=(1,),
        padding=[((k - 1) // 2, k // 2)], dimension_numbers=('NWC', 'WIO', 'NWC'),
        feature_group_count=x.shape[-1])

def to_heads(a, n_heads):
    b, t, _ = a.shape
    return a.reshape(b, t, n_heads, -1).transpose(0, 2, 1, 3)

def axial_rope_tables(t_len):
    rows = t_len // GRID_W
    row = jnp.repeat(jnp.arange(rows, dtype=F32), GRID_W)
    col = jnp.tile(jnp.arange(GRID_W, dtype=F32), rows)
    axis_dim = DIFF_DQK // 2
    inv = ROPE_BASE ** (-jnp.arange(0, axis_dim, 2, dtype=F32) / axis_dim)
    ang_r = row[:, None] * inv
    ang_c = col[:, None] * inv
    return jnp.cos(ang_r), jnp.sin(ang_r), jnp.cos(ang_c), jnp.sin(ang_c)

def rotate(x, cos, sin):
    x1, x2 = jnp.split(x, 2, axis=-1)
    return jnp.concatenate([x1 * cos - x2 * sin, x2 * cos + x1 * sin], axis=-1)

def apply_axial_rope(x, tables):
    cr, sr, cc, sc = tables
    xr, xc = jnp.split(x.astype(F32), 2, axis=-1)
    return jnp.concatenate([rotate(xr, cr, sr), rotate(xc, cc, sc)], axis=-1).astype(x.dtype)

def mlstm_gates(g, gate_b):
    g = (g + gate_b).astype(F32)
    b, t, _ = g.shape
    g = g.reshape(b, t, 4, MLSTM_HEADS).transpose(2, 0, 3, 1)
    return g[0], jax.nn.log_sigmoid(g[1]), g[2], jax.nn.log_sigmoid(g[3])

def mlstm_state_update(C, n, m, k, v, ig, b):
    b_last = b[..., -1]
    log_s = b_last[..., None] - b + ig
    m_new = jnp.maximum(b_last + m, jnp.max(log_s, axis=-1))
    ws = jnp.exp(log_s - m_new[..., None])
    decay = jnp.exp(b_last + m - m_new)
    C_new = decay[..., None, None] * C + jnp.einsum('bhs,bhsd,bhse->bhde', ws, k, v)
    n_new = decay[..., None] * n + jnp.einsum('bhs,bhsd->bhd', ws, k)
    return C_new, n_new, m_new

def mlstm_chunk(carry, inp):
    C, n, m = carry
    q, k, v, ig, lf = inp
    L = q.shape[2]
    b = jnp.cumsum(lf, axis=-1)
    order = jnp.tril(jnp.ones((L, L), dtype=bool))
    log_d = jnp.where(order, b[..., :, None] - b[..., None, :] + ig[..., None, :], -jnp.inf)
    log_inter = b + m[..., None]
    m_t = jnp.maximum(log_inter, jnp.max(log_d, axis=-1))
    s = jnp.einsum('bhtd,bhsd->bhts', q, k) * jnp.exp(log_d - m_t[..., None])
    w_inter = jnp.exp(log_inter - m_t)
    num = w_inter[..., None] * jnp.einsum('bhtd,bhde->bhte', q, C) + jnp.einsum('bhts,bhse->bhte', s, v)
    den = w_inter * jnp.einsum('bhtd,bhd->bht', q, n) + jnp.sum(s, axis=-1)
    h = num / jnp.maximum(jnp.abs(den), jnp.exp(-m_t))[..., None]
    return mlstm_state_update(C, n, m, k, v, ig, b), h

def mlstm_scan(q, k, v, ig, lf, state):
    b, h, t, _ = q.shape
    nc = t // MLSTM_CHUNK

    def chunks(a):
        return jnp.moveaxis(a.reshape(a.shape[:2] + (nc, MLSTM_CHUNK) + a.shape[3:]), 2, 0)

    _, out = lax.scan(mlstm_chunk, state, (chunks(q), chunks(k), chunks(v), chunks(ig), chunks(lf)))
    return jnp.moveaxis(out, 0, 2).reshape(b, h, t, -1)

def mlstm_context_state(k, v, ig, lf):
    b, h, _, dk = k.shape
    C0 = jnp.zeros((b, h, dk, v.shape[-1]), F32)
    n0 = jnp.zeros((b, h, dk), F32)
    m0 = jnp.zeros((b, h), F32)
    return mlstm_state_update(C0, n0, m0, k, v, ig, jnp.cumsum(lf, axis=-1))

def mlstm_mixer(q, k, v, o, ig_f, lf_f, ig_b, lf_b, k_c, v_c, igc_f, lfc_f, igc_b, lfc_b, norm_g):
    H = MLSTM_HEADS
    B_, T_, _ = q.shape
    q = to_heads(q, H).astype(F32) * (MLSTM_DQK ** -0.5)
    k = to_heads(k, H).astype(F32)
    v = to_heads(v, H).astype(F32)
    k_c = to_heads(k_c, H).astype(F32)
    v_c = to_heads(v_c, H).astype(F32)
    st_f = mlstm_context_state(k_c, v_c, igc_f, lfc_f)
    st_b = mlstm_context_state(jnp.flip(k_c, 2), jnp.flip(v_c, 2), jnp.flip(igc_b, -1), jnp.flip(lfc_b, -1))
    h_f = mlstm_scan(q, k, v, ig_f, lf_f, st_f)
    h_b = jnp.flip(mlstm_scan(jnp.flip(q, 2), jnp.flip(k, 2), jnp.flip(v, 2),
                              jnp.flip(ig_b, -1), jnp.flip(lf_b, -1), st_b), 2)
    h = (h_f + h_b).transpose(0, 2, 1, 3)
    h = rmsnorm(h, norm_g.reshape(H, MLSTM_DV)).reshape(B_, T_, MV)
    return (h * jax.nn.sigmoid(o.astype(F32))).astype(o.dtype)

def diff_attention_blocks(q1, q2, k1_all, k2_all, v_all, lam):
    B_, H, T_, d = q1.shape
    nb = T_ // Q_BLOCK
    scale = DIFF_DQK ** -0.5

    def blocks(a):
        return a.reshape(B_, H, nb, Q_BLOCK, d).transpose(2, 0, 1, 3, 4)

    def one_block(qs):
        a1, a2 = qs
        s1 = jnp.einsum('bhqd,bhkd->bhqk', a1, k1_all).astype(F32) * scale
        s2 = jnp.einsum('bhqd,bhkd->bhqk', a2, k2_all).astype(F32) * scale
        p = jax.nn.softmax(s1, axis=-1) - lam * jax.nn.softmax(s2, axis=-1)
        return jnp.einsum('bhqk,bhkv->bhqv', p.astype(v_all.dtype), v_all)

    out = lax.map(one_block, (blocks(q1), blocks(q2)))
    return out.transpose(1, 2, 0, 3, 4).reshape(B_, H, T_, -1)

def diff_mixer(q, k, v, k_c, v_c, lq1, lk1, lq2, lk2, norm_g, layer_idx):
    H = DIFF_HEADS
    B_, T_, _ = q.shape

    def split_qk(a):
        a = a.reshape(a.shape[0], a.shape[1], H, 2, DIFF_DQK)
        return a[..., 0, :].transpose(0, 2, 1, 3), a[..., 1, :].transpose(0, 2, 1, 3)

    tables = axial_rope_tables(T_)
    q1, q2 = [apply_axial_rope(a, tables) for a in split_qk(q)]
    k1, k2 = [apply_axial_rope(a, tables) for a in split_qk(k)]
    k1c, k2c = split_qk(k_c)
    k1_all = jnp.concatenate([k1c, k1], axis=2)
    k2_all = jnp.concatenate([k2c, k2], axis=2)
    v_all = jnp.concatenate([to_heads(v_c, H), to_heads(v, H)], axis=2)
    lam_init = 0.8 - 0.6 * math.exp(-0.3 * layer_idx)
    lam = (jnp.exp(jnp.sum(lq1.astype(F32) * lk1.astype(F32)))
           - jnp.exp(jnp.sum(lq2.astype(F32) * lk2.astype(F32))) + lam_init)
    o = diff_attention_blocks(q1, q2, k1_all, k2_all, v_all, lam).transpose(0, 2, 1, 3)
    o = rmsnorm(o, norm_g.reshape(H, DIFF_DV)) * (1.0 - lam_init)
    return o.reshape(B_, T_, DVW)

def swiglu(u, w1, w3, w2):
    return (jax.nn.silu(u @ w1) * (u @ w3)) @ w2

def moe_swiglu(u, router_w, w1, w3, w2):
    B_, T_, D = u.shape
    tokens = u.reshape(-1, D)
    N = tokens.shape[0]
    logits = (tokens @ router_w).astype(F32)
    top_vals, top_idx = lax.top_k(logits, TOP_K)
    gates = jax.nn.softmax(top_vals, axis=-1)
    A = N * TOP_K
    flat_e = top_idx.reshape(-1)
    flat_tok = jnp.repeat(jnp.arange(N, dtype=jnp.int32), TOP_K)
    flat_g = gates.reshape(-1)
    order = jnp.argsort(flat_e)
    s_e, s_tok, s_g = flat_e[order], flat_tok[order], flat_g[order]
    counts = jnp.bincount(flat_e, length=N_EXPERTS)
    starts = jnp.cumsum(counts) - counts
    padded = ((counts + MOE_BLOCK - 1) // MOE_BLOCK) * MOE_BLOCK
    pends = jnp.cumsum(padded)
    pstarts = pends - padded
    dest = pstarts[s_e] + (jnp.arange(A) - starts[s_e])
    n_blk = (A + MOE_BLOCK - 1) // MOE_BLOCK + N_EXPERTS
    R = n_blk * MOE_BLOCK
    slot_tok = jnp.zeros((R,), jnp.int32).at[dest].set(s_tok)
    slot_g = jnp.zeros((R,), F32).at[dest].set(s_g)
    block_e = jnp.clip(jnp.searchsorted(pends, jnp.arange(n_blk) * MOE_BLOCK, side='right'), 0, N_EXPERTS - 1)

    def run_block(args):
        tok_idx, e = args
        xb = tokens[tok_idx]
        return (jax.nn.silu(xb @ w1[e]) * (xb @ w3[e])) @ w2[e]

    y = lax.map(run_block, (slot_tok.reshape(n_blk, MOE_BLOCK), block_e)).reshape(R, D)
    y = y * slot_g[:, None].astype(y.dtype)
    out = jnp.zeros((N, D), y.dtype).at[slot_tok].add(y)
    return out.reshape(B_, T_, D)

def even_layer(x, c, ctx, c_ctx, layer_idx, mod_w, mod_b, mix_pre_g, mix_post_g, w_in, mlstm_gate_b,
               mlstm_conv_w, mlstm_norm_g, lambda_q1, lambda_k1, lambda_q2, lambda_k2, diff_norm_g,
               w_out, ffn_pre_g, ffn_post_g, ffn_w1, ffn_w3, ffn_w2):
    sh_m, sc_m, gt_m, sh_f, sc_f, gt_f = jnp.split(adaln(c, mod_w, mod_b)[:, None, :], 6, axis=-1)
    sh_c, sc_c = jnp.split(adaln(c_ctx, mod_w, mod_b), 6, axis=-1)[:2]
    u = modulate(x, mix_pre_g, sh_m, sc_m)
    p = u @ w_in
    q_m = jax.nn.silu(depthwise_conv(p[..., OFF_MQ:OFF_MK], mlstm_conv_w[:, :MQK]))
    k_m = jax.nn.silu(depthwise_conv(p[..., OFF_MK:OFF_MV], mlstm_conv_w[:, MQK:]))
    v_m = p[..., OFF_MV:OFF_MO]
    o_m = p[..., OFF_MO:OFF_MG]
    ig_f, lf_f, ig_b, lf_b = mlstm_gates(p[..., OFF_MG:OFF_DQ], mlstm_gate_b)
    uc = modulate(ctx, mix_pre_g, sh_c, sc_c)
    kv_mc = uc @ w_in[:, OFF_MK:OFF_MO]
    k_mc = jax.nn.silu(depthwise_conv(kv_mc[..., :MQK], mlstm_conv_w[:, MQK:]))
    v_mc = kv_mc[..., MQK:]
    igc_f, lfc_f, igc_b, lfc_b = mlstm_gates(uc @ w_in[:, OFF_MG:OFF_DQ], mlstm_gate_b)
    kv_dc = uc @ w_in[:, OFF_DK:]
    h_m = mlstm_mixer(q_m, k_m, v_m, o_m, ig_f, lf_f, ig_b, lf_b,
                      k_mc, v_mc, igc_f, lfc_f, igc_b, lfc_b, mlstm_norm_g)
    h_d = diff_mixer(p[..., OFF_DQ:OFF_DK], p[..., OFF_DK:OFF_DV], p[..., OFF_DV:],
                     kv_dc[..., :DQK], kv_dc[..., DQK:],
                     lambda_q1, lambda_k1, lambda_q2, lambda_k2, diff_norm_g, layer_idx)
    mix = jnp.concatenate([h_m, h_d], axis=-1) @ w_out
    x = x + gt_m * rmsnorm(mix, mix_post_g)
    y = swiglu(modulate(x, ffn_pre_g, sh_f, sc_f), ffn_w1, ffn_w3, ffn_w2)
    return x + gt_f * rmsnorm(y, ffn_post_g)

def odd_layer(x, c, mod_w, mod_b, mix_pre_g, mix_post_g, pw1_w, pw1_b, dw_w, dw_b, ln_g, ln_b,
              pw2_w, pw2_b, ffn_pre_g, ffn_post_g, router_w, moe_w1, moe_w3, moe_w2):
    sh_m, sc_m, gt_m, sh_f, sc_f, gt_f = jnp.split(adaln(c, mod_w, mod_b)[:, None, :], 6, axis=-1)
    u = modulate(x, mix_pre_g, sh_m, sc_m)
    a, g = jnp.split(u @ pw1_w + pw1_b, 2, axis=-1)
    h = a * jax.nn.sigmoid(g)
    h = depthwise_conv(h, dw_w) + dw_b
    h = jax.nn.silu(layernorm(h, ln_g, ln_b))
    y = h @ pw2_w + pw2_b
    x = x + gt_m * rmsnorm(y, mix_post_g)
    y = moe_swiglu(modulate(x, ffn_pre_g, sh_f, sc_f), router_w, moe_w1, moe_w3, moe_w2)
    return x + gt_f * rmsnorm(y, ffn_post_g)

def first_inputs(seed: int = 0) -> dict:
    key = jax.random.key(seed)
    keys = list(jax.random.split(key, 48))
    D = D_MODEL

    def nrm(shape, scale):
        return jax.random.normal(keys.pop(), shape, F32) * scale

    def gain(n):
        return 1.0 + nrm((n,), 0.05)

    inp = {}
    inp['x'] = nrm((BATCH, SEQ, D), 1.0)
    inp['c'] = nrm((BATCH, D), 1.0)
    inp['ctx'] = nrm((BATCH, CTX_LEN, D), 1.0)
    inp['c_ctx'] = nrm((D,), 1.0)
    inp['l0_mod_w'] = nrm((D, 6 * D), 0.5 * D ** -0.5)
    inp['l0_mod_b'] = nrm((6 * D,), 0.02)
    inp['l0_mix_pre_g'] = gain(D)
    inp['l0_mix_post_g'] = gain(D)
    inp['l0_w_in'] = nrm((D, IN0_WIDTH), D ** -0.5)
    gate_offsets = jnp.concatenate([
        jnp.full((MLSTM_HEADS,), -1.0, F32), jnp.linspace(3.0, 6.0, MLSTM_HEADS, dtype=F32),
        jnp.full((MLSTM_HEADS,), -1.0, F32), jnp.linspace(3.0, 6.0, MLSTM_HEADS, dtype=F32)])
    inp['l0_mlstm_gate_b'] = gate_offsets + nrm((MG,), 0.1)
    inp['l0_mlstm_conv_w'] = nrm((MLSTM_CONV, 2 * MQK), MLSTM_CONV ** -0.5)
    inp['l0_mlstm_norm_g'] = gain(MV)
    inp['l0_lambda_q1'] = nrm((DIFF_DQK,), 0.1)
    inp['l0_lambda_k1'] = nrm((DIFF_DQK,), 0.1)
    inp['l0_lambda_q2'] = nrm((DIFF_DQK,), 0.1)
    inp['l0_lambda_k2'] = nrm((DIFF_DQK,), 0.1)
    inp['l0_diff_norm_g'] = gain(DVW)
    inp['l0_w_out'] = nrm((MIX0_WIDTH, D), MIX0_WIDTH ** -0.5)
    inp['l0_ffn_pre_g'] = gain(D)
    inp['l0_ffn_post_g'] = gain(D)
    inp['l0_ffn_w1'] = nrm((D, D_FF), D ** -0.5)
    inp['l0_ffn_w3'] = nrm((D, D_FF), D ** -0.5)
    inp['l0_ffn_w2'] = nrm((D_FF, D), D_FF ** -0.5)
    inp['l1_mod_w'] = nrm((D, 6 * D), 0.5 * D ** -0.5)
    inp['l1_mod_b'] = nrm((6 * D,), 0.02)
    inp['l1_mix_pre_g'] = gain(D)
    inp['l1_mix_post_g'] = gain(D)
    inp['l1_conv_pw1_w'] = nrm((D, 2 * D), D ** -0.5)
    inp['l1_conv_pw1_b'] = nrm((2 * D,), 0.02)
    inp['l1_conv_dw_w'] = nrm((CONV_WIDTH, D), CONV_WIDTH ** -0.5)
    inp['l1_conv_dw_b'] = nrm((D,), 0.02)
    inp['l1_conv_ln_g'] = gain(D)
    inp['l1_conv_ln_b'] = nrm((D,), 0.02)
    inp['l1_conv_pw2_w'] = nrm((D, D), D ** -0.5)
    inp['l1_conv_pw2_b'] = nrm((D,), 0.02)
    inp['l1_ffn_pre_g'] = gain(D)
    inp['l1_ffn_post_g'] = gain(D)
    inp['l1_router_w'] = nrm((D, N_EXPERTS), D ** -0.5)
    inp['l1_moe_w1'] = nrm((N_EXPERTS, D, D_FF_EXPERT), D ** -0.5)
    inp['l1_moe_w3'] = nrm((N_EXPERTS, D, D_FF_EXPERT), D ** -0.5)
    inp['l1_moe_w2'] = nrm((N_EXPERTS, D_FF_EXPERT, D), D_FF_EXPERT ** -0.5)
    return inp

def first_block(x, c, ctx, c_ctx,
              l0_mod_w, l0_mod_b, l0_mix_pre_g, l0_mix_post_g, l0_w_in, l0_mlstm_gate_b,
              l0_mlstm_conv_w, l0_mlstm_norm_g, l0_lambda_q1, l0_lambda_k1, l0_lambda_q2,
              l0_lambda_k2, l0_diff_norm_g, l0_w_out, l0_ffn_pre_g, l0_ffn_post_g,
              l0_ffn_w1, l0_ffn_w3, l0_ffn_w2,
              l1_mod_w, l1_mod_b, l1_mix_pre_g, l1_mix_post_g, l1_conv_pw1_w, l1_conv_pw1_b,
              l1_conv_dw_w, l1_conv_dw_b, l1_conv_ln_g, l1_conv_ln_b, l1_conv_pw2_w,
              l1_conv_pw2_b, l1_ffn_pre_g, l1_ffn_post_g, l1_router_w, l1_moe_w1, l1_moe_w3,
              l1_moe_w2):
    layer_params = (
        (l0_mod_w, l0_mod_b, l0_mix_pre_g, l0_mix_post_g, l0_w_in, l0_mlstm_gate_b,
         l0_mlstm_conv_w, l0_mlstm_norm_g, l0_lambda_q1, l0_lambda_k1, l0_lambda_q2,
         l0_lambda_k2, l0_diff_norm_g, l0_w_out, l0_ffn_pre_g, l0_ffn_post_g,
         l0_ffn_w1, l0_ffn_w3, l0_ffn_w2),
        (l1_mod_w, l1_mod_b, l1_mix_pre_g, l1_mix_post_g, l1_conv_pw1_w, l1_conv_pw1_b,
         l1_conv_dw_w, l1_conv_dw_b, l1_conv_ln_g, l1_conv_ln_b, l1_conv_pw2_w,
         l1_conv_pw2_b, l1_ffn_pre_g, l1_ffn_post_g, l1_router_w, l1_moe_w1, l1_moe_w3,
         l1_moe_w2),
    )
    for layer in range(DEPTH):
        if layer % 2 == 0:
            x = even_layer(x, c, ctx, c_ctx, layer, *layer_params[layer])
        else:
            x = odd_layer(x, c, *layer_params[layer])
    return x


CHUNK = 64
N_MIXERS = 2
MIX_WIDTH = D_MODEL // 2
SGU_CHUNK = 128
SGU_HEADS = 4
SGU_HEAD_DIM = MIX_WIDTH // SGU_HEADS
CONV_WIDTH_2 = 3
N_MEM = 256
XA_HEADS = 4
XA_HEAD_DIM = MIX_WIDTH // XA_HEADS
N_EXPERTS_2 = 16
N_GROUPS = 4
GROUP_SIZE = N_EXPERTS_2 // N_GROUPS
D_EXPERT = D_MODEL // 2
N_A = (DEPTH + 1) // 2
N_B = DEPTH // 2
ALPHA = (2 * DEPTH) ** 0.25
BETA = (8 * DEPTH) ** -0.25
LN_EPS = 1e-5


def layer_norm(x, g, b):
    xf = x.astype(jnp.float32)
    mu = xf.mean(-1, keepdims=True)
    var = jnp.square(xf - mu).mean(-1, keepdims=True)
    y = (xf - mu) * lax.rsqrt(var + LN_EPS) * g.astype(jnp.float32) + b.astype(jnp.float32)
    return y.astype(x.dtype)

def spatial_gating(z, ln_g, ln_b, w_s, b_s):
    u, v = jnp.split(z, 2, axis=-1)
    v = layer_norm(v, ln_g, ln_b)
    bsz, seq, _ = v.shape
    v = v.reshape(bsz, seq // SGU_CHUNK, SGU_CHUNK, SGU_HEADS, SGU_HEAD_DIM)
    frame_chunk = jnp.arange(SGU_CHUNK) // CHUNK
    mask = frame_chunk[:, None] >= frame_chunk[None, :]
    w = jnp.where(mask[None], w_s, jnp.zeros_like(w_s))
    mixed = jnp.einsum('hij,bcjhd->bcihd', w, v) + b_s.T[None, None, :, :, None]
    return u * mixed.reshape(bsz, seq, MIX_WIDTH)

def short_conv_mixer(z, conv_w):
    bg, cg, xt = jnp.split(z, 3, axis=-1)
    h = cg * xt
    h = lax.conv_general_dilated(
        h, conv_w[:, None, :].astype(h.dtype), window_strides=(1,),
        padding=[(CONV_WIDTH_2 - 1, 0)], dimension_numbers=('NWC', 'WIO', 'NWC'),
        feature_group_count=MIX_WIDTH)
    return bg * h

def memory_cross_attention(q, mem, w_kv):
    bsz, seq, _ = q.shape
    n_mem = mem.shape[1]
    k, v = jnp.split(mem @ w_kv, 2, axis=-1)
    q = q.reshape(bsz, seq, XA_HEADS, XA_HEAD_DIM)
    k = k.reshape(bsz, n_mem, XA_HEADS, XA_HEAD_DIM)
    v = v.reshape(bsz, n_mem, XA_HEADS, XA_HEAD_DIM)
    s = jnp.einsum('bshd,bmhd->bhsm', q, k).astype(jnp.float32) * (XA_HEAD_DIM ** -0.5)
    p = jax.nn.softmax(s, axis=-1).astype(v.dtype)
    o = jnp.einsum('bhsm,bmhd->bshd', p, v)
    return o.reshape(bsz, seq, MIX_WIDTH)

def grouped_moe(x, router_w, router_b, w_gate, w_up, w_down):
    bsz, seq, d = x.shape
    xt = x.reshape(-1, d)
    scores = jax.nn.sigmoid(jnp.dot(xt.astype(jnp.float32), router_w.astype(jnp.float32)))
    sel = scores + router_b.astype(jnp.float32)
    group_score = lax.top_k(sel.reshape(-1, N_GROUPS, GROUP_SIZE), TOP_K)[0].sum(-1)
    top_group = jnp.argmax(group_score, axis=-1)
    expert_group = jnp.arange(N_EXPERTS_2) // GROUP_SIZE
    in_group = expert_group[None, :] == top_group[:, None]
    _, idx = lax.top_k(jnp.where(in_group, sel, -jnp.inf), TOP_K)
    gate = jnp.take_along_axis(scores, idx, axis=-1)
    gate = gate / gate.sum(-1, keepdims=True)
    combine = jnp.einsum('tk,tke->te', gate,
                         jax.nn.one_hot(idx, N_EXPERTS_2, dtype=jnp.float32)).astype(x.dtype)
    out = jnp.zeros_like(xt)
    for e in range(N_EXPERTS_2):
        h = jax.nn.silu(xt @ w_gate[e]) * (xt @ w_up[e])
        out = out + combine[:, e:e + 1] * (h @ w_down[e])
    return out.reshape(bsz, seq, d)

def second_inputs(seed: int = 0) -> dict:
    key = jax.random.key(seed)
    ks = jax.random.split(key, 20)
    d = D_MODEL

    def nrm(k, shape, scale):
        return jax.random.normal(k, shape, jnp.float32) * scale

    x = nrm(ks[0], (BATCH, SEQ, d), 1.0)
    mem = nrm(ks[1], (BATCH, N_MEM, d), 1.0)
    w_in_a = nrm(ks[2], (N_A, d, 3 * MIX_WIDTH), d ** -0.5)
    sgu_ln_g = 1.0 + nrm(ks[3], (N_A, MIX_WIDTH), 0.02)
    sgu_ln_b = nrm(ks[4], (N_A, MIX_WIDTH), 0.02)
    sgu_w = nrm(ks[5], (N_A, SGU_HEADS, SGU_CHUNK, SGU_CHUNK), SGU_CHUNK ** -0.5)
    sgu_b = 1.0 + nrm(ks[6], (N_A, SGU_HEADS, SGU_CHUNK), 0.02)
    w_in_b = nrm(ks[7], (N_B, d, 4 * MIX_WIDTH), d ** -0.5)
    conv_w = nrm(ks[8], (N_B, CONV_WIDTH_2, MIX_WIDTH), CONV_WIDTH_2 ** -0.5)
    kv_scale = jnp.concatenate([jnp.ones((MIX_WIDTH,), jnp.float32),
                                jnp.full((MIX_WIDTH,), BETA, jnp.float32)]) * (d ** -0.5)
    w_kv = nrm(ks[9], (DEPTH, d, 2 * MIX_WIDTH), 1.0) * kv_scale
    w_out = nrm(ks[10], (DEPTH, 2 * MIX_WIDTH, d), BETA * (2 * MIX_WIDTH) ** -0.5)
    ln1_g = 1.0 + nrm(ks[11], (DEPTH, d), 0.02)
    ln1_b = nrm(ks[12], (DEPTH, d), 0.02)
    router_w = nrm(ks[13], (d, N_EXPERTS_2), d ** -0.5)
    router_b = nrm(ks[14], (N_EXPERTS_2,), 0.01)
    w_gate = nrm(ks[15], (DEPTH, N_EXPERTS_2, d, D_EXPERT), d ** -0.5)
    w_up = nrm(ks[16], (DEPTH, N_EXPERTS_2, d, D_EXPERT), d ** -0.5)
    w_down = nrm(ks[17], (DEPTH, N_EXPERTS_2, D_EXPERT, d), BETA * D_EXPERT ** -0.5)
    ln2_g = 1.0 + nrm(ks[18], (DEPTH, d), 0.02)
    ln2_b = nrm(ks[19], (DEPTH, d), 0.02)
    return {"x": x, "mem": mem, "w_in_a": w_in_a, "sgu_ln_g": sgu_ln_g, "sgu_ln_b": sgu_ln_b,
            "sgu_w": sgu_w, "sgu_b": sgu_b, "w_in_b": w_in_b, "conv_w": conv_w,
            "w_kv": w_kv, "w_out": w_out, "ln1_g": ln1_g, "ln1_b": ln1_b,
            "router_w": router_w, "router_b": router_b, "w_gate": w_gate, "w_up": w_up,
            "w_down": w_down, "ln2_g": ln2_g, "ln2_b": ln2_b}

def second_block(x, mem, w_in_a, sgu_ln_g, sgu_ln_b, sgu_w, sgu_b, w_in_b, conv_w,
              w_kv, w_out, ln1_g, ln1_b, router_w, router_b, w_gate, w_up, w_down,
              ln2_g, ln2_b):
    for i in range(DEPTH):
        j = i // N_MIXERS
        if i % N_MIXERS == 0:
            z = x @ w_in_a[j]
            uv = jax.nn.gelu(z[..., :2 * MIX_WIDTH], approximate=False)
            tok = spatial_gating(uv, sgu_ln_g[j], sgu_ln_b[j], sgu_w[j], sgu_b[j])
            q = z[..., 2 * MIX_WIDTH:]
        else:
            z = x @ w_in_b[j]
            tok = short_conv_mixer(z[..., :3 * MIX_WIDTH], conv_w[j])
            q = z[..., 3 * MIX_WIDTH:]
        xa = memory_cross_attention(q, mem, w_kv[i])
        o = jnp.concatenate([tok, xa], axis=-1) @ w_out[i]
        x = layer_norm(ALPHA * x + o, ln1_g[i], ln1_b[i])
        f = grouped_moe(x, router_w, router_b, w_gate[i], w_up[i], w_down[i])
        x = layer_norm(ALPHA * x + f, ln2_g[i], ln2_b[i])
    return x


def setup_inputs(seed=0):
    out = dict(first_inputs(seed))
    for name, value in second_inputs(seed + 1).items():
        if name != "x":
            out[name + "_2"] = value
    return out


def reference(
    x, c, ctx, c_ctx, l0_mod_w, l0_mod_b, l0_mix_pre_g, l0_mix_post_g, l0_w_in, l0_mlstm_gate_b,
    l0_mlstm_conv_w, l0_mlstm_norm_g, l0_lambda_q1, l0_lambda_k1, l0_lambda_q2, l0_lambda_k2,
    l0_diff_norm_g, l0_w_out, l0_ffn_pre_g, l0_ffn_post_g, l0_ffn_w1, l0_ffn_w3, l0_ffn_w2,
    l1_mod_w, l1_mod_b, l1_mix_pre_g, l1_mix_post_g, l1_conv_pw1_w, l1_conv_pw1_b, l1_conv_dw_w,
    l1_conv_dw_b, l1_conv_ln_g, l1_conv_ln_b, l1_conv_pw2_w, l1_conv_pw2_b, l1_ffn_pre_g,
    l1_ffn_post_g, l1_router_w, l1_moe_w1, l1_moe_w3, l1_moe_w2, mem_2, w_in_a_2, sgu_ln_g_2,
    sgu_ln_b_2, sgu_w_2, sgu_b_2, w_in_b_2, conv_w_2, w_kv_2, w_out_2, ln1_g_2, ln1_b_2,
    router_w_2, router_b_2, w_gate_2, w_up_2, w_down_2, ln2_g_2, ln2_b_2,
):
    x = first_block(
        x, c, ctx, c_ctx, l0_mod_w, l0_mod_b, l0_mix_pre_g, l0_mix_post_g, l0_w_in,
        l0_mlstm_gate_b, l0_mlstm_conv_w, l0_mlstm_norm_g, l0_lambda_q1, l0_lambda_k1,
        l0_lambda_q2, l0_lambda_k2, l0_diff_norm_g, l0_w_out, l0_ffn_pre_g, l0_ffn_post_g,
        l0_ffn_w1, l0_ffn_w3, l0_ffn_w2, l1_mod_w, l1_mod_b, l1_mix_pre_g, l1_mix_post_g,
        l1_conv_pw1_w, l1_conv_pw1_b, l1_conv_dw_w, l1_conv_dw_b, l1_conv_ln_g, l1_conv_ln_b,
        l1_conv_pw2_w, l1_conv_pw2_b, l1_ffn_pre_g, l1_ffn_post_g, l1_router_w, l1_moe_w1,
        l1_moe_w3, l1_moe_w2,
    )
    return second_block(
        x, mem_2, w_in_a_2, sgu_ln_g_2, sgu_ln_b_2, sgu_w_2, sgu_b_2, w_in_b_2, conv_w_2,
        w_kv_2, w_out_2, ln1_g_2, ln1_b_2, router_w_2, router_b_2, w_gate_2, w_up_2, w_down_2,
        ln2_g_2, ln2_b_2,
    )


_drawn_inputs = setup_inputs


def setup_inputs(seed=0):
    import zlib

    import numpy as np

    out = dict(_drawn_inputs(seed))
    spreads = {}
    factors = {'sgu_ln_g_2': 5.386, 'sgu_ln_b_2': 15.381, 'sgu_b_2': 8.0}
    for name, (base, spread) in spreads.items():
        noise = np.random.default_rng([zlib.crc32(name.encode()), seed]).standard_normal(out[name].shape)
        drawn = base * np.exp(spread * noise) if base else spread * noise
        out[name] = jnp.asarray(drawn.astype(out[name].dtype))
    for name, factor in factors.items():
        out[name] = (out[name] * factor).astype(out[name].dtype)
    return out
```

```python
from contextlib import ExitStack

import numpy as np

import concourse.bass as bass
from concourse import mybir

P = 128
F32 = mybir.dt.float32
ALU = mybir.AluOpType
ACT = mybir.ActivationFunctionType
AX = mybir.AxisListType

D = 1024
KC = D // P
T = 256
TT = T // P
NCH = 512
HALF = NCH // 2
FF = 2816
FSTEP = 256
NSTEP = FF // FSTEP
NE1 = 8
NE2 = 16
NG = 4
GS = NE2 // NG
NSTEP2 = (D // 2) // FSTEP
MH, MD = 8, 64
DH, DQ, DV = 4, 64, 128
XH = 4
TAPS = 31
EPS = 1e-6
LN_EPS = 1e-5
LAM_INIT = 0.8 - 0.6
ALPHA = 4 ** 0.25
GR = 40
RING = 4
NBANK = 4


def plan_stream():
    names = [f"mod0_{c}" for c in range(4)]
    names += ["dq", "dk", "dv", "gates", "mk", "mq", "mv", "mo"]
    names += FILL
    names += ["wo0", "wo1"]
    g_at, d_at, pos, filled = {}, {}, 0, [0] * RING
    dfilled = [0] * RING
    loops = {}

    def put(name):
        nonlocal pos
        s = pos % RING
        g_at[name] = (s, filled[s])
        filled[s] += 1
        pos += 1

    def loop(name, count, steps):
        nonlocal pos
        pos += -pos % RING
        per = [len([s for s in range(steps) if s % RING == r]) for r in range(RING)]
        loops[name] = (list(filled), list(dfilled), per)
        for r in range(RING):
            filled[r] += per[r] * count
            dfilled[r] += per[r] * count

    for n in names:
        put(n)
    loop("ffn0", 1, NSTEP)
    for n in ["pa0", "pg0", "pa1", "pg1"] + LATE + ["pw2_0", "pw2_1"]:
        put(n)
    loop("moe1", NE1, NSTEP)
    for n in ["kv0_0", "kv0_1", "kv1_0", "kv1_1", "za0", "za1", "za2", "woA0", "woA1"]:
        put(n)
    loop("moeA", NE2 // 2, 2 * NSTEP2)
    for n in ["zb0", "zb1", "zb2", "zb3", "woB0", "woB1"]:
        put(n)
    loop("moeB", NE2 // 2, 2 * NSTEP2)
    return g_at, loops


LATE = ["mod1_4", "mod1_5", "mod1_10", "mod1_11"]
FILL = [f"mod0_{c}" for c in range(4, 12)] + [f"mod1_{c}" for c in range(12) if f"mod1_{c}" not in LATE]
NFILL = len(FILL)
SLOTS = 2 * DH + MH


def fills_at(i):
    return FILL[NFILL * i // SLOTS:NFILL * (i + 1) // SLOTS]


def plan_banks():
    names = [f"mod0_{c}" for c in range(4)]
    names += ["dq0", "dq1", "dk0", "dk1", "dkc0", "dkc1", "dv0", "dv1", "dvc0", "dvc1", "ig", "fg"]
    names += ["mk0", "mk1", "mkc0", "mkc1", "mq0", "mq1"]
    names += ["mv0", "mv1", "mvc0", "mvc1", "mo0", "mo1", "dqT0", "dqT1", "dkT0", "dkT1", "gT"]
    names += FILL
    names += [f"wo{n}{t}" for n in range(2) for t in range(TT)]
    names += [f"{w}{c}{j}" for c in range(2) for w in ("pa", "pg") for j in range(2)]
    names += LATE
    names += [f"pw2{n}{t}" for n in range(2) for t in range(TT)]
    names += ["rt1"]
    names += ["sguT"]
    names += [f"kv{l}{w}{j}" for l in range(2) for w in "kv" for j in range(2)]
    names += [f"za{n}{j}" for n in range(3) for j in range(2)]
    names += [f"sg{t}" for t in range(TT)] + ["tokT0", "tokT1"]
    names += [f"woA{n}{t}" for n in range(2) for t in range(TT)] + ["rtA"]
    names += [f"zb{n}{j}" for n in range(4) for j in range(2)]
    names += [f"woB{n}{t}" for n in range(2) for t in range(TT)] + ["rtB"]
    return {n: (i % NBANK, i // NBANK) for i, n in enumerate(names)}


def two_blocks(nc, A, out):
    g_at, loops = plan_stream()
    bank_of = plan_banks()

    with ExitStack() as ctx:
        def sb(name, shape, dt=F32):
            return ctx.enter_context(nc.sbuf_tensor(name, shape, dt))

        sems = {}

        def sem(name):
            if name not in sems:
                sems[name] = ctx.enter_context(nc.semaphore(name))
            return sems[name]

        ring = sb("ring", [P, RING, KC, NCH])
        dreg = sb("dreg", [P, RING * 2 * D])
        arena = sb("arena", [P, 5664])
        X = sb("X", [P, TT, D])
        XN = sb("XN", [P, TT, D])
        TOK = sb("TOK", [P, TT, D])
        T1 = sb("T1", [P, KC, T])
        T2 = sb("T2", [P, KC, T])
        GP = sb("GP", [P, 2, D])
        RB = sb("RB", [P, 2, NCH])
        RS = sb("RS", [P, 4, D])
        CB = sb("CB", [P, KC, P])
        ident = sb("ident", [P, P])
        pack = T2[:, :, :].rearrange("p k t -> p (k t)")[:, 0:4 * P].rearrange("p (a n) -> p a n", a=4)
        PCOL = sb("PCOL", [P, 4, P])
        CT = sb("CT", [P, KC, 2])
        MODX = sb("MODX", [P, 2, 48])
        MODC = sb("MODC", [P, 16])
        SCL = sb("SCL", [P, 5, KC])
        mskf = sb("mskf", [P, 3, P])
        mskb = sb("mskb", [P, 3, P])
        sm = sb("sm", [P, 512])
        gbias = sb("gbias", [GR, 2])
        wrt = sb("wrt", [P, KC, NE1 + NE2])
        rbias = sb("rbias", [P, NE2])
        tri8 = sb("tri8", [P, NE1, NE1])
        gates = sb("gates", [P, TT, NE2])
        gcol = sb("gcol", [P, TT])
        SG = sb("SG", [P, 2, FSTEP])
        H = sb("H", [P, 2, FSTEP])
        HT = sb("HT", [P, 2, 2, P])

        def carve(region, at, *shape):
            n = int(np.prod(shape))
            v = region[:, at:at + n]
            if len(shape) == 1:
                return v
            names = "abcd"[:len(shape)]
            spec = " ".join(names)
            return v.rearrange(f"p ({spec}) -> p {spec}", **{names[i]: shape[i] for i in range(len(shape))})

        dring = carve(dreg, 0, RING, 2, D)
        kT = carve(dreg, 0, 4, 2 * T)
        qT = carve(dreg, 2048, 4, T)
        kdT = carve(dreg, 3072, 4, 2 * T)
        qdT = carve(dreg, 5120, 4, T)
        vd = carve(dreg, 6144, 4, NCH)
        vaug = carve(arena, 0, 4, MH, MD + 1)
        osig = carve(arena, 2080, TT, NCH)
        WD = carve(arena, 3104, 2, 896)
        AR = carve(arena, 4896, 2, 384)
        EX = carve(arena, 3104, 2, 2, NCH)
        RSf = RS[:, :, :].rearrange("p a n -> p (a n)")
        CV = carve(RSf, 1024, 2, NCH)
        PR = carve(RSf, 2048, 2, NCH)
        PT = carve(RSf, 3072, 2, NCH)
        HR = carve(RSf, 1024, MH, 4, MD + 1)
        T2f = T2[:, :, :].rearrange("p k t -> p (k t)")
        SEL = carve(T2f, 0, 2 * MH, P)
        XNf = XN[:, :, :].rearrange("p t n -> p (t n)")
        gi = arena[0:GR, 3104:3104 + 512]
        gf = arena[0:GR, 3616:3616 + 512]
        gt_ = arena[0:GR, 4128:4128 + 512]
        gB = arena[0:GR, 4640:4640 + 512]
        GCt = sb("GCt", [P, 6, GR])
        onesr = SG[0:GR, :, :].rearrange("p a n -> p (a n)")
        gG = H[0:GR, :, :].rearrange("p a n -> p (a n)")
        nM = HT[0:GR, 0, :, :].rearrange("p a n -> p (a n)")
        gE = HT[0:GR, 1, :, :].rearrange("p a n -> p (a n)")
        WG = carve(RSf, 3104, KC, 2, GR)
        rope = carve(RSf, 2048, TT, 2, 64)
        lamv = carve(RSf, 2304, 4, DQ)
        rk = carve(arena, 4096, 2, 64)
        hT = carve(dreg, 0, KC, T + TAPS - 1)
        SGC = carve(dreg, 2304, 2, NCH)
        memT = T2
        kmT = carve(arena, 0, 2, XH, T)
        vm = carve(arena, 2048, 2, 2, NCH)
        UV = carve(dreg, 0, TT, 2, NCH)
        xqT = carve(dreg, 2048, XH, T)
        EM = carve(dreg, 3072, 2, TT, T)
        PMT = carve(dreg, 4096, 2, 2, T)
        sguw = carve(dreg, 5120, XH, P)
        sguT = carve(dreg, 5632, XH, P)
        cgT = carve(dreg, 0, 4, T)
        bgT = carve(dreg, 1024, 4, T)
        hT2 = carve(dreg, 6144, 4, T + 2)
        cvB = carve(dreg, 7176, 2, T)

        banks = [ctx.enter_context(nc.psum_tensor(f"bank{i}", [P, NCH], F32)) for i in range(8)]
        block = ctx.enter_context(nc.Block())

        def chunk(w, c, n=NCH):
            return w.rearrange("(k p) n -> p k n", p=P)[:, :, c:c + n]

        win = A["l0_w_in"]
        wsrc = {}
        for l in range(2):
            for c in range(12):
                wsrc[f"mod{l}_{c}"] = chunk(A[f"l{l}_mod_w"], c * NCH)
        for i, n in enumerate(["mq", "mk", "mv", "mo"]):
            wsrc[n] = chunk(win, i * NCH)
        wsrc["gates"] = chunk(win, 2048, 32)
        for i, n in enumerate(["dq", "dk", "dv"]):
            wsrc[n] = chunk(win, 2080 + i * NCH)
        for c in range(2):
            wsrc[f"wo{c}"] = chunk(A["l0_w_out"], c * NCH)
            wsrc[f"pa{c}"] = chunk(A["l1_conv_pw1_w"], c * NCH)
            wsrc[f"pg{c}"] = chunk(A["l1_conv_pw1_w"], D + c * NCH)
            wsrc[f"pw2_{c}"] = chunk(A["l1_conv_pw2_w"], c * NCH)
            for l in range(2):
                wsrc[f"kv{l}_{c}"] = chunk(A["w_kv_2"][l], c * NCH)
            wsrc[f"woA{c}"] = chunk(A["w_out_2"][0], c * NCH)
            wsrc[f"woB{c}"] = chunk(A["w_out_2"][1], c * NCH)
        for c in range(3):
            wsrc[f"za{c}"] = chunk(A["w_in_a_2"][0], c * NCH)
        for c in range(4):
            wsrc[f"zb{c}"] = chunk(A["w_in_b_2"][0], c * NCH)

        last_output = {f: f for f in wsrc if f.startswith("mod")}
        last_output.update(dq="dq1", dk="dkc1", dv="dvc1", gates="fg", mk="mkc1", mq="mq1", mv="mvc1", mo="mo1")
        for c in range(2):
            last_output.update({f"wo{c}": f"wo{c}1", f"pa{c}": f"pa{c}1", f"pg{c}": f"pg{c}1", f"pw2_{c}": f"pw2{c}1",
                                f"woA{c}": f"woA{c}1", f"woB{c}": f"woB{c}1", f"kv{c}_0": f"kv{c}k1", f"kv{c}_1": f"kv{c}v1"})
        last_output.update({f"za{c}": f"za{c}1" for c in range(3)})
        last_output.update({f"zb{c}": f"zb{c}1" for c in range(4)})

        def row(v, n):
            return v.rearrange("(a n) -> a n", a=1).broadcast_to([P, n])

        def wait_output(eng, name):
            b, n = bank_of[name]
            eng.wait_ge(sem(f"bank_ready{b}"), n + 1)

        @block.sync
        def _(sp):
            sp.dma_start(X[:, :, :], A["x"][0].rearrange("(t p) d -> p t d", p=P)).then_inc(sem("x_loaded"), 16)
            sp.dma_start(TOK[:, :, :], A["ctx"][0].rearrange("(t p) d -> p t d", p=P)).then_inc(sem("ctx_loaded"), 16)

            holder = [None] * RING

            def slot_free(s):
                h = holder[s]
                if isinstance(h, str):
                    wait_output(sp, last_output[h])
                elif h is not None:
                    sp.wait_ge(sem("upped1"), h)

            def load(name):
                s, n = g_at[name]
                slot_free(s)
                w = 32 if name == "gates" else NCH
                sp.dma_start(ring[:, s, :, 0:w], wsrc[name]).then_inc(sem(f"chunk_in{s}"), 16)
                holder[s] = name

            def experts(count, steps, w1, w3, w2, hid0):
                n = len(steps)
                before = list(holder)

                def body(it):
                    for q, (e, st) in enumerate(steps):
                        s = q % RING
                        f = slice(st * FSTEP, (st + 1) * FSTEP)
                        if q < RING and isinstance(before[s], str):
                            wait_output(sp, last_output[before[s]])
                        prev = q - RING if q >= RING else max(p for p in range(n) if p % RING == s) - n
                        done = hid0 + prev + 1 + it * n
                        if not (isinstance(done, int) and done <= 0):
                            sp.wait_ge(sem("upped1"), done)
                        for i, w in enumerate((w1, w3)):
                            sp.dma_start(ring[:, s, :, i * FSTEP:(i + 1) * FSTEP],
                                         w(it, e).rearrange("(k p) n -> p k n", p=P)[:, :, f]).then_inc(sem(f"pair_in{s}"), 16)
                        if not (isinstance(done, int) and done <= 0):
                            sp.wait_ge(sem("down_done1"), done)
                        sp.dma_start(dring[:, s, :, :], w2(it, e)[f, :].rearrange("(j p) n -> p j n", p=P)).then_inc(
                            sem(f"down_in{s}"), 16)
                if count == 1:
                    body(0)
                else:
                    with sp.Fori(0, count) as it:
                        body(it)
                for s in range(RING):
                    holder[s] = hid0 + n * (count - 1) + max(p for p in range(n) if p % RING == s) + 1

            for n in [f"mod0_{c}" for c in range(4)] + ["dq", "dk", "dv", "gates", "mk", "mq", "mv", "mo"] + FILL:
                load(n)
            load("wo0")
            load("wo1")
            sp.wait_ge(sem("x_updated"), 1)
            one = [(0, st) for st in range(NSTEP)]
            experts(1, one, lambda it, e: A["l0_ffn_w1"], lambda it, e: A["l0_ffn_w3"], lambda it, e: A["l0_ffn_w2"], 0)
            for n in ["pa0", "pg0", "pa1", "pg1"] + LATE + ["pw2_0", "pw2_1"]:
                load(n)
            sp.wait_ge(sem("x_updated"), 3)
            experts(NE1, one, lambda it, e: A["l1_moe_w1"][it], lambda it, e: A["l1_moe_w3"][it],
                    lambda it, e: A["l1_moe_w2"][it], NSTEP)
            for n in ["kv0_0", "kv0_1", "kv1_0", "kv1_1", "za0", "za1", "za2", "woA0", "woA1"]:
                load(n)
            two = [(e, st) for e in range(2) for st in range(NSTEP2)]
            for l, v in ((0, 5), (1, 7)):
                sp.wait_ge(sem("x_updated"), v)
                experts(NE2 // 2, two, lambda it, e: A["w_gate_2"][l, it * 2 + e], lambda it, e: A["w_up_2"][l, it * 2 + e],
                        lambda it, e: A["w_down_2"][l, it * 2 + e], NSTEP * (1 + NE1) + l * NE2 * NSTEP2)
                if l == 0:
                    for n in ["zb0", "zb1", "zb2", "zb3", "woB0", "woB1"]:
                        load(n)
            sp.wait_ge(sem("x_updated"), 8)
            sp.dma_start(out[0].rearrange("(t p) d -> p t d", p=P), X[:, :, :]).then_inc(sem("stored"), 16)
            sp.wait_ge(sem("stored"), 16)

        @block.gpsimd
        def _(pool):
            cnt = {}

            def step(ins, name="pool_step"):
                cnt[name] = cnt.get(name, 0) + 1
                ins.then_inc(sem(name), 1)
                pool.wait_ge(sem(name), cnt[name])

            row0 = 0
            for v, n in (("l0_mod_b", 48), ("l0_mix_pre_g", 8), ("l0_ffn_pre_g", 8),
                         ("l1_mod_b", 48), ("l1_mix_pre_g", 8), ("l1_ffn_pre_g", 8)):
                pool.dma_start(pack[row0:row0 + n, 0, :], A[v].rearrange("(r n) -> r n", n=P)).then_inc(sem("packed"), 16)
                row0 += n
            row0 = 0
            for v, n in ((A["c"][0], 8), (A["c_ctx"], 8), (A["l0_mlstm_conv_w"].rearrange("a n -> (a n)"), 24),
                         (A["l1_conv_dw_b"], 8), (A["l1_conv_pw1_b"], 16),
                         (A["conv_w_2"][0].rearrange("a n -> (a n)"), 12),
                         (A["sgu_b_2"][0].rearrange("a n -> (a n)"), 4)):
                pool.dma_start(pack[row0:row0 + n, 1, :], v.rearrange("(r n) -> r n", n=P)).then_inc(sem("packed"), 16)
                row0 += n
            dw = A["l1_conv_dw_w"].rearrange("a (r n) -> (a r) n", n=P)
            pool.dma_start(pack[:, 2, :], dw[0:P, :]).then_inc(sem("packed"), 16)
            pool.dma_start(pack[0:TAPS * KC - P, 3, :], dw[P:TAPS * KC, :]).then_inc(sem("packed"), 16)
            step(pool.memset(ident[:, :], 0.0))
            step(pool.affine_select(out=ident[:, :], in_=ident[:, :], compare_op=ALU.not_equal, fill=1.0, base=0,
                                    pattern=[[-1, P]], channel_multiplier=1), "ident_made")
            step(pool.memset(gbias[:, :], 0.0))
            for d in range(2):
                for w in range(2):
                    pool.dma_start(gbias[32 * d:32 * d + 8, w:w + 1],
                                   A["l0_mlstm_gate_b"][16 * d + 8 * w:16 * d + 8 * w + 8].rearrange("(n a) -> n a", a=1)
                                   ).then_inc(sem("consts_in"), 16)
            for i, n in enumerate(("l0_lambda_q1", "l0_lambda_k1", "l0_lambda_q2", "l0_lambda_k2")):
                pool.dma_start(lamv[:, i, :], row(A[n], DQ)).then_inc(sem("consts_in"), 16)
            pool.dma_start(rope[:, :, :, :], A["rope"].rearrange("(t p) a n -> p t a n", p=P)).then_inc(sem("consts_in"), 16)
            pool.dma_start(wrt[:, :, 0:NE1], A["l1_router_w"].rearrange("(k p) n -> p k n", p=P)).then_inc(sem("consts_in"), 16)
            pool.dma_start(wrt[:, :, NE1:], A["router_w_2"].rearrange("(k p) n -> p k n", p=P)).then_inc(sem("consts_in"), 16)
            pool.dma_start(rbias[:, :], row(A["router_b_2"], NE2)).then_inc(sem("consts_in"), 16)
            pool.dma_start(RS[:, 0, 0:NCH], row(A["l0_mlstm_norm_g"], NCH)).then_inc(sem("consts_in"), 16)
            pool.dma_start(RS[:, 0, NCH:D], row(A["l0_diff_norm_g"], NCH)).then_inc(sem("consts_in"), 16)
            step(pool.memset(onesr, 1.0))
            step(pool.memset(WG[:, :, :, :], 0.0), "gate_pad")
            step(pool.memset(mskf[:, :, :], 0.0))
            step(pool.memset(mskb[:, :, :], 0.0))
            step(pool.affine_select(out=mskf[:, 1:3, :], in_=mskf[:, 1:3, :], compare_op=ALU.is_ge, fill=-1e30, base=0,
                                    pattern=[[0, 2], [1, P]], channel_multiplier=-1))
            step(pool.affine_select(out=mskb[:, 0:2, :], in_=mskb[:, 0:2, :], compare_op=ALU.is_ge, fill=-1e30, base=0,
                                    pattern=[[0, 2], [-1, P]], channel_multiplier=1))
            step(pool.memset(tri8[:, :, :], 1.0))
            step(pool.affine_select(out=tri8[:, :, :], in_=tri8[:, :, :], compare_op=ALU.is_ge, fill=0.0, base=-1,
                                    pattern=[[1, NE1], [-1, NE1]], channel_multiplier=0))
            step(pool.memset(vaug[:, :, :, MD:MD + 1], 1.0))
            step(pool.memset(WG[:, 0:1, 0, 39:40], 0.0), "masks_made")
            gated = [0]

            def gate_rows(names):
                for f in names:
                    l, c = int(f[3]), int(f[5:])
                    if c not in (4, 5, 10, 11):
                        continue
                    if gated[0]:
                        pool.wait_ge(sem("rows_used"), gated[0])
                    h = c % 2
                    post = A[f"l{l}_mix_post_g"] if c < 6 else A[f"l{l}_ffn_post_g"]
                    pool.dma_start(RB[:, 0, :], row(A[f"l{l}_mod_b"][c * NCH:(c + 1) * NCH], NCH)).then_inc(sem("rows_in"), 16)
                    pool.dma_start(RB[:, 1, :], row(post[h * NCH:(h + 1) * NCH], NCH)).then_inc(sem("rows_in"), 16)
                    gated[0] += 1

            gate_rows(FILL)

            def rows_after(v, loads):
                pool.wait_ge(sem("x_updated"), v)
                for s, lo, a, n in loads:
                    pool.dma_start(RS[:, s, lo:lo + n], row(a, n)).then_inc(sem("params_in"), 16)

            rows_after(1, [(1, 0, A["l1_conv_ln_g"], D), (2, 0, A["l1_conv_ln_b"], D), (3, 0, A["l1_conv_pw2_b"], D),
                           (0, 0, A["sgu_ln_g_2"][0], NCH), (0, NCH, A["sgu_ln_b_2"][0], NCH)])
            pool.wait_ge(sem("x_updated"), 2)
            step(pool.memset(hT[:, :, 0:TAPS // 2], 0.0), "margins")
            step(pool.memset(hT[:, :, T + TAPS // 2:], 0.0), "margins")
            gate_rows(LATE)
            rows_after(3, [(1, 0, A["ln1_g_2"][0], D), (2, 0, A["ln1_b_2"][0], D), (3, 0, A["ln2_g_2"][0], D)])
            pool.wait_ge(sem("x_updated"), 4)
            pool.dma_start(TOK[:, :, :], A["mem_2"][0].rearrange("(t p) d -> p t d", p=P)).then_inc(sem("mem_loaded"), 16)
            pool.dma_start(sguw, A["sgu_w_2"][0].rearrange("h i j -> i h j")).then_inc(sem("sgu_in"), 16)
            rows_after(5, [(0, 0, A["ln2_b_2"][0], D), (1, 0, A["ln1_g_2"][1], D), (2, 0, A["ln1_b_2"][1], D)])
            pool.wait_ge(sem("x_updated"), 6)
            step(pool.memset(hT2[:, :, 0:2], 0.0), "margins")
            rows_after(6, [(3, 0, A["ln2_g_2"][1], D), (0, 0, A["ln2_b_2"][1], D)])

        @block.tensor
        def _(pe):
            def bank_for(name):
                b, n = bank_of[name]
                if n:
                    pe.wait_ge(sem(f"bank_read{b}"), n)
                return banks[b]

            def filled(ins, name):
                ins.then_inc(sem(f"bank_ready{bank_of[name][0]}"), 1)

            seen = [0] * RING

            def chunk_in(name):
                s, _ = g_at[name]
                seen[s] += 1
                pe.wait_ge(sem(f"chunk_in{s}"), 16 * seen[s])
                return ring[:, s, :, :]

            def tok_unit(name, src, t, w, n=NCH, lo=0):
                o = bank_for(name)
                for k in range(KC):
                    m = pe.matmul(o[:, lo:lo + n], src[:, k, t * P:(t + 1) * P], w[:, k, 0:n], start=k == 0, stop=k == KC - 1)
                filled(m, name)
                return m

            def feat_unit(name, src, j, w):
                o = bank_for(name)
                for i in range(2):
                    for k in range(KC):
                        m = pe.matmul(o[:, i * T:(i + 1) * T], w[:, k, (2 * j + i) * P:(2 * j + i + 1) * P], src[:, k, :],
                                      start=k == 0, stop=k == KC - 1)
                filled(m, name)
                return m

            def mod_job(name):
                c = int(name.split("_")[1])
                w = chunk_in(name)
                o = bank_for(name)
                if c in (4, 5, 10, 11):
                    for k in range(KC):
                        m = pe.matmul(o[:, :], CB[:, k, :], w[:, k, :], start=k == 0, stop=k == KC - 1)
                else:
                    for j in range(4):
                        for k in range(KC):
                            m = pe.matmul(o[:, 2 * j:2 * j + 2], w[:, k, j * P:(j + 1) * P], CT[:, k, :],
                                          start=k == 0, stop=k == KC - 1)
                filled(m, name)

            turn = [0]

            def turn_job(src, back=False):
                for b in range(4):
                    if turn[0]:
                        pe.wait_ge(sem("turned_read"), 4 * (turn[0] - 1) + b + 1)
                    for i in range(4):
                        if back:
                            t, k = b // 2, 4 * (b % 2) + i
                            m = pe.transpose(banks[4 + b][:, i * P:(i + 1) * P], src[:, k, t * P:(t + 1) * P], ident[:, :])
                        else:
                            k, t = 2 * b + i // 2, i % 2
                            m = pe.transpose(banks[4 + b][:, i * P:(i + 1) * P], src[:, t, k * P:(k + 1) * P], ident[:, :])
                    m.then_inc(sem("turned"), 1)
                turn[0] += 1

            def wait_operand(n):
                pe.wait_ge(sem("operand_ready"), n)

            pe.wait_ge(sem("ident_made"), 1)
            pe.wait_ge(sem("packed"), 16 * 15)
            for i, n in enumerate((P, 80, P, TAPS * KC - P)):
                m = pe.transpose(banks[7][:, i * P:i * P + n], pack[0:n, i, :], ident[0:n, 0:n])
            m.then_inc(sem("cols_turned"), 1)
            pe.wait_ge(sem("silu_c"), 1)
            for c in range(4):
                mod_job(f"mod0_{c}")
            pe.wait_ge(sem("cols_read"), 1)
            pe.wait_ge(sem("normed"), 1)
            turn_job(XN)
            pe.wait_ge(sem("normed"), 2)
            turn_job(TOK)
            wait_operand(2)
            w = chunk_in("dq")
            for t in range(TT):
                tok_unit(f"dq{t}", T1, t, w)
            w = chunk_in("dk")
            for t in range(TT):
                tok_unit(f"dk{t}", T1, t, w)
            for j in range(2):
                feat_unit(f"dkc{j}", T2, j, w)
            w = chunk_in("dv")
            for t in range(TT):
                tok_unit(f"dv{t}", T1, t, w)
            for t in range(TT):
                tok_unit(f"dvc{t}", T2, t, w)
            chunk_in("gates")
            pe.wait_ge(sem("gate_weights"), 1)
            for i, name in enumerate(("ig", "fg")):
                o = bank_for(name)
                for j, src in enumerate((T2, T1)):
                    for k in range(KC):
                        m = pe.matmul(o[0:GR, j * T:(j + 1) * T], WG[:, k, i, :], src[:, k, :], start=k == 0, stop=k == KC - 1)
                filled(m, name)
            w = chunk_in("mk")
            for j in range(2):
                feat_unit(f"mk{j}", T1, j, w)
            for j in range(2):
                feat_unit(f"mkc{j}", T2, j, w)
            w = chunk_in("mq")
            for j in range(2):
                feat_unit(f"mq{j}", T1, j, w)
            w = chunk_in("mv")
            for t in range(TT):
                tok_unit(f"mv{t}", T1, t, w)
            for t in range(TT):
                tok_unit(f"mvc{t}", T2, t, w)
            w = chunk_in("mo")
            for t in range(TT):
                m = tok_unit(f"mo{t}", T1, t, w)
            for i, n in enumerate("qk"):
                pe.wait_ge(sem("rotated"), i + 1)
                for b in range(2):
                    o = bank_for(f"d{n}T{b}")
                    for j in range(2):
                        for t in range(TT):
                            c = 2 * b + j
                            m = pe.transpose(o[:, j * T + t * P:j * T + (t + 1) * P],
                                             XN[:, t, i * NCH + c * P:i * NCH + (c + 1) * P], ident[:, :])
                    filled(m, f"d{n}T{b}")
            pe.wait_ge(sem("gate_rows"), 1)
            o = bank_for("gT")
            for s in range(4):
                pe.transpose(o[:, s * GR:(s + 1) * GR], gG[:, s * P:(s + 1) * P], ident[0:GR, 0:GR])
            for t in range(TT):
                m = pe.transpose(o[:, (4 + t) * GR:(5 + t) * GR], gE[:, t * P:(t + 1) * P], ident[0:GR, 0:GR])
            filled(m, "gT")

            pe.wait_ge(sem("diff_operands"), 1)

            def diff_scores(u):
                h, t = divmod(u, TT)
                if u:
                    pe.wait_ge(sem("diff_exp"), 2 * u)
                for i in range(2):
                    r = slice(i * DQ, (i + 1) * DQ)
                    pe.matmul(banks[4 + i][:, :], qdT[r, h, t * P:(t + 1) * P], kdT[r, h, :], start=True, stop=True
                              ).then_inc(sem("diff_scored"), 1)

            def diff_values(u):
                h, t = divmod(u, TT)
                pe.wait_ge(sem("diff_prob"), u + 1)
                if u:
                    pe.wait_ge(sem("diff_prob_turned"), u)
                for s in range(4):
                    m = pe.transpose(banks[6][:, s * P:(s + 1) * P], PR[:, u % 2, s * P:(s + 1) * P], ident[:, :])
                m.then_inc(sem("diff_turned"), 1)
                pe.wait_ge(sem("diff_prob_turned"), u + 1)
                if u:
                    pe.wait_ge(sem("diff_out"), u)
                for s in range(4):
                    m = pe.matmul(banks[7][:, 0:DV], PT[:, u % 2, s * P:(s + 1) * P], vd[:, s, h * DV:(h + 1) * DV],
                                  start=s == 0, stop=s == 3)
                m.then_inc(sem("diff_summed"), 1)

            diff_scores(0)
            for u in range(2 * DH):
                if u + 1 < 2 * DH:
                    diff_scores(u + 1)
                for f in fills_at(u):
                    mod_job(f)
                diff_values(u)

            pe.wait_ge(sem("mlstm_operands"), 1)
            pe.wait_ge(sem("diff_out"), 2 * DH)

            def mlstm_scores(h):
                r = slice((h % 2) * MD, (h % 2) * MD + MD)
                if h:
                    pe.wait_ge(sem("mlstm_weighted"), 2 * h)
                    pe.wait_ge(sem("mlstm_exp"), 2 * h)
                for s in range(4):
                    pe.matmul(banks[4 + s // 2][:, (s % 2) * T:(s % 2 + 1) * T], kT[r, h // 2, s * P:(s + 1) * P],
                              qT[r, h // 2, :], start=True, stop=True)
                for d in range(2):
                    m = pe.matmul(banks[6][:, d * T:(d + 1) * T], SEL[0:GR, d * MH + h, :], nM, start=True, stop=True)
                m.then_inc(sem("mlstm_scored"), 1)

            def mlstm_values(h):
                if h:
                    pe.wait_ge(sem("mlstm_out"), h)
                parts = ([[(0, 128), (1, 384), (2, 640)], [(0, 0), (1, 256), (2, 512), (3, 768)]],
                         [[(0, 128), (1, 384), (2, 512), (3, 768)], [(0, 0), (1, 256), (3, 640)]])
                for d in range(2):
                    pe.wait_ge(sem("mlstm_weighted"), 2 * h + d + 1)
                    for t in range(TT):
                        ps = parts[d][t]
                        for n, (s, at) in enumerate(ps):
                            lo = (2 * d + t) * (MD + 1)
                            m = pe.matmul(banks[7][:, lo:lo + MD + 1], WD[:, d, at:at + P], vaug[:, s, h, :],
                                          start=n == 0, stop=n == len(ps) - 1)
                m.then_inc(sem("mlstm_summed"), 1)

            for h in range(MH):
                mlstm_scores(h)
                for f in fills_at(2 * DH + h):
                    mod_job(f)
                mlstm_values(h)

            pe.wait_ge(sem("mixed"), 1)
            pe.wait_ge(sem("mlstm_out"), MH)
            turn_job(TOK)
            wait_operand(3)
            for n in range(2):
                w = chunk_in(f"wo{n}")
                for t in range(TT):
                    tok_unit(f"wo{n}{t}", T1, t, w)
            pe.wait_ge(sem("normed"), 3)
            turn_job(XN)
            wait_operand(4)

            def run_expert(n_steps, slot0, hid0, it, hper, pin, din, out0, oper):
                nu = TT * n_steps

                def up(i):
                    st, t = divmod(i, TT)
                    s = (slot0 + st) % RING
                    if t == 0:
                        pe.wait_ge(sem(f"pair_in{s}"), pin(s, slot0 + st))
                    if not (isinstance(it, int) and hid0 + st == 0):
                        pe.wait_ge(sem(f"hidden{t}"), hid0 + hper * it + st)
                    for k in range(KC):
                        m = pe.matmul(banks[t][:, :], T1[:, k, t * P:(t + 1) * P], ring[:, s, k, :], start=k == 0, stop=k == KC - 1)
                    m.then_inc(sem(f"upped{t}"), 1)

                def turn_h(i):
                    st, t = divmod(i, TT)
                    pe.wait_ge(sem(f"hidden{t}"), hid0 + hper * it + st + 1)
                    if not (isinstance(it, int) and hid0 + st == 0):
                        pe.wait_ge(sem(f"hidden_turned{t}"), hid0 + hper * it + st)
                    for j in range(2):
                        m = pe.transpose(banks[2 + t][:, j * P:(j + 1) * P], H[:, t, j * P:(j + 1) * P], ident[:, :])
                    m.then_inc(sem(f"turned_h{t}"), 1)

                def down(i):
                    st, t = divmod(i, TT)
                    s = (slot0 + st) % RING
                    if t == 0:
                        pe.wait_ge(sem(f"down_in{s}"), din(s, slot0 + st))
                    if st == 0 and not (isinstance(it, int) and out0 == 0):
                        pe.wait_ge(sem(f"summed_read{t}"), out0 + oper * it)
                    pe.wait_ge(sem(f"hidden_turned{t}"), hid0 + hper * it + st + 1)
                    for j in range(2):
                        for n in range(2):
                            m = pe.matmul(banks[4 + 2 * t + n][:, :], HT[:, t, j, :], dring[:, s, j, n * NCH:(n + 1) * NCH],
                                          start=st == 0 and j == 0, stop=st == n_steps - 1 and j == 1)
                    m.then_inc(sem(f"down_done{t}"), 1)

                for i in range(nu + 2):
                    if i < nu:
                        up(i)
                    if i >= 2:
                        down(i - 2)
                    if 1 <= i <= nu:
                        turn_h(i - 1)

            pbase = {n: [0] * RING for n in loops}
            tot, dtot = [0] * RING, [0] * RING
            for n, c in (("ffn0", 1), ("moe1", NE1), ("moeA", NE2 // 2), ("moeB", NE2 // 2)):
                pbase[n] = (list(tot), list(dtot))
                for r in range(RING):
                    tot[r] += loops[n][2][r] * c
                    dtot[r] += loops[n][2][r] * c

            def moe(name, count, n_steps, hid0, out0, per_iter=1):
                pb, db = pbase[name]
                per = loops[name][2]

                def body(it):
                    for u in range(per_iter):
                        run_expert(n_steps, u * n_steps, hid0 + u * n_steps, it, n_steps * per_iter,
                                   lambda s, q: 32 * (pb[s] + q // RING + 1) + 32 * per[s] * it,
                                   lambda s, q: 16 * (db[s] + q // RING + 1) + 16 * per[s] * it,
                                   out0 + u, per_iter)
                if count == 1:
                    body(0)
                else:
                    with pe.Fori(0, count) as it:
                        body(it)

            def banks_read_before(name):
                i = list(bank_of).index(name)
                for b in range(NBANK):
                    pe.wait_ge(sem(f"bank_read{b}"), len([q for q in range(i) if q % NBANK == b]))

            banks_read_before("pa00")
            moe("ffn0", 1, NSTEP, 0, 0)

            pe.wait_ge(sem("normed"), 4)
            turn_job(XN)
            wait_operand(5)
            for c in range(2):
                for w_ in ("pa", "pg"):
                    w = chunk_in(f"{w_}{c}")
                    for j in range(2):
                        feat_unit(f"{w_}{c}{j}", T1, j, w)
            for f in LATE:
                mod_job(f)
            pe.wait_ge(sem("convolved"), 1)
            turn_job(T2, back=True)
            pe.wait_ge(sem("normed"), 5)
            turn_job(XN)
            wait_operand(6)
            for n in range(2):
                w = chunk_in(f"pw2_{n}")
                for t in range(TT):
                    tok_unit(f"pw2{n}{t}", T1, t, w)
            pe.wait_ge(sem("normed"), 6)
            turn_job(XN)
            wait_operand(7)

            def router(name, lo, n):
                o = bank_for(name)
                for t in range(TT):
                    for k in range(KC):
                        m = pe.matmul(o[:, t * n:(t + 1) * n], T1[:, k, t * P:(t + 1) * P], wrt[:, k, lo:lo + n],
                                      start=k == 0, stop=k == KC - 1)
                filled(m, name)

            router("rt1", 0, NE1)
            banks_read_before("sguT")
            moe("moe1", NE1, NSTEP, NSTEP, 1)

            pe.wait_ge(sem("mem_loaded"), 16)
            pe.wait_ge(sem("x_updated"), 4)
            turn_job(TOK)
            pe.wait_ge(sem("sgu_in"), 16)
            o = bank_for("sguT")
            for h in range(XH):
                m = pe.transpose(o[:, h * P:(h + 1) * P], sguw[:, h, :], ident[:, :])
            filled(m, "sguT")
            wait_operand(8)
            for l in range(2):
                w = chunk_in(f"kv{l}_0")
                for j in range(2):
                    feat_unit(f"kv{l}k{j}", memT, j, w)
                w = chunk_in(f"kv{l}_1")
                for j in range(2):
                    tok_unit(f"kv{l}v{j}", memT, j, w)
            turn_job(X)
            wait_operand(9)
            for n in range(2):
                w = chunk_in(f"za{n}")
                for t in range(TT):
                    tok_unit(f"za{n}{t}", T1, t, w)
            w = chunk_in("za2")
            for j in range(2):
                feat_unit(f"za2{j}", T1, j, w)

            def memory_attention(l, units):
                pe.wait_ge(sem("memory_operands"), l + 1)

                def scores(h):
                    u = units + h
                    if h >= 2:
                        pe.wait_ge(sem("mem_exp"), 2 * (u - 1))
                    for t in range(TT):
                        m = pe.matmul(banks[4 + h % 2][:, t * T:(t + 1) * T], xqT[:, h, t * P:(t + 1) * P], kmT[:, l, h, :],
                                      start=True, stop=True)
                    m.then_inc(sem("mem_scored"), 1)

                def values(h):
                    u = units + h
                    pe.wait_ge(sem("mem_prob"), u + 1)
                    if u:
                        pe.wait_ge(sem("mem_prob_turned"), u)
                    for c in range(2):
                        for t in range(TT):
                            m = pe.transpose(banks[6][:, c * T + t * P:c * T + (t + 1) * P], EM[:, h % 2, t, c * P:(c + 1) * P],
                                             ident[:, :])
                    m.then_inc(sem("mem_turned"), 1)
                    pe.wait_ge(sem("mem_prob_turned"), u + 1)
                    if u:
                        pe.wait_ge(sem("mem_out"), u)
                    for c in range(2):
                        m = pe.matmul(banks[7][:, 0:T], vm[:, l, c, h * P:(h + 1) * P], PMT[:, h % 2, c, :],
                                      start=c == 0, stop=c == 1)
                    m.then_inc(sem("mem_summed"), 1)

                scores(0)
                for h in range(XH):
                    if h + 1 < XH:
                        scores(h + 1)
                    values(h)

            memory_attention(0, 0)
            pe.wait_ge(sem("sgu_ready"), 1)
            for t in range(TT):
                o = bank_for(f"sg{t}")
                for h in range(XH):
                    m = pe.matmul(o[:, h * P:(h + 1) * P], sguT[:, h, :], UV[:, t, 1, h * P:(h + 1) * P], start=True, stop=True)
                filled(m, f"sg{t}")
            pe.wait_ge(sem("gated_tokens"), 1)
            for b in range(2):
                o = bank_for(f"tokT{b}")
                for j in range(2):
                    for t in range(TT):
                        c = 2 * b + j
                        m = pe.transpose(o[:, j * T + t * P:j * T + (t + 1) * P], TOK[:, t, c * P:(c + 1) * P], ident[:, :])
                filled(m, f"tokT{b}")
            pe.wait_ge(sem("cat_ready"), 1)
            for n in range(2):
                w = chunk_in(f"woA{n}")
                for t in range(TT):
                    tok_unit(f"woA{n}{t}", T2, t, w)
            pe.wait_ge(sem("x_updated"), 5)
            turn_job(X)
            wait_operand(10)
            router("rtA", NE1, NE2)
            banks_read_before("zb00")
            hid = NSTEP * (1 + NE1)
            moe("moeA", NE2 // 2, NSTEP2, hid, 1 + NE1, 2)
            pe.wait_ge(sem("x_updated"), 6)
            turn_job(X)
            wait_operand(11)
            for n in range(4):
                w = chunk_in(f"zb{n}")
                for j in range(2):
                    feat_unit(f"zb{n}{j}", T1, j, w)
            memory_attention(1, XH)
            pe.wait_ge(sem("cat_ready"), 2)
            for n in range(2):
                w = chunk_in(f"woB{n}")
                for t in range(TT):
                    tok_unit(f"woB{n}{t}", T2, t, w)
            pe.wait_ge(sem("x_updated"), 7)
            turn_job(X)
            wait_operand(12)
            router("rtB", NE1, NE2)
            for b in range(NBANK):
                pe.wait_ge(sem(f"bank_read{b}"), len([1 for v in bank_of.values() if v[0] == b]))
            moe("moeB", NE2 // 2, NSTEP2, hid + NE2 * NSTEP2, 1 + NE1 + NE2, 2)

        @block.scalar
        def _(act):
            cnt = {}

            def step(ins, name="act_step"):
                cnt[name] = cnt.get(name, 0) + 1
                ins.then_inc(sem(name), 1)
                act.wait_ge(sem(name), cnt[name])

            def take(name):
                b, n = bank_of[name]
                act.wait_ge(sem(f"bank_ready{b}"), n + 1)
                return banks[b]

            def freed(ins, name):
                ins.then_inc(sem(f"bank_read{bank_of[name][0]}"), 1)

            def root():
                n = cnt.get("rooted", 0)
                act.wait_ge(sem("variance"), n + 1)
                step(act.activation(sm[:, 16:32], sm[:, 0:16], ACT.Sqrt), "rooted")

            turn = [0]

            def operand(dst, scl=None, shf=None, ready=True):
                for b in range(4):
                    act.wait_ge(sem("turned"), 4 * turn[0] + b + 1)
                    for j in range(2):
                        k = 2 * b + j
                        src = banks[4 + b][:, j * T:(j + 1) * T]
                        if scl is None:
                            m = act.activation(dst[:, k, :], src, ACT.Copy)
                        else:
                            m = act.activation(dst[:, k, :], src, ACT.Identity, scale=scl[:, k:k + 1], bias=shf[:, k:k + 1])
                    step(m, "turned_read")
                turn[0] += 1
                step(act.activation(sm[:, 500:501], sm[:, 500:501], ACT.Copy), "operand_ready")

            act.wait_ge(sem("scratch_set"), 1)
            act.wait_ge(sem("cols_read"), 1)
            step(act.activation(CT[:, :, :].rearrange("p k j -> p j k"), PCOL[:, 1, 0:16].rearrange("p (j k) -> p j k", j=2),
                                ACT.Silu), "silu_c")
            for _ in range(2):
                root()
            act.wait_ge(sem("mod_cols"), 1)
            operand(T1, SCL[:, 0, :], MODX[:, 0, 0:8])
            operand(T2, SCL[:, 1, :], MODC[:, 0:8])

            def copy_feat(name, dst):
                o = take(name)
                freed(act.activation(dst, o[:, :].rearrange("p (j t) -> p j t", j=2), ACT.Copy), name)

            for j in range(2):
                copy_feat(f"dkc{j}", kdT[:, 2 * j:2 * j + 2, 0:T])
            for n, t in (("dv0", 2), ("dv1", 3), ("dvc0", 0), ("dvc1", 1)):
                o = take(n)
                freed(act.activation(vd[:, t, :], o[:, :], ACT.Copy), n)
            act.wait_ge(sem("consts_in"), 16 * 14)
            o = take("ig")
            m = act.activation(gi, o[0:GR, :], ACT.Identity, bias=gbias[:, 0:1])
            freed(m, "ig")
            act.wait_ge(sem(f"bank_read{bank_of['ig'][0]}"), bank_of["ig"][1] + 1)
            o = take("fg")
            m = act.activation(gf, o[0:GR, :], ACT.Identity, bias=gbias[:, 1:2])
            freed(m, "fg")
            act.wait_ge(sem(f"bank_read{bank_of['fg'][0]}"), bank_of["fg"][1] + 1)
            step(act.activation(gt_, gf, ACT.Abs))
            step(act.activation(gt_, gt_, ACT.Exp, scale=-1.0))
            step(act.activation(gt_, gt_, ACT.Ln, bias=1.0), "gate_logs")
            for i, n in enumerate(("mk0", "mk1", "mkc0", "mkc1", "mq0", "mq1")):
                act.wait_ge(sem("conv3"), i + 1)
                j = int(n[-1])
                src = CV[:, i % 2, :].rearrange("p (j t) -> p j t", j=2)
                if n[1] == "k":
                    lo = 0 if "c" in n else T
                    step(act.activation(kT[:, 2 * j:2 * j + 2, lo:lo + T], src, ACT.Silu), "conv3_read")
                else:
                    for t in range(TT):
                        m = act.activation(qT[:, 2 * j:2 * j + 2, (1 - t) * P:(2 - t) * P], src[:, :, t * P:(t + 1) * P], ACT.Silu)
                    step(m, "conv3_read")
            act.wait_ge(sem("masks_made"), 1)
            for n, s in (("mv0", 2), ("mv1", 3), ("mvc0", 0), ("mvc1", 1)):
                o = take(n)
                freed(act.activation(vaug[:, s, :, 0:MD], o[:, :].rearrange("p (h d) -> p h d", h=MH), ACT.Copy), n)
            for t in range(TT):
                o = take(f"mo{t}")
                freed(act.activation(osig[:, t, :], o[:, :], ACT.Sigmoid), f"mo{t}")
            for b in range(2):
                copy_feat(f"dqT{b}", qdT[:, 2 * b:2 * b + 2, :])
            for b in range(2):
                copy_feat(f"dkT{b}", kdT[:, 2 * b:2 * b + 2, T:2 * T])
            step(act.activation(sm[:, 500:501], sm[:, 500:501], ACT.Copy), "diff_operands")
            act.wait_ge(sem("gate_sums"), 1)
            step(act.activation(gE, gE, ACT.Exp), "gate_rows")
            act.wait_ge(sem("lambdas"), 1)
            step(act.activation(sm[:, 40:42], sm[:, 40:42], ACT.Exp), "lambda_exp")
            for u in range(2 * DH):
                act.wait_ge(sem("diff_bias"), u + 1)
                if u >= 2:
                    act.wait_ge(sem("diff_prob"), u - 1)
                for i in range(2):
                    act.activation(EX[:, u % 2, i, :], banks[4 + i][:, :], ACT.Exp, scale=DQ ** -0.5,
                                   bias=sm[:, 48 + 2 * (u % 2) + i:49 + 2 * (u % 2) + i],
                                   accum_out=sm[:, 52 + 2 * (u % 2) + i:53 + 2 * (u % 2) + i]).then_inc(sem("diff_exp"), 1)
                if u >= 1:
                    act.wait_ge(sem("diff_turned"), u)
                    if u >= 3:
                        act.wait_ge(sem("diff_summed"), u - 2)
                    act.activation(PT[:, (u - 1) % 2, :], banks[6][:, :], ACT.Copy).then_inc(sem("diff_prob_turned"), 1)
            act.wait_ge(sem("diff_turned"), 2 * DH)
            act.activation(PT[:, 1, :], banks[6][:, :], ACT.Copy).then_inc(sem("diff_prob_turned"), 1)
            def mlstm_evict(h):
                act.wait_ge(sem("mlstm_summed"), h + 1)
                step(act.activation(HR[:, h, :, :], banks[7][:, 0:4 * (MD + 1)].rearrange("p (a d) -> p a d", a=4), ACT.Copy),
                     "mlstm_out")
            act.wait_ge(sem("diff_out"), 2 * DH)
            act.wait_ge(sem("gate_cols"), 1)
            for h in range(MH):
                act.wait_ge(sem("mlstm_scored"), h + 1)
                if h:
                    act.wait_ge(sem("mlstm_summed"), h)
                act.wait_ge(sem("mlstm_args"), 2 * h + 2)
                for d in range(2):
                    for s in range(2):
                        act.activation(WD[:, d, s * T:(s + 1) * T], banks[6][:, d * T:(d + 1) * T], ACT.Exp,
                                       bias=GCt[:, s, 32 * d + h:32 * d + h + 1])
                    act.activation(WD[:, d, 2 * T:896], AR[:, d, :], ACT.Exp).then_inc(sem("mlstm_exp"), 1)
                if h:
                    mlstm_evict(h - 1)
            mlstm_evict(MH - 1)

            def evict_tok(name, n, t):
                o = take(f"{name}{n}{t}")
                act.activation(XN[:, t, n * NCH:(n + 1) * NCH], o[:, :], ACT.Copy).then_inc(
                    sem(f"bank_read{bank_of[f'{name}{n}{t}'][0]}"), 1)

            root()
            root()
            operand(T1)
            for n in range(2):
                for t in range(TT):
                    evict_tok("wo", n, t)
            root()
            root()
            operand(T1, SCL[:, 2, :], MODX[:, 0, 24:32])

            def hidden(n_steps, hid0, it, hper):
                for st in range(n_steps):
                    for t in range(TT):
                        act.wait_ge(sem(f"upped{t}"), hid0 + hper * it + st + 1)
                        if not (isinstance(it, int) and hid0 + st == 0):
                            act.wait_ge(sem(f"hidden{t}"), hid0 + hper * it + st)
                        act.activation(SG[:, t, :], banks[t][:, 0:FSTEP], ACT.Silu).then_inc(sem(f"silued{t}"), 1)
                        if st or t:
                            turned_h(1 - t, hid0 + hper * it + (st if t else st - 1), isinstance(it, int) and hid0 + (st if t else st - 1) == 0)
                turned_h(1, hid0 + hper * it + n_steps - 1, False)

            def turned_h(t, n, first):
                act.wait_ge(sem(f"turned_h{t}"), n + 1)
                if not first:
                    act.wait_ge(sem(f"down_done{t}"), n)
                act.activation(HT[:, t, :, :], banks[2 + t][:, 0:2 * P].rearrange("p (j n) -> p j n", j=2),
                               ACT.Copy).then_inc(sem(f"hidden_turned{t}"), 1)

            hidden(NSTEP, 0, 0, NSTEP)
            for t in range(TT):
                act.wait_ge(sem(f"down_done{t}"), NSTEP)
                for n in range(2):
                    m = act.activation(XN[:, t, n * NCH:(n + 1) * NCH], banks[4 + 2 * t + n][:, :], ACT.Copy)
                m.then_inc(sem(f"summed_read{t}"), 1)
            root()
            root()
            operand(T1, SCL[:, 3, :], MODX[:, 1, 0:8])
            for c in range(2):
                for j in range(2):
                    i = 2 * c + j
                    o = take(f"pg{c}{j}")
                    if i >= 2:
                        act.wait_ge(sem("glu"), i - 1)
                    for q in range(2):
                        k = 4 * c + 2 * j + q
                        m = act.activation(SGC[:, i % 2, q * T:(q + 1) * T], o[:, q * T:(q + 1) * T], ACT.Sigmoid,
                                           bias=PCOL[:, 1, 56 + k:57 + k])
                    freed(m, f"pg{c}{j}")
            for b in range(4):
                act.wait_ge(sem("turned"), 4 * turn[0] + b + 1)
                act.activation(XN[:, b // 2, (b % 2) * NCH:(b % 2 + 1) * NCH], banks[4 + b][:, :], ACT.Copy).then_inc(
                    sem("turned_read"), 1)
                cnt["turned_read"] += 1
            turn[0] += 1
            root()
            act.wait_ge(sem("conv_normed"), 1)
            for t in range(TT):
                m = act.activation(XN[:, t, :], XN[:, t, :], ACT.Silu)
            act.wait_ge(sem("normed"), 4)
            m.then_inc(sem("normed"), 1)
            operand(T1)
            root()
            root()
            operand(T1, SCL[:, 4, :], MODX[:, 1, 24:32])
            act.wait_ge(sem("router_max"), 1)
            for t in range(TT):
                m = act.activation(gates[:, t, 0:NE1], gates[:, t, 0:NE1], ACT.Exp, bias=sm[:, 60 + t:61 + t])
            step(m, "router_act")
            with act.Fori(0, NE1) as e:
                hidden(NSTEP, NSTEP, e, NSTEP)
            root()
            operand(memT)
            o = take("sguT")
            freed(act.activation(sguT, o[:, :].rearrange("p (h i) -> p h i", h=XH), ACT.Copy), "sguT")
            for l in range(2):
                for j in range(2):
                    copy_feat(f"kv{l}k{j}", kmT[:, l, 2 * j:2 * j + 2, :])
                for j in range(2):
                    o = take(f"kv{l}v{j}")
                    freed(act.activation(vm[:, l, j, :], o[:, :], ACT.Copy), f"kv{l}v{j}")
            operand(T1)
            for n in range(2):
                for t in range(TT):
                    o = take(f"za{n}{t}")
                    freed(act.activation(UV[:, t, n, :], o[:, :], ACT.Gelu), f"za{n}{t}")
            step(act.activation(sm[:, 500:501], sm[:, 500:501], ACT.Copy), "gelu_done")
            for j in range(2):
                copy_feat(f"za2{j}", xqT[:, 2 * j:2 * j + 2, :])
            step(act.activation(sm[:, 500:501], sm[:, 500:501], ACT.Copy), "memory_operands")

            def memory_attention(units):
                for h in range(XH + 1):
                    u = units + h
                    if h < XH:
                        act.wait_ge(sem("mem_bias"), u + 1)
                        if u >= 2:
                            act.wait_ge(sem("mem_turned"), u - 1)
                        for t in range(TT):
                            c = 2 * (u % 2) + t
                            act.activation(EM[:, h % 2, t, :], banks[4 + h % 2][:, t * T:(t + 1) * T], ACT.Exp, scale=P ** -0.5,
                                           bias=sm[:, 48 + c:49 + c], accum_out=sm[:, 52 + c:53 + c]).then_inc(sem("mem_exp"), 1)
                    if h:
                        act.wait_ge(sem("mem_turned"), u)
                        if u >= 3:
                            act.wait_ge(sem("mem_summed"), u - 2)
                        act.activation(PMT[:, (h - 1) % 2, :, :], banks[6][:, :].rearrange("p (c t) -> p c t", c=2),
                                       ACT.Copy).then_inc(sem("mem_prob_turned"), 1)
                        act.wait_ge(sem("mem_summed"), u)
                        step(act.activation(T2[:, 4 + h - 1, :], banks[7][:, 0:T], ACT.Copy), "mem_out")

            wait_output(act, "kv1v1")
            memory_attention(0)
            root()
            act.wait_ge(sem("gated_tokens"), 1)
            for b in range(2):
                copy_feat(f"tokT{b}", T2[:, 2 * b:2 * b + 2, :])
            step(act.activation(sm[:, 500:501], sm[:, 500:501], ACT.Copy), "cat_ready")
            root()
            operand(T1)
            for l, name in ((0, "A"), (1, "B")):
                o = take(f"rt{name}")
                m = act.activation(gates[:, :, :], o[:, 0:TT * NE2].rearrange("p (t e) -> p t e", t=TT), ACT.Sigmoid)
                freed(m, f"rt{name}")
                with act.Fori(0, NE2 // 2) as i:
                    for u in range(2):
                        hidden(NSTEP2, NSTEP * (1 + NE1) + l * NE2 * NSTEP2 + u * NSTEP2, i, 2 * NSTEP2)
                root()
                if l == 0:
                    operand(T1)
                    for j in range(2):
                        copy_feat(f"zb0{j}", bgT[:, 2 * j:2 * j + 2, :])
                    for j in range(2):
                        copy_feat(f"zb1{j}", cgT[:, 2 * j:2 * j + 2, :])
                    step(act.activation(sm[:, 500:501], sm[:, 500:501], ACT.Copy), "conv_gates")
                    for j in range(2):
                        copy_feat(f"zb3{j}", xqT[:, 2 * j:2 * j + 2, :])
                    step(act.activation(sm[:, 500:501], sm[:, 500:501], ACT.Copy), "memory_operands")
                    memory_attention(XH)
                    root()
                    operand(T1)

        @block.vector
        def _(dve):
            cnt = {}

            def step(ins, name="dve_step"):
                cnt[name] = cnt.get(name, 0) + 1
                ins.then_inc(sem(name), 1)
                dve.wait_ge(sem(name), cnt[name])

            def take(name):
                b, n = bank_of[name]
                dve.wait_ge(sem(f"bank_ready{b}"), n + 1)
                return banks[b]

            def free(ins, name):
                b, n = bank_of[name]
                ins.then_inc(sem(f"bank_read{b}"), 1)
                dve.wait_ge(sem(f"bank_read{b}"), n + 1)

            def invert_root():
                n = cnt.get("variance", 0)
                dve.wait_ge(sem("rooted"), n)
                step(dve.reciprocal(sm[:, 64:80], sm[:, 16:32]))

            stats = sm[:, 96:96 + 24].rearrange("p (t c s) -> p t c s", t=2, c=2)
            mv = sm[:, 120:124].rearrange("p (t s) -> p t s", t=2)
            junk = sm[:, 124:125]

            def rms(src, eps=EPS):
                for t in range(TT):
                    for c in range(2):
                        m = dve.bn_stats(stats[:, t, c, :], src[:, t, c * NCH:(c + 1) * NCH])
                step(m)
                for t in range(TT):
                    m = dve.bn_aggr(mv[:, t, :], stats[:, t, :, :])
                step(m)
                for t in range(TT):
                    m = dve.scalar_tensor_tensor(sm[:, 32 + t:33 + t], mv[:, t, 0:1], mv[:, t, 0:1], mv[:, t, 1:2], ALU.mult, ALU.add)
                step(m)
                step(dve.tensor_scalar(sm[:, 0:2], sm[:, 32:34], eps, None, ALU.add), "variance")
                invert_root()

            def layer_norm(src, dst, g, b, eps, width):
                nb = width // NCH
                for t in range(TT):
                    for c in range(nb):
                        m = dve.bn_stats(stats[:, t, c, :], src[:, t, c * NCH:(c + 1) * NCH])
                step(m)
                for t in range(TT):
                    m = dve.bn_aggr(mv[:, t, :], stats[:, t, 0:nb, :])
                step(m)
                step(dve.tensor_scalar(sm[:, 0:2], mv[:, :, 1], eps, None, ALU.add), "variance")
                invert_root()
                for t in range(TT):
                    m = dve.tensor_scalar(src[:, t, :], src[:, t, :], mv[:, t, 0:1], sm[:, 64 + t:65 + t], ALU.subtract, ALU.mult)
                step(m)
                for t in range(TT):
                    m = dve.tensor_tensor(src[:, t, :], src[:, t, :], g, ALU.mult)
                step(m)
                for t in range(TT):
                    m = dve.tensor_tensor(dst[:, t, :], src[:, t, :], b, ALU.add)
                return m

            def scale_rows(dst, src, name="normed"):
                for t in range(TT):
                    m = dve.tensor_scalar(dst[:, t, :], src[:, t, :], sm[:, 64 + t:65 + t], None, ALU.mult)
                step(m, name)

            def post(g):
                rms(XN)
                for t in range(TT):
                    m = dve.scalar_tensor_tensor(XN[:, t, :], XN[:, t, :], sm[:, 64 + t:65 + t], GP[:, g, :], ALU.mult, ALU.mult)
                step(m)
                for t in range(TT):
                    m = dve.tensor_tensor(X[:, t, :], X[:, t, :], XN[:, t, :], ALU.add)
                step(m, "x_updated")

            step(dve.memset(sm[:, :], 1.0), "scratch_set")
            dve.wait_ge(sem("cols_turned"), 1)
            for i, n in enumerate((P, 80, P, TAPS * KC - P)):
                m = dve.tensor_copy(PCOL[:, i, 0:n], banks[7][:, i * P:i * P + n])
            step(m, "cols_read")
            dve.wait_ge(sem("x_loaded"), 16)
            rms(X)
            scale_rows(XN, X)
            dve.wait_ge(sem("ctx_loaded"), 16)
            rms(TOK)
            scale_rows(TOK, TOK)
            dve.wait_ge(sem("silu_c"), 1)
            step(dve.tensor_copy(CB[:, :, :], CT[:, :, 0:1].broadcast_to([P, KC, P])), "c_spread")

            row_jobs = [0]

            def mod_job(name):
                l, c = int(name[3]), int(name[5:])
                o = take(name)
                if c in (4, 5, 10, 11):
                    row_jobs[0] += 1
                    dve.wait_ge(sem("rows_in"), 32 * row_jobs[0])
                    dst = GP[:, int(c > 5), (c % 2) * NCH:(c % 2 + 1) * NCH]
                    free(dve.tensor_tensor(dst, o[:, :], RB[:, 0, :], ALU.add), name)
                    step(dve.tensor_tensor(dst, dst, RB[:, 1, :], ALU.mult), "rows_used")
                    return
                v = o[:, 0:8].rearrange("p (j c) -> p c j", c=2)
                b = PCOL[:, 0, 64 * l + 4 * c:64 * l + 4 * c + 4]
                m = dve.tensor_tensor(MODX[:, l, 4 * c:4 * c + 4], v[:, 0, :], b, ALU.add)
                if l == 0 and c < 4:
                    step(m)
                    m = dve.tensor_tensor(MODC[:, 4 * c:4 * c + 4], v[:, 1, :], b, ALU.add)
                free(m, name)

            def gains(i, l, which, sc):
                g = PCOL[:, 0, 64 * l + 48 + 8 * which:64 * l + 56 + 8 * which]
                return dve.scalar_tensor_tensor(SCL[:, i, :], sc, 1.0, g, ALU.add, ALU.mult)

            for c in range(4):
                mod_job(f"mod0_{c}")
            gains(0, 0, 0, MODX[:, 0, 8:16])
            step(gains(1, 0, 0, MODC[:, 8:16]), "mod_cols")
            dve.wait_ge(sem("consts_in"), 16 * 14)
            for i, n in enumerate("qk"):
                for t in range(TT):
                    o = take(f"d{n}{t}")
                    v = XN[:, t, i * NCH:(i + 1) * NCH]
                    if i == 0 and t == 0:
                        dve.wait_ge(sem("turned"), 4)
                    c = rope[:, t:t + 1, 0, :].broadcast_to([P, 8, 64])
                    dve.tensor_tensor(v.rearrange("p (g d) -> p g d", g=8), o[:, :].rearrange("p (g d) -> p g d", g=8), c, ALU.mult)
                    ov = o[:, :].rearrange("p (g a f d) -> p g a f d", g=8, a=2, f=2)
                    tv = TOK[:, t, i * NCH:(i + 1) * NCH].rearrange("p (g a f d) -> p g a f d", g=8, a=2, f=2)
                    sv = rope[:, t, 1, :].rearrange("p (b a f d) -> p b a f d", b=1, a=2, f=2)
                    if i == 0 and t == 0:
                        dve.wait_ge(sem("turned"), 8)
                    for f in range(2):
                        m = dve.tensor_tensor(tv[:, :, :, f, :], ov[:, :, :, 1 - f, :], sv[:, :, :, f, :].broadcast_to([P, 8, 2, 16]), ALU.mult)
                    free(m, f"d{n}{t}")
                    m = dve.tensor_tensor(v, v, TOK[:, t, i * NCH:(i + 1) * NCH], ALU.add)
                step(m, "rotated")
            s = g_at["gates"][0]
            dve.wait_ge(sem("gate_pad"), 1)
            dve.wait_ge(sem("masks_made"), 1)
            dve.wait_ge(sem(f"chunk_in{s}"), 16 * (g_at["gates"][1] + 1))
            for d in range(2):
                for w in range(2):
                    m = dve.tensor_copy(WG[:, :, w, 32 * d:32 * d + 8], ring[:, s, :, 16 * d + 8 * w:16 * d + 8 * w + 8])
            step(m, "gate_weights")
            for i, n in enumerate(("mk0", "mk1", "mkc0", "mkc1", "mq0", "mq1")):
                j = int(n[-1])
                o = take(n)
                if i >= 2:
                    dve.wait_ge(sem("conv3_read"), i - 1)
                cv = CV[:, i % 2, :].rearrange("p (j t) -> p j t", j=2)
                ov = o[:, :].rearrange("p (j t) -> p j t", j=2)
                col = lambda tap, q: PCOL[:, 1, 16 + 8 * tap + (4 if n[1] == "k" else 0) + 2 * j + q:
                                          17 + 8 * tap + (4 if n[1] == "k" else 0) + 2 * j + q]
                for q in range(2):
                    m = dve.tensor_scalar(cv[:, q, :], ov[:, q, :], col(1, q), None, ALU.mult)
                step(m)
                for q in range(2):
                    m = dve.scalar_tensor_tensor(cv[:, q, 1:T], ov[:, q, 0:T - 1], col(0, q), cv[:, q, 1:T], ALU.mult, ALU.add)
                step(m)
                for q in range(2):
                    m = dve.scalar_tensor_tensor(cv[:, q, 0:T - 1], ov[:, q, 1:T], col(2, q), cv[:, q, 0:T - 1], ALU.mult, ALU.add)
                free(m, n)
                step(dve.memset(junk, 0.0), "conv3")
            dve.wait_ge(sem("gate_logs"), 1)
            step(dve.tensor_scalar(gf, gf, 0.0, None, ALU.min))
            step(dve.tensor_tensor(gf, gf, gt_, ALU.subtract))
            fw, bw = slice(0, 8), slice(32, 40)

            def scans(dst, src, data0, op0, op1):
                c, s = slice(0, T), slice(T, 2 * T)
                init = 0.0 if op0 == ALU.mult else -3e38
                dve.tensor_tensor_scan(dst[fw, :], data0[fw, :], src[fw, :], init, op0, op1)
                step(dve.tensor_tensor_scan(dst[bw, T - 1::-1], data0[bw, T - 1::-1], src[bw, T - 1::-1], init, op0, op1))
                step(dve.tensor_tensor_scan(dst[bw, 2 * T - 1:T - 1:-1], data0[bw, 2 * T - 1:T - 1:-1],
                                            src[bw, 2 * T - 1:T - 1:-1], dst[bw, 0:1], op0, op1))

            step(dve.memset(gB, 0.0))
            scans(gB, gf, onesr, ALU.mult, ALU.add)
            step(dve.tensor_tensor(gG, gi, gB, ALU.subtract))
            step(dve.memset(gt_, 0.0))
            scans(gt_, gG, gG, ALU.max, ALU.max)
            for t in range(TT):
                m = dve.tensor_scalar(nM[:, (1 - t) * P:(2 - t) * P], gt_[:, T + t * P:T + (t + 1) * P], -1.0, None, ALU.mult)
            step(m)
            step(dve.scalar_tensor_tensor(gE, gB[:, T:2 * T], -1.0, gt_[:, T:2 * T], ALU.mult, ALU.subtract))
            step(dve.tensor_scalar(gE, gE, 80.0, None, ALU.min), "gate_sums")
            for i in range(2):
                m = dve.tensor_tensor(lamv[:, 2 * i, :], lamv[:, 2 * i, :], lamv[:, 2 * i + 1, :], ALU.mult)
            step(m)
            for i in range(2):
                m = dve.reduce_sum(sm[:, 40 + i:41 + i], lamv[:, 2 * i, :], axis=AX.X)
            step(m, "lambdas")
            dve.wait_ge(sem("lambda_exp"), 1)
            step(dve.tensor_tensor(sm[:, 42:43], sm[:, 40:41], sm[:, 41:42], ALU.subtract))
            step(dve.tensor_scalar(sm[:, 43:44], sm[:, 42:43], LAM_INIT, -1.0, ALU.add, ALU.mult))
            o = take("gT")
            free(dve.tensor_copy(GCt[:, :, :], o[:, 0:6 * GR].rearrange("p (a n) -> p a n", a=6)), "gT")
            wait_output(dve, "mo1")
            for d in range(2):
                m = dve.tensor_copy(SEL[0:GR, d * MH:(d + 1) * MH, :],
                                    ident[0:GR, 32 * d:32 * d + MH].rearrange("p (h a) -> p h a", a=1).broadcast_to([GR, MH, P]))
            step(m)
            step(dve.memset(junk, 0.0), "gate_cols")
            def diff_bias(u):
                c = 2 * (u % 2)
                for i in range(2):
                    dve.wait_ge(sem("diff_scored"), 2 * u + i + 1)
                    m = dve.reduce_max(sm[:, 44 + i:45 + i], banks[4 + i][:, :], axis=AX.X)
                step(m)
                step(dve.tensor_scalar(sm[:, 48 + c:50 + c], sm[:, 44:46], -(DQ ** -0.5), None, ALU.mult), "diff_bias")

            def diff_prob(u):
                c = 2 * (u % 2)
                dve.wait_ge(sem("diff_exp"), 2 * u + 2)
                step(dve.reciprocal(sm[:, 56:58], sm[:, 52 + c:54 + c]))
                step(dve.tensor_tensor(sm[:, 57:58], sm[:, 57:58], sm[:, 43:44], ALU.mult))
                step(dve.tensor_scalar(EX[:, u % 2, 1, :], EX[:, u % 2, 1, :], sm[:, 57:58], None, ALU.mult))
                if u >= 2:
                    dve.wait_ge(sem("diff_turned"), u - 1)
                step(dve.scalar_tensor_tensor(PR[:, u % 2, :], EX[:, u % 2, 0, :], sm[:, 56:57], EX[:, u % 2, 1, :], ALU.mult, ALU.add),
                     "diff_prob")

            def diff_out(u):
                h, t = divmod(u, TT)
                dve.wait_ge(sem("diff_summed"), u + 1)
                step(dve.tensor_copy(TOK[:, t, NCH + h * DV:NCH + (h + 1) * DV], banks[7][:, 0:DV]), "diff_out")

            diff_bias(0)
            for u in range(2 * DH):
                diff_prob(u)
                if u + 1 < 2 * DH:
                    diff_bias(u + 1)
                for f in fills_at(u):
                    mod_job(f)
                diff_out(u)
            dve.wait_ge(sem(f"bank_read{bank_of['mo1'][0]}"), bank_of["mo1"][1] + 1)
            step(dve.memset(junk, 0.0), "mlstm_operands")
            for h in range(MH):
                dve.wait_ge(sem("mlstm_scored"), h + 1)
                for d, msk in enumerate((mskf, mskb)):
                    at = 32 * d + h
                    lo = d * T
                    if h:
                        dve.wait_ge(sem("mlstm_exp"), 2 * (h - 1) + d + 1)
                    if d == 0:
                        parts = ((2, slice(0, 256), slice(0, 2), slice(lo, lo + 256)), (3, slice(256, 384), slice(2, 3), slice(lo, lo + 128)))
                    else:
                        parts = ((2, slice(0, 128), slice(0, 1), slice(lo + 128, lo + 256)), (3, slice(128, 384), slice(1, 3), slice(lo, lo + 256)))
                    for s, a, q, b in parts:
                        m = dve.scalar_tensor_tensor(AR[:, d, a], banks[6][:, b], GCt[:, s, at:at + 1],
                                                     msk[:, q, :].rearrange("p a n -> p (a n)"), ALU.add, ALU.min)
                    step(m, "mlstm_args")
                for d in range(2):
                    dve.wait_ge(sem("mlstm_exp"), 2 * h + d + 1)
                    dve.scalar_tensor_tensor(WD[:, d, 0:512], banks[4][:, :], MD ** -0.5, WD[:, d, 0:512], ALU.mult, ALU.mult)
                    step(dve.scalar_tensor_tensor(WD[:, d, 512:896], banks[5][:, d * P:d * P + 384], MD ** -0.5, WD[:, d, 512:896],
                                                  ALU.mult, ALU.mult), "mlstm_weighted")
                for f in fills_at(2 * DH + h):
                    mod_job(f)
            gains(2, 0, 1, MODX[:, 0, 32:40])
            gains(3, 1, 0, MODX[:, 1, 8:16])
            step(gains(4, 1, 1, MODX[:, 1, 32:40]))
            dve.wait_ge(sem("mlstm_out"), MH)
            DN = sm[:, 128:128 + 32].rearrange("p (a h) -> p a h", a=4)
            for a in range(4):
                m = dve.scalar_tensor_tensor(DN[:, a, :], HR[:, :, a, MD], -1.0, HR[:, :, a, MD], ALU.mult, ALU.max)
            step(m)
            for a in range(4):
                d, t = divmod(a, TT)
                m = dve.tensor_tensor(DN[:, a, :], DN[:, a, :], GCt[:, 4 + t, 32 * d:32 * d + MH], ALU.max)
            step(m)
            step(dve.reciprocal(sm[:, 128:160], sm[:, 128:160]))
            for a in range(4):
                m = dve.tensor_tensor(HR[:, :, a, 0:MD], HR[:, :, a, 0:MD],
                                      DN[:, a, :].rearrange("p (h a) -> p h a", a=1).broadcast_to([P, MH, MD]), ALU.mult)
            step(m)
            for t in range(TT):
                m = dve.tensor_tensor(TOK[:, t, 0:NCH].rearrange("p (h d) -> p h d", h=MH), HR[:, :, t, 0:MD], HR[:, :, 2 + t, 0:MD], ALU.add)
            step(m)
            for t in range(TT):
                m = dve.tensor_tensor(XN[:, t, :], TOK[:, t, :], TOK[:, t, :], ALU.mult)
            step(m)
            hs = sm[:, 160:184].rearrange("p (t n) -> p t n", t=TT)
            for t in range(TT):
                dve.tensor_reduce(hs[:, t, 0:8], XN[:, t, 0:NCH].rearrange("p (h d) -> p h d", h=8), axis=AX.X, op=ALU.add)
                m = dve.tensor_reduce(hs[:, t, 8:12], XN[:, t, NCH:D].rearrange("p (h d) -> p h d", h=4), axis=AX.X, op=ALU.add)
            step(m)
            step(dve.tensor_scalar(sm[:, 0:16].rearrange("p (t n) -> p t n", t=TT), hs[:, :, 0:8], 1.0 / MD, EPS, ALU.mult, ALU.add))
            step(dve.tensor_scalar(sm[:, 184:192].rearrange("p (t n) -> p t n", t=TT), hs[:, :, 8:12], 1.0 / DV, EPS, ALU.mult, ALU.add), "variance")
            invert_root()
            step(dve.tensor_copy(sm[:, 192:208], sm[:, 64:80]))
            step(dve.tensor_copy(sm[:, 0:8], sm[:, 184:192]), "variance")
            invert_root()
            for t in range(TT):
                a = sm[:, 192 + 8 * t:200 + 8 * t].rearrange("p (h a) -> p h a", a=1).broadcast_to([P, 8, MD])
                b = sm[:, 64 + 4 * t:68 + 4 * t].rearrange("p (h a) -> p h a", a=1).broadcast_to([P, 4, DV])
                dve.tensor_tensor(TOK[:, t, 0:NCH].rearrange("p (h d) -> p h d", h=8), TOK[:, t, 0:NCH].rearrange("p (h d) -> p h d", h=8), a, ALU.mult)
                m = dve.tensor_tensor(TOK[:, t, NCH:D].rearrange("p (h d) -> p h d", h=4), TOK[:, t, NCH:D].rearrange("p (h d) -> p h d", h=4), b, ALU.mult)
            step(m)
            for t in range(TT):
                m = dve.tensor_tensor(TOK[:, t, :], TOK[:, t, :], RS[:, 0, :], ALU.mult)
            step(m)
            for t in range(TT):
                dve.tensor_tensor(TOK[:, t, 0:NCH], TOK[:, t, 0:NCH], osig[:, t, :], ALU.mult)
                m = dve.tensor_scalar(TOK[:, t, NCH:D], TOK[:, t, NCH:D], 1.0 - LAM_INIT, None, ALU.mult)
            step(m, "mixed")

            def wait_taken(prefix):
                for n in range(2):
                    for t in range(TT):
                        b, k = bank_of[f"{prefix}{n}{t}"]
                        dve.wait_ge(sem(f"bank_read{b}"), k + 1)

            wait_taken("wo")
            post(0)
            rms(X)
            scale_rows(XN, X)

            def hidden(n_steps, hid0, it, hper):
                for st in range(n_steps):
                    for t in range(TT):
                        dve.wait_ge(sem(f"silued{t}"), hid0 + hper * it + st + 1)
                        if not (isinstance(it, int) and hid0 + st == 0):
                            dve.wait_ge(sem(f"turned_h{t}"), hid0 + hper * it + st)
                        dve.tensor_tensor(H[:, t, :], SG[:, t, :], banks[t][:, FSTEP:NCH], ALU.mult).then_inc(sem(f"hidden{t}"), 1)

            hidden(NSTEP, 0, 0, NSTEP)
            for t in range(TT):
                dve.wait_ge(sem(f"summed_read{t}"), 1)
            post(1)
            rms(X)
            scale_rows(XN, X)
            dve.wait_ge(sem("margins"), 2)
            for c in range(2):
                for j in range(2):
                    b, k = bank_of[f"pg{c}{j}"]
                    dve.wait_ge(sem(f"bank_read{b}"), k + 1)
                    o = take(f"pa{c}{j}")
                    i = 2 * c + j
                    for q in range(2):
                        k = 4 * c + 2 * j + q
                        m = dve.scalar_tensor_tensor(hT[:, k, TAPS // 2:TAPS // 2 + T], o[:, q * T:(q + 1) * T], PCOL[:, 1, 48 + k:49 + k],
                                                     SGC[:, i % 2, q * T:(q + 1) * T], ALU.add, ALU.mult)
                    free(m, f"pa{c}{j}")
                    step(dve.memset(junk, 0.0), "glu")
            dve.wait_ge(sem("operand_ready"), 5)
            for tap in range(TAPS):
                for k in range(KC):
                    r = tap * KC + k
                    w = PCOL[:, 2 + r // P, r % P:r % P + 1]
                    if tap == 0:
                        dve.tensor_scalar(T2[:, k, :], hT[:, k, 0:T], w, PCOL[:, 1, 40 + k:41 + k], ALU.mult, ALU.add).then_inc(sem("tap"), 1)
                    else:
                        dve.wait_ge(sem("tap"), r - KC + 1)
                        dve.scalar_tensor_tensor(T2[:, k, :], hT[:, k, tap:tap + T], w, T2[:, k, :], ALU.mult, ALU.add).then_inc(sem("tap"), 1)
            dve.wait_ge(sem("tap"), TAPS * KC)
            step(dve.memset(junk, 0.0), "convolved")
            for f in LATE:
                mod_job(f)
            dve.wait_ge(sem("turned_read"), 4 * 6)
            dve.wait_ge(sem("params_in"), 16 * 5)
            step(layer_norm(XN, XN, RS[:, 1, :], RS[:, 2, :], EPS, D), "conv_normed")
            for n in range(2):
                for t in range(TT):
                    o = take(f"pw2{n}{t}")
                    free(dve.tensor_tensor(XN[:, t, n * NCH:(n + 1) * NCH], o[:, :], RS[:, 3, n * NCH:(n + 1) * NCH], ALU.add), f"pw2{n}{t}")
            post(0)
            rms(X)
            cnt["normed"] += 1
            scale_rows(XN, X)

            def ranks(dst, v, g, n, scratch):
                a = v.rearrange("p (g a j) -> p g a j", g=g, a=1).broadcast_to([P, g, n, n])
                b = v.rearrange("p (g e a) -> p g e a", g=g, a=1).broadcast_to([P, g, n, n])
                s0 = scratch[0].rearrange("p (g e j) -> p g e j", g=g, e=n)
                s1 = scratch[1].rearrange("p (g e j) -> p g e j", g=g, e=n)
                dve.tensor_tensor(s0, a, b, ALU.is_gt)
                step(dve.tensor_tensor(s1, a, b, ALU.is_equal))
                tri = tri8[:, 0:n, 0:n].rearrange("p (a e) j -> p a e j", a=1).broadcast_to([P, g, n, n])
                step(dve.tensor_tensor(s1, s1, tri, ALU.mult))
                step(dve.tensor_tensor(s0, s0, s1, ALU.add))
                step(dve.tensor_reduce(dst, s0, axis=AX.X, op=ALU.add))

            o = take("rt1")
            free(dve.tensor_copy(gates[:, :, 0:NE1], o[:, 0:TT * NE1].rearrange("p (t e) -> p t e", t=TT)), "rt1")
            R1 = sm[:, 208:224].rearrange("p (t e) -> p t e", t=TT)
            for t in range(TT):
                ranks(R1[:, t, :], gates[:, t, 0:NE1], 1, NE1, (rk[:, 0, 0:64], rk[:, 1, 0:64]))
            step(dve.tensor_scalar(sm[:, 208:224], sm[:, 208:224], 2.0, None, ALU.is_lt))
            step(dve.reduce_max(sm[:, 62:64], gates[:, :, 0:NE1], axis=AX.X))
            step(dve.tensor_scalar(sm[:, 60:62], sm[:, 62:64], -1.0, None, ALU.mult), "router_max")
            dve.wait_ge(sem("router_act"), 1)
            step(dve.tensor_tensor(gates[:, :, 0:NE1], gates[:, :, 0:NE1], R1, ALU.mult))
            step(dve.reduce_sum(sm[:, 62:64], gates[:, :, 0:NE1], axis=AX.X))
            step(dve.reciprocal(sm[:, 62:64], sm[:, 62:64]))
            for t in range(TT):
                m = dve.tensor_scalar(gates[:, t, 0:NE1], gates[:, t, 0:NE1], sm[:, 62 + t:63 + t], None, ALU.mult)
            step(m)
            step(dve.memset(TOK[:, :, :], 0.0))

            def add_expert(e, n_done, y, dst, ny):
                for t in range(TT):
                    dve.wait_ge(sem(f"down_done{t}"), n_done)
                    dve.memset(junk, 0.0)
                    dve.tensor_scalar(gcol[:, t:t + 1], gates[:, t, bass.ds(e, 1)], 1.0, None, ALU.mult).then_inc(sem("gate_picked"), 1)
                    dve.wait_ge(sem("gate_picked"), ny * TT + t + 1)
                    for n in range(2):
                        v = dst[:, t, n * NCH:(n + 1) * NCH]
                        m = dve.scalar_tensor_tensor(v, banks[4 + 2 * t + n][:, :], gcol[:, t:t + 1], v, ALU.mult, ALU.add)
                    m.then_inc(sem(f"summed_read{t}"), 1)
                    dve.wait_ge(sem(f"summed_read{t}"), y)

            with dve.Fori(0, NE1) as e:
                hidden(NSTEP, NSTEP, e, NSTEP)
                add_expert(e, NSTEP * (e + 2), e + 2, TOK, e)
            step(dve.tensor_copy(XN[:, :, :], TOK[:, :, :]))
            post(1)
            b, k = bank_of["sguT"]
            dve.wait_ge(sem(f"bank_read{b}"), k + 1)
            step(dve.memset(sguT[64:P, :, 0:64], 0.0))
            dve.wait_ge(sem("gelu_done"), 1)

            def memory_attention(units):
                def bias(h):
                    u = units + h
                    c = 2 * (u % 2)
                    dve.wait_ge(sem("mem_scored"), u + 1)
                    step(dve.reduce_max(sm[:, 44:46], banks[4 + h % 2][:, :].rearrange("p (t m) -> p t m", t=TT), axis=AX.X))
                    step(dve.tensor_scalar(sm[:, 48 + c:50 + c], sm[:, 44:46], -(P ** -0.5), None, ALU.mult), "mem_bias")

                bias(0)
                for h in range(XH):
                    u = units + h
                    c = 2 * (u % 2)
                    dve.wait_ge(sem("mem_exp"), 2 * u + 2)
                    step(dve.reciprocal(sm[:, 56:58], sm[:, 52 + c:54 + c]))
                    for t in range(TT):
                        m = dve.tensor_scalar(EM[:, h % 2, t, :], EM[:, h % 2, t, :], sm[:, 56 + t:57 + t], None, ALU.mult)
                    step(m, "mem_prob")
                    if h + 1 < XH:
                        bias(h + 1)

            memory_attention(0)
            dve.wait_ge(sem("params_in"), 16 * 8)
            V = UV[:, :, 1, :]
            step(layer_norm(V, V, RS[:, 0, 0:NCH], RS[:, 0, NCH:D], LN_EPS, NCH), "sgu_ready")
            for t in range(TT):
                o = take(f"sg{t}")
                for h in range(XH):
                    m = dve.scalar_tensor_tensor(TOK[:, t, h * P:(h + 1) * P], o[:, h * P:(h + 1) * P], PCOL[:, 1, 76 + h:77 + h],
                                                 UV[:, t, 0, h * P:(h + 1) * P], ALU.add, ALU.mult)
                free(m, f"sg{t}")
            step(dve.memset(junk, 0.0), "gated_tokens")

            def projected(name, rows):
                for n in range(2):
                    for t in range(TT):
                        o = take(f"wo{name}{n}{t}")
                        v = slice(n * NCH, (n + 1) * NCH)
                        free(dve.scalar_tensor_tensor(XN[:, t, v], X[:, t, v], ALPHA, o[:, :], ALU.mult, ALU.add), f"wo{name}{n}{t}")
                dve.wait_ge(sem("params_in"), 16 * rows)
                step(layer_norm(XN, X, RS[:, 1, :], RS[:, 2, :], LN_EPS, D), "x_updated")

            def group_router(name):
                b, k = bank_of[f"rt{name}"]
                dve.wait_ge(sem(f"bank_read{b}"), k + 1)
                sel = sm[:, 208:240].rearrange("p (t e) -> p t e", t=TT)
                m2 = sm[:, 240:272].rearrange("p (t e) -> p t e", t=TT)
                gs = sm[:, 272:280].rearrange("p (t g) -> p t g", t=TT)
                gr = sm[:, 280:288].rearrange("p (t g) -> p t g", t=TT)
                for t in range(TT):
                    m = dve.tensor_tensor(sel[:, t, :], gates[:, t, :], rbias[:, :], ALU.add)
                step(m)
                for t in range(TT):
                    ranks(m2[:, t, :].rearrange("p (g e) -> p g e", g=NG), sel[:, t, :], NG, GS, (rk[:, 0, 0:64], rk[:, 1, 0:64]))
                step(dve.tensor_scalar(sm[:, 240:272], sm[:, 240:272], 2.0, None, ALU.is_lt))
                step(dve.tensor_tensor(sel, sel, m2, ALU.mult))
                step(dve.tensor_reduce(sm[:, 272:280], sm[:, 208:240].rearrange("p (g e) -> p g e", e=GS), axis=AX.X, op=ALU.add))
                for t in range(TT):
                    ranks(gr[:, t, :], gs[:, t, :], 1, NG, (rk[:, 0, 0:16], rk[:, 1, 0:16]))
                step(dve.tensor_scalar(sm[:, 280:288], sm[:, 280:288], 1.0, None, ALU.is_lt))
                step(dve.tensor_tensor(sm[:, 240:272].rearrange("p (g e) -> p g e", e=GS), sm[:, 240:272].rearrange("p (g e) -> p g e", e=GS),
                                       sm[:, 280:288].rearrange("p (g a) -> p g a", a=1).broadcast_to([P, 2 * NG, GS]), ALU.mult))
                step(dve.tensor_tensor(gates[:, :, :], gates[:, :, :], m2, ALU.mult))
                step(dve.reduce_sum(sm[:, 62:64], gates[:, :, :], axis=AX.X))
                step(dve.reciprocal(sm[:, 62:64], sm[:, 62:64]))
                for t in range(TT):
                    m = dve.tensor_scalar(gates[:, t, :], gates[:, t, :], sm[:, 62 + t:63 + t], None, ALU.mult)
                step(m)

            for l, name in ((0, "A"), (1, "B")):
                projected(name, 8 if l == 0 else 11)
                group_router(name)
                step(dve.tensor_scalar(TOK[:, :, :], X[:, :, :], ALPHA, None, ALU.mult))
                h0 = NSTEP * (1 + NE1) + l * NE2 * NSTEP2
                y0 = 1 + NE1 + l * NE2
                with dve.Fori(0, NE2 // 2) as i:
                    for u in range(2):
                        hidden(NSTEP2, h0 + u * NSTEP2, i, 2 * NSTEP2)
                        add_expert(i * 2 + u, h0 + (u + 1) * NSTEP2 + i * (2 * NSTEP2), i * 2 + (y0 + u + 1), TOK, i * 2 + (NE1 + l * NE2 + u))
                dve.wait_ge(sem("params_in"), 16 * (11 if l == 0 else 13))
                step(layer_norm(TOK, X, RS[:, 3, :], RS[:, 0, :], LN_EPS, D), "x_updated")
                if l == 0:
                    dve.wait_ge(sem("margins"), 3)
                    dve.wait_ge(sem("conv_gates"), 1)
                    for j in range(2):
                        o = take(f"zb2{j}")
                        free(dve.tensor_tensor(hT2[:, 2 * j:2 * j + 2, 2:T + 2], cgT[:, 2 * j:2 * j + 2, :],
                                               o[:, :].rearrange("p (j t) -> p j t", j=2), ALU.mult), f"zb2{j}")
                    for k in range(4):
                        col = lambda tap: PCOL[:, 1, 64 + 4 * tap + k:65 + 4 * tap + k]
                        step(dve.tensor_scalar(cvB[:, 0, :], hT2[:, k, 0:T], col(0), None, ALU.mult))
                        for tap in (1, 2):
                            step(dve.scalar_tensor_tensor(cvB[:, 0, :], hT2[:, k, tap:tap + T], col(tap), cvB[:, 0, :], ALU.mult, ALU.add))
                        step(dve.tensor_tensor(T2[:, k, :], cvB[:, 0, :], bgT[:, k, :], ALU.mult))
                    memory_attention(XH)
                    dve.wait_ge(sem("mem_out"), 2 * XH)
                    dve.wait_ge(sem("cat_ready"), 1)
                    dve.memset(junk, 0.0).then_inc(sem("cat_ready"), 1)


def rope_table():
    width, axis = 64, 32
    rows = T // width
    r = np.repeat(np.arange(rows, dtype=np.float32), width)
    c = np.tile(np.arange(width, dtype=np.float32), rows)
    inv = (np.float32(10000.0) ** (-np.arange(0, axis, 2, dtype=np.float32) / np.float32(axis))).astype(np.float32)
    parts = []
    for f, sign in ((np.cos, 1), (np.sin, -1)):
        cols = []
        for pos in (r, c):
            a = f(pos[:, None] * inv).astype(np.float32)
            cols += [sign * a, a]
        parts.append(np.concatenate(cols, axis=1))
    return np.stack(parts, axis=1).astype(np.float32)


def kernel(**inputs):
    import concourse.bacc as _bacc
    from concourse.bass_utils import run_bass_kernel_spmd as _run

    nc = _bacc.Bacc("TRN2", target_bir_lowering=False, num_devices=1)
    arrays, args = {}, {}
    for name, a in inputs.items():
        arrays[f"in_{name}"] = np.ascontiguousarray(a)
    arrays["in_rope"] = rope_table()
    for name, a in arrays.items():
        args[name[3:]] = nc.dram_tensor(name, a.shape, mybir.dt.from_np(a.dtype), kind="ExternalInput").ap()
    out = nc.dram_tensor("out_0", (1, T, D), F32, kind="ExternalOutput").ap()
    two_blocks(nc, args, out)
    r = _run(nc, [arrays], core_ids=[0])
    return r.results[0]["out_0"]
```

```python
from contextlib import ExitStack

import numpy as np

import concourse.bass as bass
from concourse import mybir

P = 128
F32 = mybir.dt.float32
ALU = mybir.AluOpType
ACT = mybir.ActivationFunctionType
AX = mybir.AxisListType

D = 1024
KC = D // P
T = 256
TT = T // P
NCH = 512
HALF = NCH // 2
FF = 2816
FSTEP = 256
NSTEP = FF // FSTEP
NE1 = 8
NE2 = 16
NG = 4
GS = NE2 // NG
NSTEP2 = (D // 2) // FSTEP
MH, MD = 8, 64
DH, DQ, DV = 4, 64, 128
XH = 4
TAPS = 31
EPS = 1e-6
LN_EPS = 1e-5
LAM_INIT = 0.8 - 0.6
ALPHA = 4 ** 0.25
GR = 40
SL = P
RING = 4
NBANK = 4


class Moe:

    def __init__(self, name, bins, experts, halves, u0, f0):
        self.name, self.bins, self.experts, self.halves = name, bins, experts, halves
        self.steps = experts * halves
        self.u0, self.f0 = u0, f0


U_FFN = TT * NSTEP
MOE1 = Moe("1", NE1, 1, NSTEP, U_FFN, 0)
MOEA = Moe("A", NG, GS, NSTEP2, MOE1.u0 + MOE1.bins * MOE1.steps, NE1 + 1)
MOEB = Moe("B", NG, GS, NSTEP2, MOEA.u0 + MOEA.bins * MOEA.steps, NE1 + NG + 2)
MOES = (MOE1, MOEA, MOEB)


def plan_stream():
    names = [f"mod0_{c}" for c in range(4)]
    names += ["dq", "dk", "dv", "gates", "mk", "mq", "mv", "mo"]
    names += FILL + GAP1
    names += ["wo0", "wo1"] + GAP2
    g_at, d_at, pos, filled = {}, {}, 0, [0] * RING
    dfilled = [0] * RING
    loops = {}

    def put(name):
        nonlocal pos
        s = pos % RING
        g_at[name] = (s, filled[s])
        filled[s] += 1
        pos += 1

    def loop(name, count, steps):
        nonlocal pos
        pos += -pos % RING
        per = [len([s for s in range(steps) if s % RING == r]) for r in range(RING)]
        loops[name] = (list(filled), list(dfilled), per)
        for r in range(RING):
            filled[r] += per[r] * count
            dfilled[r] += per[r] * count

    for n in names:
        put(n)
    loop("ffn0", 1, NSTEP)
    for n in GAP3 + ["pa0", "pg0", "pa1", "pg1"] + LATE + MEMORY + GAP4 + ["pw2_0", "pw2_1"] + GAP5:
        put(n)
    loop("moe1", NE1 // 2, 2 * NSTEP)
    for n in ["za0", "za1", "za2", "woA0", "woA1"]:
        put(n)
    loop("moeA", NG // 2, 2 * MOEA.steps)
    for n in ["zb0", "zb1", "zb2", "zb3", "woB0", "woB1"]:
        put(n)
    loop("moeB", NG // 2, 2 * MOEB.steps)
    return g_at, loops


FILL = ["mod0_6", "mod0_7", "mod0_8", "mod0_9", "mod1_3"]
GAP1 = ["mod0_4", "mod0_5", "mod0_10"]
GAP2 = ["mod0_11", "mod1_0"]
GAP3 = ["mod1_1", "mod1_2"]
LATE = ["mod1_4", "mod1_5", "mod1_6", "mod1_7"]
MEMORY = ["kv0_0", "kv0_1", "kv1_0", "kv1_1"]
GAP4 = ["mod1_8", "mod1_9"]
GAP5 = ["mod1_10", "mod1_11"]
NFILL = len(FILL)
SLOTS = 2 * DH + MH


def fills_at(i):
    return FILL[NFILL * i // SLOTS:NFILL * (i + 1) // SLOTS]


def plan_banks():
    names = [f"mod0_{c}" for c in range(4)] + ["mod0T"]
    names += ["dq0", "dq1", "dk0", "dk1", "dkc0", "dkc1", "dv0", "dv1", "dvc0", "dvc1", "ig", "fg"]
    names += ["mk0", "mk1", "mkc0", "mkc1", "mq0", "mq1"]
    names += ["mv0", "mv1", "mvc0", "mvc1", "mo0", "mo1", "dqT0", "dqT1", "dkT0", "dkT1", "gT"]
    names += FILL + GAP1
    names += [f"wo{n}{t}" for n in range(2) for t in range(TT)] + GAP2 + GAP3
    names += [f"{w}{c}{j}" for c in range(2) for w in ("pa", "pg") for j in range(2)]
    names += LATE
    names += [f"kv{l}{w}{j}" for l in range(2) for w in "kv" for j in range(2)]
    names += GAP4 + [f"pw2{n}{t}" for n in range(2) for t in range(TT)]
    names += GAP5 + ["rt1", "pos1"]
    names += [f"za{n}{j}" for n in range(3) for j in range(2)] + ["sguT"]
    names += [f"sg{t}" for t in range(TT)] + ["tokT0", "tokT1"]
    names += [f"woA{n}{t}" for n in range(2) for t in range(TT)] + ["rtA", "posA"]
    names += [f"zb{n}{j}" for n in range(4) for j in range(2)]
    names += [f"woB{n}{t}" for n in range(2) for t in range(TT)] + ["rtB", "posB"]
    return {n: (i % NBANK, i // NBANK) for i, n in enumerate(names)}


def two_blocks(nc, A, out):
    g_at, loops = plan_stream()
    bank_of = plan_banks()

    with ExitStack() as ctx:
        def sb(name, shape, dt=F32):
            return ctx.enter_context(nc.sbuf_tensor(name, shape, dt))

        sems = {}

        def sem(name):
            if name not in sems:
                sems[name] = ctx.enter_context(nc.semaphore(name))
            return sems[name]

        ring = sb("ring", [P, RING, KC, NCH])
        dreg = sb("dreg", [P, RING * 2 * D])
        arena = sb("arena", [P, 5664])
        X = sb("X", [P, TT, D])
        XN = sb("XN", [P, TT, D])
        TOK = sb("TOK", [P, TT, D])
        T1 = sb("T1", [P, KC, T])
        T2 = sb("T2", [P, KC, T])
        GP = sb("GP", [P, 2, D])
        RB = sb("RB", [P, 2, NCH])
        RS = sb("RS", [P, 4, D])
        CB = sb("CB", [P, KC, P])
        ident = sb("ident", [P, P])
        pack = T2[:, :, :].rearrange("p k t -> p (k t)")[:, 0:4 * P].rearrange("p (a n) -> p a n", a=4)
        PCOL = sb("PCOL", [P, 4, P])
        CT = sb("CT", [P, KC, 2])
        MODX = sb("MODX", [P, 2, 48])
        MODC = sb("MODC", [P, 16])
        SCL = sb("SCL", [P, 5, KC])
        mskf = sb("mskf", [P, 3, P])
        mskb = sb("mskb", [P, 3, P])
        sm = sb("sm", [P, 512])
        gbias = sb("gbias", [GR, 2])
        wrt = sb("wrt", [P, KC, NE1 + NE2])
        rbias = sb("rbias", [P, NE2])
        tri8 = sb("tri8", [P, NE1, NE1])
        gates = sb("gates", [P, TT, NE2 + GS])
        chosen = sb("chosen", [P, TT, NE1])
        place = sb("place", [P, TT, NE1 + 1])
        bplace = sb("bplace", [P, TT])
        bgates = sb("bgates", [P, TT, GS])
        sgates = sb("sgates", [P, 2, GS])
        flag = sb("flag", [P, 4], mybir.dt.int32)
        SG = sb("SG", [P, 2, FSTEP])
        H = sb("H", [P, 2, FSTEP])
        HT = sb("HT", [P, 2, 2, P])

        def carve(region, at, *shape):
            n = int(np.prod(shape))
            v = region[:, at:at + n]
            if len(shape) == 1:
                return v
            names = "abcd"[:len(shape)]
            spec = " ".join(names)
            return v.rearrange(f"p ({spec}) -> p {spec}", **{names[i]: shape[i] for i in range(len(shape))})

        dring = carve(dreg, 0, RING, 2, D)
        mod_rows = T1[0:2, :, :].rearrange("p k t -> p (k t)")
        kT = carve(dreg, 0, 4, 2 * T)
        qT = carve(dreg, 2048, 4, T)
        kdT = carve(dreg, 3072, 4, 2 * T)
        qdT = carve(dreg, 5120, 4, T)
        vd = carve(dreg, 6144, 4, NCH)
        vaug = carve(arena, 0, 4, MH, MD + 1)
        osig = carve(arena, 2080, TT, NCH)
        WDs = (carve(arena, 3104, 2, 896), carve(T1[:, :, :].rearrange("p k t -> p (k t)"), 0, 2, 896))
        AR = carve(arena, 4896, 2, 384)
        EX = carve(arena, 3104, 2, 2, NCH)
        RSf = RS[:, :, :].rearrange("p a n -> p (a n)")
        CV = carve(RSf, 1024, 2, NCH)
        PR = carve(RSf, 2048, 2, NCH)
        PT = carve(RSf, 3072, 2, NCH)
        HR = carve(RSf, 1024, MH, 4, MD + 1)
        T2f = T2[:, :, :].rearrange("p k t -> p (k t)")
        SEL = carve(T2f, 0, 2 * MH, P)
        XNf = XN[:, :, :].rearrange("p t n -> p (t n)")
        gi = arena[0:GR, 3104:3104 + 512]
        gf = arena[0:GR, 3616:3616 + 512]
        gt_ = arena[0:GR, 4128:4128 + 512]
        gB = arena[0:GR, 4640:4640 + 512]
        GCt = sb("GCt", [P, 6, GR])
        onesr = SG[0:GR, :, :].rearrange("p a n -> p (a n)")
        gG = H[0:GR, :, :].rearrange("p a n -> p (a n)")
        nM = HT[0:GR, 0, :, :].rearrange("p a n -> p (a n)")
        gE = HT[0:GR, 1, :, :].rearrange("p a n -> p (a n)")
        WG = carve(RSf, 3104, KC, 2, GR)
        rope = carve(RSf, 2048, TT, 2, 64)
        lamv = carve(RSf, 2304, 4, DQ)
        rk = carve(arena, 4096, 2, P)
        RB2 = carve(arena, 4352, 2, NCH)
        hT = carve(dreg, 0, KC, T + TAPS - 1)
        SGC = carve(dreg, 2304, 2, NCH)
        XG = T1[:, :, :].rearrange("p k t -> p (k t)").rearrange("p (b k n) -> p b k n", b=2, k=KC)
        YS = carve(T2f, 0, D)
        PM = carve(T2f, D, 2, TT * SL)
        PTM = carve(T2f, D + 2 * TT * SL, 2, TT * P)
        CBf = CB[:, :, :].rearrange("p k n -> p (k n)")
        upper = CBf[:, 0:P]
        ones = CBf[:, P:2 * P]
        slots = carve(CBf, 2 * P, 2, SL)
        memT = T1
        kmT = carve(arena, 0, 2, XH, T)
        vm = carve(arena, 2048, 2, 2, NCH)
        UV = carve(dreg, 0, TT, 2, NCH)
        xqT = carve(dreg, 2048, XH, T)
        EM = carve(dreg, 3072, 2, TT, T)
        PMT = carve(dreg, 4096, 2, 2, T)
        sguw = carve(dreg, 5120, XH, P)
        sguT = carve(dreg, 5632, XH, P)
        cgT = carve(dreg, 0, 4, T)
        bgT = carve(dreg, 1024, 4, T)
        hT2 = carve(dreg, 6144, 4, T + 2)
        cvB = carve(dreg, 7176, 2, T)

        banks = [ctx.enter_context(nc.psum_tensor(f"bank{i}", [P, NCH], F32)) for i in range(8)]
        block = ctx.enter_context(nc.Block())

        def chunk(w, c, n=NCH):
            return w.rearrange("(k p) n -> p k n", p=P)[:, :, c:c + n]

        win = A["l0_w_in"]
        wsrc = {}
        for l in range(2):
            for c in range(12):
                wsrc[f"mod{l}_{c}"] = chunk(A[f"l{l}_mod_w"], c * NCH)
        for i, n in enumerate(["mq", "mk", "mv", "mo"]):
            wsrc[n] = chunk(win, i * NCH)
        wsrc["gates"] = chunk(win, 2048, 32)
        for i, n in enumerate(["dq", "dk", "dv"]):
            wsrc[n] = chunk(win, 2080 + i * NCH)
        for c in range(2):
            wsrc[f"wo{c}"] = chunk(A["l0_w_out"], c * NCH)
            wsrc[f"pa{c}"] = chunk(A["l1_conv_pw1_w"], c * NCH)
            wsrc[f"pg{c}"] = chunk(A["l1_conv_pw1_w"], D + c * NCH)
            wsrc[f"pw2_{c}"] = chunk(A["l1_conv_pw2_w"], c * NCH)
            for l in range(2):
                wsrc[f"kv{l}_{c}"] = chunk(A["w_kv_2"][l], c * NCH)
            wsrc[f"woA{c}"] = chunk(A["w_out_2"][0], c * NCH)
            wsrc[f"woB{c}"] = chunk(A["w_out_2"][1], c * NCH)
        for c in range(3):
            wsrc[f"za{c}"] = chunk(A["w_in_a_2"][0], c * NCH)
        for c in range(4):
            wsrc[f"zb{c}"] = chunk(A["w_in_b_2"][0], c * NCH)

        last_output = {f: f for f in wsrc if f.startswith("mod")}
        last_output.update(dq="dq1", dk="dkc1", dv="dvc1", gates="fg", mk="mkc1", mq="mq1", mv="mvc1", mo="mo1")
        for c in range(2):
            last_output.update({f"wo{c}": f"wo{c}1", f"pa{c}": f"pa{c}1", f"pg{c}": f"pg{c}1", f"pw2_{c}": f"pw2{c}1",
                                f"woA{c}": f"woA{c}1", f"woB{c}": f"woB{c}1", f"kv{c}_0": f"kv{c}k1", f"kv{c}_1": f"kv{c}v1"})
        last_output.update({f"za{c}": f"za{c}1" for c in range(3)})
        last_output.update({f"zb{c}": f"zb{c}1" for c in range(4)})

        def row(v, n):
            return v.rearrange("(a n) -> a n", a=1).broadcast_to([P, n])

        def wait_output(eng, name):
            b, n = bank_of[name]
            eng.wait_ge(sem(f"bank_ready{b}"), n + 1)

        def spilled(eng, m):
            eng.wait_ge(sem("flag_ready"), 1 + MOES.index(m))
            return eng.value_load(flag[0:1, MOES.index(m):MOES.index(m) + 1], min_val=0, max_val=1)

        def unrolled(m):
            return 1 if m is MOE1 else m.halves

        def baton_bin(m):
            return 4 + 7 * m.steps + 2

        def baton_at(m, b, c, h):
            return b * baton_bin(m) + c * (7 * unrolled(m)) + (5 + 7 * h)

        def second_pass(eng, m, first, steps, tail, end=False):
            def run(phases, base, *a):
                for j, fn in phases:
                    eng.wait_ge(sem(f"baton{m.name}"), base + j)
                    fn(*a).then_inc(sem(f"baton{m.name}"), 1)
            with eng.If(spilled(eng, m) > 0):
                with eng.Fori(0, m.bins) as b:
                    run(first, b * baton_bin(m) + 1, b)
                    with eng.Fori(0, m.steps // unrolled(m)) as c:
                        for h in range(unrolled(m)):
                            run(steps, baton_at(m, b, c, h), b, c, h)
                    run(tail, b * baton_bin(m) + (5 + 7 * m.steps), b)
                if end:
                    eng.wait_ge(sem(f"baton{m.name}"), 1 + m.bins * baton_bin(m))

        @block.sync
        def _(sp):
            row0 = 0
            for v, n in (("l0_mod_b", 48), ("l0_mix_pre_g", 8), ("l0_ffn_pre_g", 8),
                         ("l1_mod_b", 48), ("l1_mix_pre_g", 8), ("l1_ffn_pre_g", 8)):
                sp.dma_start(pack[row0:row0 + n, 0, :], A[v].rearrange("(r n) -> r n", n=P)).then_inc(sem("packed"), 16)
                row0 += n
            row0 = 0
            for v, n in ((A["c"][0], 8), (A["c_ctx"], 8), (A["l0_mlstm_conv_w"].rearrange("a n -> (a n)"), 24),
                         (A["l1_conv_dw_b"], 8), (A["l1_conv_pw1_b"], 16),
                         (A["conv_w_2"][0].rearrange("a n -> (a n)"), 12),
                         (A["sgu_b_2"][0].rearrange("a n -> (a n)"), 4)):
                sp.dma_start(pack[row0:row0 + n, 1, :], v.rearrange("(r n) -> r n", n=P)).then_inc(sem("packed"), 16)
                row0 += n
            dw = A["l1_conv_dw_w"].rearrange("a (r n) -> (a r) n", n=P)
            sp.dma_start(pack[:, 2, :], dw[0:P, :]).then_inc(sem("packed"), 16)
            sp.dma_start(pack[0:TAPS * KC - P, 3, :], dw[P:TAPS * KC, :]).then_inc(sem("packed"), 16)

            holder = [None] * RING

            def slot_free(s):
                h = holder[s]
                if isinstance(h, str):
                    wait_output(sp, last_output[h])
                elif h is not None:
                    sp.wait_ge(sem("upped"), h)

            def load(name):
                s, n = g_at[name]
                slot_free(s)
                w = 32 if name == "gates" else NCH
                sp.dma_start(ring[:, s, :, 0:w], wsrc[name]).then_inc(sem(f"chunk_in{s}"), 16)
                holder[s] = name

            def experts(count, steps, w1, w3, w2, u0, per_step=1):
                n = len(steps)
                before = list(holder)

                def body(it):
                    for q, (e, st) in enumerate(steps):
                        s = q % RING
                        f = slice(st * FSTEP, (st + 1) * FSTEP)
                        if q < RING and isinstance(before[s], str):
                            wait_output(sp, last_output[before[s]])
                        prev = q - RING if q >= RING else max(p for p in range(n) if p % RING == s) - n
                        done = u0 + per_step * (prev + 1) + it * (per_step * n)
                        if not (isinstance(done, int) and done <= 0):
                            sp.wait_ge(sem("upped"), done)
                        for i, w in enumerate((w1, w3)):
                            sp.dma_start(ring[:, s, :, i * FSTEP:(i + 1) * FSTEP],
                                         w(it, e).rearrange("(k p) n -> p k n", p=P)[:, :, f]).then_inc(sem(f"pair_in{s}"), 16)
                        if not (isinstance(done, int) and done <= 0):
                            sp.wait_ge(sem("down_done"), done)
                        sp.dma_start(dring[:, s, :, :], w2(it, e)[f, :].rearrange("(j p) n -> p j n", p=P)).then_inc(
                            sem(f"down_in{s}"), 16)
                if count == 1:
                    body(0)
                else:
                    with sp.Fori(0, count) as it:
                        body(it)
                for s in range(RING):
                    holder[s] = u0 + per_step * (n * (count - 1) + max(p for p in range(n) if p % RING == s) + 1)

            def second_loads(m, w1, w3, w2):
                with sp.If(spilled(sp, m) > 0):
                    with sp.Fori(0, m.bins) as b:
                        with sp.Fori(0, m.steps // unrolled(m)) as c:
                            for h in range(unrolled(m)):
                                f = bass.ds(c * FSTEP, FSTEP) if m is MOE1 else slice(h * FSTEP, (h + 1) * FSTEP)
                                sp.wait_ge(sem(f"baton{m.name}"), baton_at(m, b, c, h))
                                for i, w in enumerate((w1, w3)):
                                    sp.dma_start(ring[:, 0, :, i * FSTEP:(i + 1) * FSTEP],
                                                 w(b, c).rearrange("(k p) n -> p k n", p=P)[:, :, f]).then_inc(
                                        sem(f"second_in{m.name}"), 16)
                                sp.dma_start(dring[:, 0, :, :], w2(b, c)[f, :].rearrange("(j p) n -> p j n", p=P)).then_inc(
                                    sem(f"second_in{m.name}"), 16)
                    sp.wait_ge(sem(f"baton{m.name}"), 1 + m.bins * baton_bin(m))

            load("mod0_0")
            sp.dma_start(X[:, :, :], A["x"][0].rearrange("(t p) d -> p t d", p=P)).then_inc(sem("x_loaded"), 16)
            load("mod0_1")
            sp.dma_start(TOK[:, :, :], A["ctx"][0].rearrange("(t p) d -> p t d", p=P)).then_inc(sem("ctx_loaded"), 16)
            for n in ["mod0_2", "mod0_3", "dq", "dk", "dv", "gates", "mk", "mq", "mv", "mo"] + FILL + GAP1 + ["wo0", "wo1"] + GAP2:
                load(n)
            sp.wait_ge(sem("x_updated"), 1)
            one = [(0, st) for st in range(NSTEP)]
            experts(1, one, lambda it, e: A["l0_ffn_w1"], lambda it, e: A["l0_ffn_w3"], lambda it, e: A["l0_ffn_w2"], 0, TT)
            for n in GAP3 + ["pa0", "pg0", "pa1", "pg1"] + LATE + MEMORY + GAP4 + ["pw2_0", "pw2_1"] + GAP5:
                load(n)
            sp.wait_ge(sem("x_updated"), 3)
            two = [(e, st) for e in range(2) for st in range(NSTEP)]
            experts(NE1 // 2, two, lambda it, e: A["l1_moe_w1"][it * 2 + e], lambda it, e: A["l1_moe_w3"][it * 2 + e],
                    lambda it, e: A["l1_moe_w2"][it * 2 + e], MOE1.u0)
            second_loads(MOE1, lambda b, c: A["l1_moe_w1"][b], lambda b, c: A["l1_moe_w3"][b], lambda b, c: A["l1_moe_w2"][b])
            for n in ["za0", "za1", "za2", "woA0", "woA1"]:
                load(n)
            eight = [(e, st) for e in range(2 * GS) for st in range(NSTEP2)]
            for l, m in ((0, MOEA), (1, MOEB)):
                sp.wait_ge(sem("x_updated"), 5 + 2 * l)
                experts(NG // 2, eight, lambda it, e: A["w_gate_2"][l, it * (2 * GS) + e],
                        lambda it, e: A["w_up_2"][l, it * (2 * GS) + e],
                        lambda it, e: A["w_down_2"][l, it * (2 * GS) + e], m.u0)
                second_loads(m, lambda b, c: A["w_gate_2"][l, b * GS + c], lambda b, c: A["w_up_2"][l, b * GS + c],
                             lambda b, c: A["w_down_2"][l, b * GS + c])
                if l == 0:
                    for n in ["zb0", "zb1", "zb2", "zb3", "woB0", "woB1"]:
                        load(n)
            sp.wait_ge(sem("x_updated"), 8)
            sp.dma_start(out[0].rearrange("(t p) d -> p t d", p=P), X[:, :, :]).then_inc(sem("stored"), 16)
            sp.wait_ge(sem("stored"), 16)

        @block.gpsimd
        def _(pool):
            cnt = {}

            def step(ins, name="pool_step"):
                cnt[name] = cnt.get(name, 0) + 1
                ins.then_inc(sem(name), 1)
                pool.wait_ge(sem(name), cnt[name])

            step(pool.memset(ident[:, :], 0.0))
            step(pool.affine_select(out=ident[:, :], in_=ident[:, :], compare_op=ALU.not_equal, fill=1.0, base=0,
                                    pattern=[[-1, P]], channel_multiplier=1), "ident_made")
            step(pool.memset(gbias[:, :], 0.0))
            for d in range(2):
                for w in range(2):
                    pool.dma_start(gbias[32 * d:32 * d + 8, w:w + 1],
                                   A["l0_mlstm_gate_b"][16 * d + 8 * w:16 * d + 8 * w + 8].rearrange("(n a) -> n a", a=1)
                                   ).then_inc(sem("consts_in"), 16)
            for i, n in enumerate(("l0_lambda_q1", "l0_lambda_k1", "l0_lambda_q2", "l0_lambda_k2")):
                pool.dma_start(lamv[:, i, :], row(A[n], DQ)).then_inc(sem("consts_in"), 16)
            pool.dma_start(rope[:, :, :, :], A["rope"].rearrange("(t p) a n -> p t a n", p=P)).then_inc(sem("consts_in"), 16)
            pool.dma_start(wrt[:, :, 0:NE1], A["l1_router_w"].rearrange("(k p) n -> p k n", p=P)).then_inc(sem("consts_in"), 16)
            pool.dma_start(wrt[:, :, NE1:], A["router_w_2"].rearrange("(k p) n -> p k n", p=P)).then_inc(sem("consts_in"), 16)
            pool.dma_start(rbias[:, :], row(A["router_b_2"], NE2)).then_inc(sem("consts_in"), 16)
            pool.dma_start(RS[:, 0, 0:NCH], row(A["l0_mlstm_norm_g"], NCH)).then_inc(sem("consts_in"), 16)
            pool.dma_start(RS[:, 0, NCH:D], row(A["l0_diff_norm_g"], NCH)).then_inc(sem("consts_in"), 16)
            step(pool.memset(onesr, 1.0))
            step(pool.memset(WG[:, :, :, :], 0.0), "gate_pad")
            step(pool.memset(mskf[:, :, :], 0.0))
            step(pool.memset(mskb[:, :, :], 0.0))
            step(pool.affine_select(out=mskf[:, 1:3, :], in_=mskf[:, 1:3, :], compare_op=ALU.is_ge, fill=-1e30, base=0,
                                    pattern=[[0, 2], [1, P]], channel_multiplier=-1))
            step(pool.affine_select(out=mskb[:, 0:2, :], in_=mskb[:, 0:2, :], compare_op=ALU.is_ge, fill=-1e30, base=0,
                                    pattern=[[0, 2], [-1, P]], channel_multiplier=1))
            step(pool.memset(tri8[:, :, :], 1.0))
            step(pool.affine_select(out=tri8[:, :, :], in_=tri8[:, :, :], compare_op=ALU.is_ge, fill=0.0, base=-1,
                                    pattern=[[1, NE1], [-1, NE1]], channel_multiplier=0))
            step(pool.memset(vaug[:, :, :, MD:MD + 1], 1.0))
            step(pool.memset(WG[:, 0:1, 0, 39:40], 0.0), "masks_made")
            gated = [0]

            def gate_rows(names):
                for f in names:
                    l, c = int(f[3]), int(f[5:])
                    if c not in (4, 5, 10, 11):
                        continue
                    if gated[0]:
                        pool.wait_ge(sem("rows_used"), gated[0])
                    h = c % 2
                    post = A[f"l{l}_mix_post_g"] if c < 6 else A[f"l{l}_ffn_post_g"]
                    pool.dma_start(RB[:, 0, :], row(A[f"l{l}_mod_b"][c * NCH:(c + 1) * NCH], NCH)).then_inc(sem("rows_in"), 16)
                    pool.dma_start(RB[:, 1, :], row(post[h * NCH:(h + 1) * NCH], NCH)).then_inc(sem("rows_in"), 16)
                    gated[0] += 1

            gate_rows(GAP1 + GAP2)

            def rows_after(v, loads):
                pool.wait_ge(sem("x_updated"), v)
                for s, lo, a, n in loads:
                    pool.dma_start(RS[:, s, lo:lo + n], row(a, n)).then_inc(sem("params_in"), 16)

            pool.wait_ge(sem("x_updated"), 1)
            pool.dma_start(TOK[:, :, :], A["mem_2"][0].rearrange("(t p) d -> p t d", p=P)).then_inc(sem("mem_loaded"), 16)
            rows_after(1, [(1, 0, A["l1_conv_ln_g"], D), (2, 0, A["l1_conv_ln_b"], D), (3, 0, A["l1_conv_pw2_b"], D),
                           (0, 0, A["sgu_ln_g_2"][0], NCH), (0, NCH, A["sgu_ln_b_2"][0], NCH)])
            pool.wait_ge(sem("x_updated"), 2)
            step(pool.memset(hT[:, :, 0:TAPS // 2], 0.0), "margins")
            step(pool.memset(hT[:, :, T + TAPS // 2:], 0.0), "margins")
            gate_rows(LATE + GAP5[:1])
            last = int(GAP5[1][5:])
            pool.dma_start(RB2[:, 0, :], row(A["l1_mod_b"][last * NCH:(last + 1) * NCH], NCH)).then_inc(sem("last_rows_in"), 16)
            pool.dma_start(RB2[:, 1, :], row(A["l1_ffn_post_g"][last % 2 * NCH:(last % 2 + 1) * NCH], NCH)).then_inc(
                sem("last_rows_in"), 16)
            k = KC - 1
            acc = T2[:, k, :]
            pool.wait_ge(sem("glu"), 4)
            pool.wait_ge(sem("operand_ready"), 5)
            for tap in range(TAPS):
                r = tap * KC + k
                w = PCOL[:, 2 + r // P, r % P:r % P + 1]
                if tap == 0:
                    step(pool.tensor_scalar(acc, hT[:, k, 0:T], w, PCOL[:, 1, 40 + k:41 + k], ALU.mult, ALU.add))
                else:
                    term = H[:, tap % 2, :]
                    step(pool.tensor_scalar(term, hT[:, k, tap:tap + T], w, None, ALU.mult))
                    step(pool.tensor_tensor(acc, acc, term, ALU.add))
            step(pool.memset(gbias[:, :], 0.0), "chunk_convolved")
            wait_output(pool, GAP5[-1])
            step(pool.memset(CBf[:, 0:2 * P], 1.0))
            step(pool.affine_select(out=upper, in_=upper, compare_op=ALU.is_ge, fill=0.0, base=-1,
                                    pattern=[[1, P]], channel_multiplier=-1))
            step(pool.iota(slots, pattern=[[SL, 2], [1, SL]], base=0, channel_multiplier=0,
                           allow_small_or_imprecise_dtypes=True), "slots_made")
            rows_after(3, [(1, 0, A["ln1_g_2"][0], D), (2, 0, A["ln1_b_2"][0], D), (3, 0, A["ln2_g_2"][0], D)])
            pool.wait_ge(sem("x_updated"), 4)
            pool.dma_start(sguw, A["sgu_w_2"][0].rearrange("h i j -> i h j")).then_inc(sem("sgu_in"), 16)
            rows_after(5, [(0, 0, A["ln2_b_2"][0], D), (1, 0, A["ln1_g_2"][1], D), (2, 0, A["ln1_b_2"][1], D)])
            pool.wait_ge(sem("x_updated"), 6)
            step(pool.memset(hT2[:, :, 0:2], 0.0), "margins")
            rows_after(6, [(3, 0, A["ln2_g_2"][1], D), (0, 0, A["ln2_b_2"][1], D)])

        @block.tensor
        def _(pe):
            def bank_for(name):
                b, n = bank_of[name]
                if n:
                    pe.wait_ge(sem(f"bank_read{b}"), n)
                return banks[b]

            def filled(ins, name):
                ins.then_inc(sem(f"bank_ready{bank_of[name][0]}"), 1)

            seen = [0] * RING

            def chunk_in(name):
                s, _ = g_at[name]
                seen[s] += 1
                pe.wait_ge(sem(f"chunk_in{s}"), 16 * seen[s])
                return ring[:, s, :, :]

            turn = [0]

            def operand_chunk(k, fresh):
                if fresh and k % 2 == 0:
                    pe.wait_ge(sem("turned_read"), 4 * (turn[0] - 1) + k // 2 + 1)

            def tok_unit(name, src, t, w, n=NCH, lo=0, fresh=False):
                o = bank_for(name)
                for k in range(KC):
                    operand_chunk(k, fresh)
                    m = pe.matmul(o[:, lo:lo + n], src[:, k, t * P:(t + 1) * P], w[:, k, 0:n], start=k == 0, stop=k == KC - 1)
                filled(m, name)
                return m

            def feat_unit(name, src, j, w, fresh=False):
                o = bank_for(name)
                for i in range(2):
                    for k in range(KC):
                        operand_chunk(k, fresh and i == 0)
                        m = pe.matmul(o[:, i * T:(i + 1) * T], w[:, k, (2 * j + i) * P:(2 * j + i + 1) * P], src[:, k, :],
                                      start=k == 0, stop=k == KC - 1)
                filled(m, name)
                return m

            def mod_job(name):
                w = chunk_in(name)
                o = bank_for(name)
                for k in range(KC):
                    m = pe.matmul(o[:, :], CB[:, k, :], w[:, k, :], start=k == 0, stop=k == KC - 1)
                filled(m, name)

            def first_mod_job(c):
                w = chunk_in(f"mod0_{c}")
                o = bank_for(f"mod0_{c}")
                for k in range(KC):
                    m = pe.matmul(o[0:2, :], CT[:, k, :], w[:, k, :], start=k == 0, stop=k == KC - 1)
                filled(m, f"mod0_{c}")

            def first_mod_turn(c):
                pe.wait_ge(sem(f"bank_read{bank_of[f'mod0_{c}'][0]}"), 1)
                for j in range(4):
                    m = pe.transpose(bank_for("mod0T")[:, 2 * (4 * c + j):2 * (4 * c + j) + 2],
                                     mod_rows[:, c * NCH + j * P:c * NCH + (j + 1) * P], ident[0:2, 0:2])
                return m

            def turn_job(src, back=False):
                for b in range(4):
                    if turn[0]:
                        pe.wait_ge(sem("turned_read"), 4 * (turn[0] - 1) + b + 1)
                    for i in range(4):
                        if back:
                            if b % 2 == 0 and i == 0:
                                pe.wait_ge(sem("convolved"), b // 2 + 1)
                                if b:
                                    pe.wait_ge(sem("chunk_convolved"), 1)
                            t, k = b % 2, 4 * (b // 2) + i
                            m = pe.transpose(banks[4 + b][:, i * P:(i + 1) * P], src[:, k, t * P:(t + 1) * P], ident[:, :])
                        else:
                            k, t = 2 * b + i // 2, i % 2
                            m = pe.transpose(banks[4 + b][:, i * P:(i + 1) * P], src[:, t, k * P:(k + 1) * P], ident[:, :])
                    m.then_inc(sem("turned"), 1)
                turn[0] += 1

            def wait_operand(n):
                pe.wait_ge(sem("operand_ready"), n)

            pe.wait_ge(sem("ident_made"), 1)
            pe.wait_ge(sem("packed"), 16 * 15)
            for i, n in enumerate((P, 80, P, TAPS * KC - P)):
                m = pe.transpose(banks[7][:, i * P:i * P + n], pack[0:n, i, :], ident[0:n, 0:n])
            m.then_inc(sem("cols_turned"), 1)
            pe.wait_ge(sem("silu_c"), 1)
            for c in range(3):
                first_mod_job(c)
            pe.wait_ge(sem("cols_read"), 1)
            pe.wait_ge(sem("normed"), 1)
            turn_job(XN)
            first_mod_job(3)
            for c in range(4):
                m = first_mod_turn(c)
            filled(m, "mod0T")
            pe.wait_ge(sem("normed"), 2)
            turn_job(TOK)
            wait_operand(1)
            w = chunk_in("dq")
            for t in range(TT):
                tok_unit(f"dq{t}", T1, t, w)
            w = chunk_in("dk")
            for t in range(TT):
                tok_unit(f"dk{t}", T1, t, w)
            for j in range(2):
                feat_unit(f"dkc{j}", T2, j, w, fresh=j == 0)
            w = chunk_in("dv")
            for t in range(TT):
                tok_unit(f"dv{t}", T1, t, w)
            for t in range(TT):
                tok_unit(f"dvc{t}", T2, t, w)
            chunk_in("gates")
            pe.wait_ge(sem("gate_weights"), 1)
            for i, name in enumerate(("ig", "fg")):
                o = bank_for(name)
                for j, src in enumerate((T2, T1)):
                    for k in range(KC):
                        m = pe.matmul(o[0:GR, j * T:(j + 1) * T], WG[:, k, i, :], src[:, k, :], start=k == 0, stop=k == KC - 1)
                filled(m, name)
            w = chunk_in("mk")
            for j in range(2):
                feat_unit(f"mk{j}", T1, j, w)
            for j in range(2):
                feat_unit(f"mkc{j}", T2, j, w)
            w = chunk_in("mq")
            for j in range(2):
                feat_unit(f"mq{j}", T1, j, w)
            w = chunk_in("mv")
            for t in range(TT):
                tok_unit(f"mv{t}", T1, t, w)
            for t in range(TT):
                tok_unit(f"mvc{t}", T2, t, w)
            w = chunk_in("mo")
            for t in range(TT):
                m = tok_unit(f"mo{t}", T1, t, w)
            for i, n in enumerate("qk"):
                pe.wait_ge(sem("rotated"), i + 1)
                for b in range(2):
                    o = bank_for(f"d{n}T{b}")
                    for j in range(2):
                        for t in range(TT):
                            c = 2 * b + j
                            m = pe.transpose(o[:, j * T + t * P:j * T + (t + 1) * P],
                                             XN[:, t, i * NCH + c * P:i * NCH + (c + 1) * P], ident[:, :])
                    filled(m, f"d{n}T{b}")
            pe.wait_ge(sem("gate_rows"), 1)
            o = bank_for("gT")
            for s in range(4):
                pe.transpose(o[:, s * GR:(s + 1) * GR], gG[:, s * P:(s + 1) * P], ident[0:GR, 0:GR])
            for t in range(TT):
                m = pe.transpose(o[:, (4 + t) * GR:(5 + t) * GR], gE[:, t * P:(t + 1) * P], ident[0:GR, 0:GR])
            filled(m, "gT")

            pe.wait_ge(sem("diff_operands"), 1)

            def diff_scores(u):
                h, t = divmod(u, TT)
                if u:
                    pe.wait_ge(sem("diff_exp"), 2 * u)
                for i in range(2):
                    r = slice(i * DQ, (i + 1) * DQ)
                    pe.matmul(banks[4 + i][:, :], qdT[r, h, t * P:(t + 1) * P], kdT[r, h, :], start=True, stop=True
                              ).then_inc(sem("diff_scored"), 1)

            def diff_turn(u):
                pe.wait_ge(sem("diff_prob"), u + 1)
                if u:
                    pe.wait_ge(sem("diff_prob_turned"), u)
                for s in range(4):
                    m = pe.transpose(banks[6][:, s * P:(s + 1) * P], PR[:, u % 2, s * P:(s + 1) * P], ident[:, :])
                m.then_inc(sem("diff_turned"), 1)

            def diff_values(u):
                h, t = divmod(u, TT)
                pe.wait_ge(sem("diff_prob_turned"), u + 1)
                if u:
                    pe.wait_ge(sem("diff_out"), u)
                for s in range(4):
                    m = pe.matmul(banks[7][:, 0:DV], PT[:, u % 2, s * P:(s + 1) * P], vd[:, s, h * DV:(h + 1) * DV],
                                  start=s == 0, stop=s == 3)
                m.then_inc(sem("diff_summed"), 1)

            diff_scores(0)
            for u in range(2 * DH):
                if u + 1 < 2 * DH:
                    diff_scores(u + 1)
                if u:
                    diff_values(u - 1)
                diff_turn(u)
                for f in fills_at(u):
                    mod_job(f)
            diff_values(2 * DH - 1)

            pe.wait_ge(sem("mlstm_operands"), 1)
            pe.wait_ge(sem("diff_out"), 2 * DH)

            def mlstm_scores(h):
                r = slice((h % 2) * MD, (h % 2) * MD + MD)
                if h:
                    pe.wait_ge(sem("mlstm_weighted"), 2 * h)
                    pe.wait_ge(sem("mlstm_exp"), 2 * h)
                for s in range(4):
                    pe.matmul(banks[4 + s // 2][:, (s % 2) * T:(s % 2 + 1) * T], kT[r, h // 2, s * P:(s + 1) * P],
                              qT[r, h // 2, :], start=True, stop=True)
                for d in range(2):
                    m = pe.matmul(banks[6][:, d * T:(d + 1) * T], SEL[0:GR, d * MH + h, :], nM, start=True, stop=True)
                m.then_inc(sem("mlstm_scored"), 1)

            def mlstm_values(h):
                if h:
                    pe.wait_ge(sem("mlstm_out"), h)
                parts = ([[(0, 128), (1, 384), (2, 640)], [(0, 0), (1, 256), (2, 512), (3, 768)]],
                         [[(0, 128), (1, 384), (2, 512), (3, 768)], [(0, 0), (1, 256), (3, 640)]])
                for d in range(2):
                    pe.wait_ge(sem("mlstm_weighted"), 2 * h + d + 1)
                    for t in range(TT):
                        ps = parts[d][t]
                        for n, (s, at) in enumerate(ps):
                            lo = (2 * d + t) * (MD + 1)
                            m = pe.matmul(banks[7][:, lo:lo + MD + 1], WDs[h % 2][:, d, at:at + P], vaug[:, s, h, :],
                                          start=n == 0, stop=n == len(ps) - 1)
                m.then_inc(sem("mlstm_summed"), 1)

            mlstm_scores(0)
            for h in range(MH):
                if h + 1 < MH:
                    mlstm_scores(h + 1)
                mlstm_values(h)
                for f in fills_at(2 * DH + h):
                    mod_job(f)

            for f in GAP1:
                mod_job(f)
            pe.wait_ge(sem("mixed"), 1)
            pe.wait_ge(sem("mlstm_out"), MH)
            turn_job(TOK)
            for n in range(2):
                w = chunk_in(f"wo{n}")
                for t in range(TT):
                    tok_unit(f"wo{n}{t}", T1, t, w, fresh=n == t == 0)
            for f in GAP2:
                mod_job(f)
            pe.wait_ge(sem("normed"), 3)
            turn_job(XN)

            def dense_ffn():
                nu = TT * NSTEP
                for i in range(nu + 2):
                    if i < nu:
                        st, t = divmod(i, TT)
                        s = st % RING
                        if t == 0:
                            pe.wait_ge(sem(f"pair_in{s}"), 32 * (st // RING + 1))
                        if i >= 2:
                            pe.wait_ge(sem("hidden"), i - 1)
                        for k in range(KC):
                            operand_chunk(k, i == 0)
                            m = pe.matmul(banks[t][:, :], T1[:, k, t * P:(t + 1) * P], ring[:, s, k, :],
                                          start=k == 0, stop=k == KC - 1)
                        m.then_inc(sem("upped"), 1)
                    if i >= 2:
                        st, t = divmod(i - 2, TT)
                        s = st % RING
                        if t == 0:
                            pe.wait_ge(sem(f"down_in{s}"), 16 * (st // RING + 1))
                        pe.wait_ge(sem("hidden_turned"), i - 1)
                        for j in range(2):
                            for n in range(2):
                                m = pe.matmul(banks[4 + 2 * t + n][:, :], HT[:, t, j, :], dring[:, s, j, n * NCH:(n + 1) * NCH],
                                              start=st == 0 and j == 0, stop=st == NSTEP - 1 and j == 1)
                        m.then_inc(sem("down_done"), 1)
                    if 1 <= i <= nu:
                        t = (i - 1) % TT
                        pe.wait_ge(sem("hidden"), i)
                        if i >= 3:
                            pe.wait_ge(sem("hidden_turned"), i - 2)
                        for j in range(2):
                            m = pe.transpose(banks[2 + t][:, j * P:(j + 1) * P], H[:, t, j * P:(j + 1) * P], ident[:, :])
                        m.then_inc(sem("turned_h"), 1)

            tot, pbase = [0] * RING, {}
            for n, c in (("ffn0", 1), ("moe1", NE1 // 2), ("moeA", NG // 2), ("moeB", NG // 2)):
                pbase[n] = list(tot)
                for q in range(RING):
                    tot[q] += loops[n][2][q] * c

            def moe(m, src):
                pb = pbase[f"moe{m.name}"]
                per = loops[f"moe{m.name}"][2]
                n = m.steps

                def slot_maps(p, f):
                    pe.wait_ge(sem("placed"), f + 1)
                    if not (isinstance(f, int) and f == 0):
                        pe.wait_ge(sem("fetch_read"), 3 * f)
                    for t in range(TT):
                        pe.matmul(banks[3][:, 2 * P:2 * P + m.experts], PM[:, p, t * SL:(t + 1) * SL], bgates[:, t, 0:m.experts],
                                  start=t == 0, stop=t == 1)
                    for t in range(TT):
                        i = pe.transpose(banks[3][:, t * P:(t + 1) * P], PM[:, p, t * SL:(t + 1) * SL], ident[:, :])
                    i.then_inc(sem("fetched"), 1)

                def gather(p, f, half):
                    pe.wait_ge(sem("fetch_read"), 3 * f + (half + 1))
                    for k in range(4):
                        for t in range(TT):
                            i = pe.matmul(banks[3][:, k * SL:(k + 1) * SL], src[:, t, (4 * half + k) * P:(4 * half + k + 1) * P],
                                          PM[:, p, t * SL:(t + 1) * SL], start=t == 0, stop=t == 1)
                    i.then_inc(sem("fetched"), 1)

                def scatter(p, f):
                    pe.wait_ge(sem("ys_ready"), f + (1 - MOES.index(m)))
                    for g in range(4):
                        t, h = divmod(g, 2)
                        pe.wait_ge(sem("added"), 4 * f + (g + 1))
                        pe.matmul(banks[6 + h][:, :], PTM[:, p, t * P:(t + 1) * P], YS[:, h * NCH:(h + 1) * NCH],
                                  start=True, stop=True).then_inc(sem("scattered"), 1)

                def body(it):
                    for u in range(2):
                        g0 = it * (2 * n) + (m.u0 + u * n)
                        f = it * 2 + (m.f0 + u)
                        for i in range(n + 2):
                            q = u * n + i
                            if i < n:
                                s = q % RING
                                pe.wait_ge(sem(f"pair_in{s}"), it * (32 * per[s]) + 32 * (pb[s] + q // RING + 1))
                                pe.wait_ge(sem("hidden"), g0 + (i - 1))
                                if i == 0:
                                    pe.wait_ge(sem("fetch_read"), 3 * f + 3)
                                for k in range(KC):
                                    mm = pe.matmul(banks[q % 2][:, :], XG[:, u, k, :], ring[:, s, k, :], start=k == 0, stop=k == KC - 1)
                                mm.then_inc(sem("upped"), 1)
                            else:
                                gather(1 - u, f + 1, i - n)
                            if i == 1:
                                scatter(1 - u, f)
                            if i == 3:
                                slot_maps(1 - u, f + 1)
                            if i >= 2:
                                s = (q - 2) % RING
                                pe.wait_ge(sem(f"down_in{s}"), it * (16 * per[s]) + 16 * (pb[s] + (q - 2) // RING + 1))
                                if i == 2:
                                    pe.wait_ge(sem("ys_ready"), f + (1 - MOES.index(m)))
                                pe.wait_ge(sem("hidden_turned"), g0 + (i - 1))
                                for j in range(2):
                                    for h in range(2):
                                        mm = pe.matmul(banks[4 + h][:, :], HT[:, q % 2, j, :], dring[:, s, j, h * NCH:(h + 1) * NCH],
                                                       start=i == 2 and j == 0, stop=i == n + 1 and j == 1)
                                mm.then_inc(sem("down_done"), 1)
                            if 1 <= i <= n:
                                pe.wait_ge(sem("hidden"), g0 + i)
                                pe.wait_ge(sem("hidden_turned"), g0 + (i - 1))
                                for j in range(2):
                                    mm = pe.transpose(banks[2][:, j * P:(j + 1) * P], H[:, (q - 1) % 2, j * P:(j + 1) * P], ident[:, :])
                                mm.then_inc(sem("turned_h"), 1)

                slot_maps(0, m.f0)
                gather(0, m.f0, 0)
                gather(0, m.f0, 1)
                with pe.Fori(0, m.bins // 2) as it:
                    body(it)
                scatter(1, m.f0 + m.bins)

                def fetch(b):
                    for t in range(TT):
                        pe.matmul(banks[3][:, 2 * P:2 * P + m.experts], PM[:, 0, t * SL:(t + 1) * SL], bgates[:, t, 0:m.experts],
                                  start=t == 0, stop=t == 1)
                    for t in range(TT):
                        pe.transpose(banks[3][:, t * P:(t + 1) * P], PM[:, 0, t * SL:(t + 1) * SL], ident[:, :])
                    for k in range(KC):
                        for t in range(TT):
                            i = pe.matmul(banks[k // 4][:, k % 4 * SL:(k % 4 + 1) * SL], src[:, t, k * P:(k + 1) * P],
                                          PM[:, 0, t * SL:(t + 1) * SL], start=t == 0, stop=t == 1)
                    return i

                def up(b, c, h):
                    pe.wait_ge(sem(f"second_in{m.name}"), b * (48 * m.steps) + c * (48 * unrolled(m)) + 48 * (h + 1))
                    for k in range(KC):
                        i = pe.matmul(banks[4][:, :], XG[:, 0, k, :], ring[:, 0, k, :], start=k == 0, stop=k == KC - 1)
                    return i

                def turn_hidden(b, c, h):
                    for j in range(2):
                        i = pe.transpose(banks[5][:, j * P:(j + 1) * P], H[:, 0, j * P:(j + 1) * P], ident[:, :])
                    return i

                def down(b, c, h):
                    for w in range(2):
                        for j in range(2):
                            i = pe.matmul(banks[6 + w][:, :], HT[:, 0, j, :], dring[:, 0, j, w * NCH:(w + 1) * NCH],
                                          start=j == 0, stop=j == 1)
                    return i

                def scatter_all(b):
                    for g in range(4):
                        t, w = divmod(g, 2)
                        i = pe.matmul(banks[g][:, :], PTM[:, 0, t * P:(t + 1) * P], YS[:, w * NCH:(w + 1) * NCH], start=True, stop=True)
                    return i

                second_pass(pe, m, [(2, fetch)], [(0, up), (3, turn_hidden), (5, down)], [(0, scatter_all)])

            def banks_read_before(name):
                i = list(bank_of).index(name)
                for b in range(NBANK):
                    pe.wait_ge(sem(f"bank_read{b}"), len([q for q in range(i) if q % NBANK == b]))

            banks_read_before(GAP3[0])
            dense_ffn()

            for f in GAP3:
                mod_job(f)
            pe.wait_ge(sem("normed"), 4)
            turn_job(XN)
            for c in range(2):
                for w_ in ("pa", "pg"):
                    w = chunk_in(f"{w_}{c}")
                    for j in range(2):
                        feat_unit(f"{w_}{c}{j}", T1, j, w, fresh=w_ == "pa" and c == j == 0)
            pe.wait_ge(sem("mem_loaded"), 16)
            turn_job(TOK)
            for f in LATE:
                mod_job(f)
            wait_operand(6)
            for l in range(2):
                w = chunk_in(f"kv{l}_0")
                for j in range(2):
                    feat_unit(f"kv{l}k{j}", memT, j, w)
                w = chunk_in(f"kv{l}_1")
                for j in range(2):
                    tok_unit(f"kv{l}v{j}", memT, j, w)
            turn_job(T2, back=True)
            for f in GAP4:
                mod_job(f)
            pe.wait_ge(sem("normed"), 5)
            turn_job(XN)
            for n in range(2):
                w = chunk_in(f"pw2_{n}")
                for t in range(TT):
                    tok_unit(f"pw2{n}{t}", T1, t, w, fresh=n == t == 0)
            for f in GAP5:
                mod_job(f)
            pe.wait_ge(sem("normed"), 6)
            turn_job(XN)

            def router(name, lo, n):
                o = bank_for(name)
                for t in range(TT):
                    for k in range(KC):
                        operand_chunk(k, t == 0)
                        m = pe.matmul(o[:, t * n:(t + 1) * n], T1[:, k, t * P:(t + 1) * P], wrt[:, k, lo:lo + n],
                                      start=k == 0, stop=k == KC - 1)
                filled(m, name)

            def places(m):
                name, nb = f"pos{m.name}", m.bins
                o = bank_for(name)
                pe.wait_ge(sem("bins_chosen"), 1 + MOES.index(m))
                pe.wait_ge(sem("slots_made"), 1)
                v = chosen[:, :, 0:nb]
                pe.matmul(o[:, 0:nb], upper, v[:, 0, :], start=True, stop=True)
                pe.matmul(o[:, nb:2 * nb], upper, v[:, 1, :], start=True, stop=False)
                pe.matmul(o[:, nb:2 * nb], ones, v[:, 0, :], start=False, stop=True)
                for t in range(TT):
                    i = pe.matmul(o[:, 2 * nb:3 * nb], ones, v[:, t, :], start=t == 0, stop=t == 1)
                filled(i, name)

            router("rt1", 0, NE1)
            places(MOE1)
            banks_read_before("za00")
            moe(MOE1, XN)

            pe.wait_ge(sem("x_updated"), 4)
            turn_job(X)
            for n in range(2):
                w = chunk_in(f"za{n}")
                for t in range(TT):
                    tok_unit(f"za{n}{t}", T1, t, w, fresh=n == t == 0)
            w = chunk_in("za2")
            for j in range(2):
                feat_unit(f"za2{j}", T1, j, w)
            pe.wait_ge(sem("sgu_in"), 16)
            o = bank_for("sguT")
            for h in range(XH):
                m = pe.transpose(o[:, h * P:(h + 1) * P], sguw[:, h, :], ident[:, :])
            filled(m, "sguT")

            def memory_attention(l, units):
                pe.wait_ge(sem("memory_operands"), l + 1)

                def scores(h):
                    u = units + h
                    if h >= 2:
                        pe.wait_ge(sem("mem_exp"), 2 * (u - 1))
                    for t in range(TT):
                        m = pe.matmul(banks[4 + h % 2][:, t * T:(t + 1) * T], xqT[:, h, t * P:(t + 1) * P], kmT[:, l, h, :],
                                      start=True, stop=True)
                    m.then_inc(sem("mem_scored"), 1)

                def values(h):
                    u = units + h
                    pe.wait_ge(sem("mem_prob"), u + 1)
                    if u:
                        pe.wait_ge(sem("mem_prob_turned"), u)
                    for c in range(2):
                        for t in range(TT):
                            m = pe.transpose(banks[6][:, c * T + t * P:c * T + (t + 1) * P], EM[:, h % 2, t, c * P:(c + 1) * P],
                                             ident[:, :])
                    m.then_inc(sem("mem_turned"), 1)
                    pe.wait_ge(sem("mem_prob_turned"), u + 1)
                    if u:
                        pe.wait_ge(sem("mem_out"), u)
                    for c in range(2):
                        m = pe.matmul(banks[7][:, 0:T], vm[:, l, c, h * P:(h + 1) * P], PMT[:, h % 2, c, :],
                                      start=c == 0, stop=c == 1)
                    m.then_inc(sem("mem_summed"), 1)

                scores(0)
                for h in range(XH):
                    if h + 1 < XH:
                        scores(h + 1)
                    values(h)

            memory_attention(0, 0)
            pe.wait_ge(sem("sgu_ready"), 1)
            for t in range(TT):
                o = bank_for(f"sg{t}")
                for h in range(XH):
                    m = pe.matmul(o[:, h * P:(h + 1) * P], sguT[:, h, :], UV[:, t, 1, h * P:(h + 1) * P], start=True, stop=True)
                filled(m, f"sg{t}")
            pe.wait_ge(sem("gated_tokens"), 1)
            for b in range(2):
                o = bank_for(f"tokT{b}")
                for j in range(2):
                    for t in range(TT):
                        c = 2 * b + j
                        m = pe.transpose(o[:, j * T + t * P:j * T + (t + 1) * P], TOK[:, t, c * P:(c + 1) * P], ident[:, :])
                filled(m, f"tokT{b}")
            pe.wait_ge(sem("cat_ready"), 1)
            for n in range(2):
                w = chunk_in(f"woA{n}")
                for t in range(TT):
                    tok_unit(f"woA{n}{t}", T2, t, w)
            pe.wait_ge(sem("x_updated"), 5)
            turn_job(X)
            router("rtA", NE1, NE2)
            places(MOEA)
            banks_read_before("zb00")
            moe(MOEA, X)
            pe.wait_ge(sem("x_updated"), 6)
            turn_job(X)
            for n in range(4):
                w = chunk_in(f"zb{n}")
                for j in range(2):
                    feat_unit(f"zb{n}{j}", T1, j, w, fresh=n == j == 0)
            memory_attention(1, XH)
            pe.wait_ge(sem("cat_ready"), 2)
            for n in range(2):
                w = chunk_in(f"woB{n}")
                for t in range(TT):
                    tok_unit(f"woB{n}{t}", T2, t, w)
            pe.wait_ge(sem("x_updated"), 7)
            turn_job(X)
            router("rtB", NE1, NE2)
            places(MOEB)
            for b in range(NBANK):
                pe.wait_ge(sem(f"bank_read{b}"), len([1 for v in bank_of.values() if v[0] == b]))
            moe(MOEB, X)

        @block.scalar
        def _(act):
            cnt = {}

            def step(ins, name="act_step"):
                cnt[name] = cnt.get(name, 0) + 1
                ins.then_inc(sem(name), 1)
                act.wait_ge(sem(name), cnt[name])

            def take(name):
                b, n = bank_of[name]
                act.wait_ge(sem(f"bank_ready{b}"), n + 1)
                return banks[b]

            def freed(ins, name):
                ins.then_inc(sem(f"bank_read{bank_of[name][0]}"), 1)

            def root():
                n = cnt.get("rooted", 0)
                act.wait_ge(sem("variance"), n + 1)
                step(act.activation(sm[:, 16:32], sm[:, 0:16], ACT.Sqrt), "rooted")

            turn = [0]

            def operand(dst, scl=None, shf=None, ready=True):
                for b in range(4):
                    act.wait_ge(sem("turned"), 4 * turn[0] + b + 1)
                    for j in range(2):
                        k = 2 * b + j
                        src = banks[4 + b][:, j * T:(j + 1) * T]
                        if scl is None:
                            m = act.activation(dst[:, k, :], src, ACT.Copy)
                        else:
                            m = act.activation(dst[:, k, :], src, ACT.Identity, scale=scl[:, k:k + 1], bias=shf[:, k:k + 1])
                    m.then_inc(sem("turned_read"), 1)
                    cnt["turned_read"] = cnt.get("turned_read", 0) + 1
                turn[0] += 1
                act.wait_ge(sem("turned_read"), cnt["turned_read"])
                step(act.activation(sm[:, 500:501], sm[:, 500:501], ACT.Copy), "operand_ready")

            act.wait_ge(sem("scratch_set"), 1)
            act.wait_ge(sem("cols_read"), 1)
            step(act.activation(CT[:, :, :].rearrange("p k j -> p j k"), PCOL[:, 1, 0:16].rearrange("p (j k) -> p j k", j=2),
                                ACT.Silu), "silu_c")
            for c in range(4):
                if c in (0, 1):
                    root()
                o = take(f"mod0_{c}")
                freed(act.activation(mod_rows[:, c * NCH:(c + 1) * NCH], o[0:2, :], ACT.Copy), f"mod0_{c}")
            act.wait_ge(sem("mod_cols"), 1)
            operand(T1, SCL[:, 0, :], MODX[:, 0, 0:8])
            operand(T2, SCL[:, 1, :], MODC[:, 0:8])

            def copy_feat(name, dst):
                o = take(name)
                freed(act.activation(dst, o[:, :].rearrange("p (j t) -> p j t", j=2), ACT.Copy), name)

            for j in range(2):
                copy_feat(f"dkc{j}", kdT[:, 2 * j:2 * j + 2, 0:T])
            for n, t in (("dv0", 2), ("dv1", 3), ("dvc0", 0), ("dvc1", 1)):
                o = take(n)
                freed(act.activation(vd[:, t, :], o[:, :], ACT.Copy), n)
            act.wait_ge(sem("consts_in"), 16 * 14)
            o = take("ig")
            m = act.activation(gi, o[0:GR, :], ACT.Identity, bias=gbias[:, 0:1])
            freed(m, "ig")
            act.wait_ge(sem(f"bank_read{bank_of['ig'][0]}"), bank_of["ig"][1] + 1)
            o = take("fg")
            m = act.activation(gf, o[0:GR, :], ACT.Identity, bias=gbias[:, 1:2])
            freed(m, "fg")
            act.wait_ge(sem(f"bank_read{bank_of['fg'][0]}"), bank_of["fg"][1] + 1)
            step(act.activation(gt_, gf, ACT.Abs))
            step(act.activation(gt_, gt_, ACT.Exp, scale=-1.0))
            step(act.activation(gt_, gt_, ACT.Ln, bias=1.0), "gate_logs")
            for i, n in enumerate(("mk0", "mk1", "mkc0", "mkc1", "mq0", "mq1")):
                act.wait_ge(sem("conv3"), i + 1)
                j = int(n[-1])
                src = CV[:, i % 2, :].rearrange("p (j t) -> p j t", j=2)
                if n[1] == "k":
                    lo = 0 if "c" in n else T
                    step(act.activation(kT[:, 2 * j:2 * j + 2, lo:lo + T], src, ACT.Silu), "conv3_read")
                else:
                    for t in range(TT):
                        m = act.activation(qT[:, 2 * j:2 * j + 2, (1 - t) * P:(2 - t) * P], src[:, :, t * P:(t + 1) * P], ACT.Silu)
                    step(m, "conv3_read")
            act.wait_ge(sem("masks_made"), 1)
            for n, s in (("mv0", 2), ("mv1", 3), ("mvc0", 0), ("mvc1", 1)):
                o = take(n)
                freed(act.activation(vaug[:, s, :, 0:MD], o[:, :].rearrange("p (h d) -> p h d", h=MH), ACT.Copy), n)
            for t in range(TT):
                o = take(f"mo{t}")
                freed(act.activation(osig[:, t, :], o[:, :], ACT.Sigmoid), f"mo{t}")
            for b in range(2):
                copy_feat(f"dqT{b}", qdT[:, 2 * b:2 * b + 2, :])
            for b in range(2):
                copy_feat(f"dkT{b}", kdT[:, 2 * b:2 * b + 2, T:2 * T])
            step(act.activation(sm[:, 500:501], sm[:, 500:501], ACT.Copy), "diff_operands")
            act.wait_ge(sem("gate_sums"), 1)
            step(act.activation(gE, gE, ACT.Exp), "gate_rows")
            act.wait_ge(sem("lambdas"), 1)
            step(act.activation(sm[:, 40:42], sm[:, 40:42], ACT.Exp), "lambda_exp")
            for u in range(2 * DH):
                act.wait_ge(sem("diff_bias"), u + 1)
                if u >= 2:
                    act.wait_ge(sem("diff_prob"), u - 1)
                for i in range(2):
                    act.activation(EX[:, u % 2, i, :], banks[4 + i][:, :], ACT.Exp, scale=DQ ** -0.5,
                                   bias=sm[:, 48 + 2 * (u % 2) + i:49 + 2 * (u % 2) + i],
                                   accum_out=sm[:, 52 + 2 * (u % 2) + i:53 + 2 * (u % 2) + i]).then_inc(sem("diff_exp"), 1)
                if u >= 1:
                    act.wait_ge(sem("diff_turned"), u)
                    if u >= 3:
                        act.wait_ge(sem("diff_summed"), u - 2)
                    act.activation(PT[:, (u - 1) % 2, :], banks[6][:, :], ACT.Copy).then_inc(sem("diff_prob_turned"), 1)
            act.wait_ge(sem("diff_turned"), 2 * DH)
            act.activation(PT[:, 1, :], banks[6][:, :], ACT.Copy).then_inc(sem("diff_prob_turned"), 1)
            def mlstm_evict(h):
                act.wait_ge(sem("mlstm_summed"), h + 1)
                step(act.activation(HR[:, h, :, :], banks[7][:, 0:4 * (MD + 1)].rearrange("p (a d) -> p a d", a=4), ACT.Copy),
                     "mlstm_out")
            act.wait_ge(sem("diff_out"), 2 * DH)
            act.wait_ge(sem("gate_cols"), 1)
            for h in range(MH):
                act.wait_ge(sem("mlstm_scored"), h + 1)
                WD = WDs[h % 2]
                if h >= 2:
                    act.wait_ge(sem("mlstm_summed"), h - 1)
                act.wait_ge(sem("mlstm_args"), 2 * h + 2)
                for d in range(2):
                    for s in range(2):
                        act.activation(WD[:, d, s * T:(s + 1) * T], banks[6][:, d * T:(d + 1) * T], ACT.Exp,
                                       bias=GCt[:, s, 32 * d + h:32 * d + h + 1])
                    act.activation(WD[:, d, 2 * T:896], AR[:, d, :], ACT.Exp).then_inc(sem("mlstm_exp"), 1)
                if h:
                    mlstm_evict(h - 1)
            mlstm_evict(MH - 1)

            def evict_tok(name, n, t):
                o = take(f"{name}{n}{t}")
                act.activation(XN[:, t, n * NCH:(n + 1) * NCH], o[:, :], ACT.Copy).then_inc(
                    sem(f"bank_read{bank_of[f'{name}{n}{t}'][0]}"), 1)

            root()
            root()
            operand(T1)
            for n in range(2):
                for t in range(TT):
                    evict_tok("wo", n, t)
            root()
            root()
            operand(T1, SCL[:, 2, :], MODX[:, 0, 24:32])

            def silu_up(i, g):
                act.wait_ge(sem("upped"), g + 1)
                if not (isinstance(g, int) and g < 2):
                    act.wait_ge(sem("hidden"), g - 1)
                act.activation(SG[:, i % 2, :], banks[i % 2][:, 0:FSTEP], ACT.Silu).then_inc(sem("silued"), 1)

            def take_turned(i, g, bank):
                act.wait_ge(sem("turned_h"), g + 1)
                if not (isinstance(g, int) and g < 2):
                    act.wait_ge(sem("down_done"), g - 1)
                act.activation(HT[:, i % 2, :, :], bank[:, 0:2 * P].rearrange("p (j n) -> p j n", j=2),
                               ACT.Copy).then_inc(sem("hidden_turned"), 1)

            for i in range(U_FFN + 1):
                if i < U_FFN:
                    silu_up(i, i)
                if i:
                    take_turned(i - 1, i - 1, banks[2 + (i - 1) % 2])
            act.wait_ge(sem("down_done"), U_FFN)
            for t in range(TT):
                for n in range(2):
                    act.activation(XN[:, t, n * NCH:(n + 1) * NCH], banks[4 + 2 * t + n][:, :], ACT.Copy).then_inc(
                        sem("sums_taken"), 1)
            act.wait_ge(sem("sums_taken"), 2 * TT)
            act.activation(sm[:, 500:501], sm[:, 500:501], ACT.Copy).then_inc(sem("ys_ready"), 1)

            def moe(m, scl=None, shf=None):
                n = m.steps

                def slot_maps(p, f):
                    act.wait_ge(sem("fetched"), 3 * f + 1)
                    act.activation(sgates[:, p, 0:m.experts], banks[3][:, 2 * P:2 * P + m.experts], ACT.Copy)
                    act.activation(PTM[:, p, :], banks[3][:, 0:2 * P], ACT.Copy).then_inc(sem("fetch_read"), 1)

                def rows(dst, bank, half):
                    if scl is None:
                        return act.activation(dst[:, 4 * half:4 * half + 4, :], bank[:, :].rearrange("p (k n) -> p k n", k=4), ACT.Copy)
                    for k in range(4):
                        c = 4 * half + k
                        i = act.activation(dst[:, c, :], bank[:, k * SL:(k + 1) * SL], ACT.Identity,
                                           scale=scl[:, c:c + 1], bias=shf[:, c:c + 1])
                    return i

                def gathered(p, f, half):
                    act.wait_ge(sem("fetched"), 3 * f + (half + 2))
                    rows(XG[:, p, :, :], banks[3], half).then_inc(sem("fetch_read"), 1)

                def body(it):
                    for u in range(2):
                        g0 = it * (2 * n) + (m.u0 + u * n)
                        f = it * 2 + (m.f0 + u)
                        for i in range(n + 2):
                            if i < n:
                                silu_up(u * n + i, g0 + i)
                            else:
                                gathered(1 - u, f + 1, i - n)
                            if i == 3:
                                slot_maps(1 - u, f + 1)
                            if 1 <= i <= n:
                                take_turned(u * n + i - 1, g0 + (i - 1), banks[2])
                        act.wait_ge(sem("down_done"), g0 + n)
                        act.wait_ge(sem("scattered"), 4 * f + 4)
                        for h in range(2):
                            i = act.activation(YS[:, h * NCH:(h + 1) * NCH], banks[4 + h][:, :], ACT.Copy)
                        i.then_inc(sem("ys_ready"), 1)

                slot_maps(0, m.f0)
                gathered(0, m.f0, 0)
                gathered(0, m.f0, 1)
                with act.Fori(0, m.bins // 2) as it:
                    body(it)

                def take(b):
                    act.activation(sgates[:, 0, 0:m.experts], banks[3][:, 2 * P:2 * P + m.experts], ACT.Copy)
                    act.activation(PTM[:, 0, :], banks[3][:, 0:2 * P], ACT.Copy)
                    rows(XG[:, 0, :, :], banks[0], 0)
                    return rows(XG[:, 0, :, :], banks[1], 1)

                def silu(b, c, h):
                    return act.activation(SG[:, 0, :], banks[4][:, 0:FSTEP], ACT.Silu)

                def take_hidden(b, c, h):
                    return act.activation(HT[:, 0, :, :], banks[5][:, 0:2 * P].rearrange("p (j n) -> p j n", j=2), ACT.Copy)

                second_pass(act, m, [(3, take)], [(1, silu), (4, take_hidden)], [])

            root()
            root()
            act.wait_ge(sem("conv_gains"), 1)
            operand(T1, SCL[:, 3, :], MODX[:, 1, 0:8])
            for c in range(2):
                for j in range(2):
                    i = 2 * c + j
                    o = take(f"pg{c}{j}")
                    if i >= 2:
                        act.wait_ge(sem("glu"), i - 1)
                    for q in range(2):
                        k = 4 * c + 2 * j + q
                        m = act.activation(SGC[:, i % 2, q * T:(q + 1) * T], o[:, q * T:(q + 1) * T], ACT.Sigmoid,
                                           bias=PCOL[:, 1, 56 + k:57 + k])
                    freed(m, f"pg{c}{j}")
            operand(memT)
            for l in range(2):
                for j in range(2):
                    copy_feat(f"kv{l}k{j}", kmT[:, l, 2 * j:2 * j + 2, :])
                for j in range(2):
                    o = take(f"kv{l}v{j}")
                    freed(act.activation(vm[:, l, j, :], o[:, :], ACT.Copy), f"kv{l}v{j}")
            for b in range(4):
                act.wait_ge(sem("turned"), 4 * turn[0] + b + 1)
                act.activation(XN[:, b % 2, (b // 2) * NCH:(b // 2 + 1) * NCH], banks[4 + b][:, :], ACT.Copy).then_inc(
                    sem("turned_read"), 1)
                cnt["turned_read"] += 1
            turn[0] += 1
            root()
            act.wait_ge(sem("conv_normed"), 1)
            for t in range(TT):
                m = act.activation(XN[:, t, :], XN[:, t, :], ACT.Silu)
            act.wait_ge(sem("normed"), 4)
            m.then_inc(sem("normed"), 1)
            operand(T1)
            root()
            root()
            operand(T1, SCL[:, 4, :], MODX[:, 1, 24:32])
            act.wait_ge(sem("router_max"), 1)
            for t in range(TT):
                m = act.activation(gates[:, t, 0:NE1], gates[:, t, 0:NE1], ACT.Exp, bias=sm[:, 60 + t:61 + t])
            step(m, "router_act")
            moe(MOE1, SCL[:, 4, :], MODX[:, 1, 24:32])
            root()
            operand(T1)
            for n in range(2):
                for t in range(TT):
                    o = take(f"za{n}{t}")
                    freed(act.activation(UV[:, t, n, :], o[:, :], ACT.Gelu), f"za{n}{t}")
            step(act.activation(sm[:, 500:501], sm[:, 500:501], ACT.Copy), "gelu_done")
            for j in range(2):
                copy_feat(f"za2{j}", xqT[:, 2 * j:2 * j + 2, :])
            step(act.activation(sm[:, 500:501], sm[:, 500:501], ACT.Copy), "memory_operands")
            o = take("sguT")
            freed(act.activation(sguT, o[:, :].rearrange("p (h i) -> p h i", h=XH), ACT.Copy), "sguT")

            def memory_attention(units):
                for h in range(XH + 1):
                    u = units + h
                    if h < XH:
                        act.wait_ge(sem("mem_bias"), u + 1)
                        if u >= 2:
                            act.wait_ge(sem("mem_turned"), u - 1)
                        for t in range(TT):
                            c = 2 * (u % 2) + t
                            act.activation(EM[:, h % 2, t, :], banks[4 + h % 2][:, t * T:(t + 1) * T], ACT.Exp, scale=P ** -0.5,
                                           bias=sm[:, 48 + c:49 + c], accum_out=sm[:, 52 + c:53 + c]).then_inc(sem("mem_exp"), 1)
                    if h:
                        act.wait_ge(sem("mem_turned"), u)
                        if u >= 3:
                            act.wait_ge(sem("mem_summed"), u - 2)
                        act.activation(PMT[:, (h - 1) % 2, :, :], banks[6][:, :].rearrange("p (c t) -> p c t", c=2),
                                       ACT.Copy).then_inc(sem("mem_prob_turned"), 1)
                        act.wait_ge(sem("mem_summed"), u)
                        step(act.activation(T2[:, 4 + h - 1, :], banks[7][:, 0:T], ACT.Copy), "mem_out")

            memory_attention(0)
            root()
            act.wait_ge(sem("gated_tokens"), 1)
            for b in range(2):
                copy_feat(f"tokT{b}", T2[:, 2 * b:2 * b + 2, :])
            step(act.activation(sm[:, 500:501], sm[:, 500:501], ACT.Copy), "cat_ready")
            root()
            operand(T1)
            for l, name in ((0, "A"), (1, "B")):
                o = take(f"rt{name}")
                m = act.activation(gates[:, :, 0:NE2], o[:, 0:TT * NE2].rearrange("p (t e) -> p t e", t=TT), ACT.Sigmoid)
                freed(m, f"rt{name}")
                moe(MOEA if l == 0 else MOEB)
                root()
                if l == 0:
                    operand(T1)
                    for j in range(2):
                        copy_feat(f"zb0{j}", bgT[:, 2 * j:2 * j + 2, :])
                    for j in range(2):
                        copy_feat(f"zb1{j}", cgT[:, 2 * j:2 * j + 2, :])
                    step(act.activation(sm[:, 500:501], sm[:, 500:501], ACT.Copy), "conv_gates")
                    for j in range(2):
                        copy_feat(f"zb3{j}", xqT[:, 2 * j:2 * j + 2, :])
                    step(act.activation(sm[:, 500:501], sm[:, 500:501], ACT.Copy), "memory_operands")
                    memory_attention(XH)
                    root()
                    operand(T1)

        @block.vector
        def _(dve):
            cnt = {}

            def step(ins, name="dve_step"):
                cnt[name] = cnt.get(name, 0) + 1
                ins.then_inc(sem(name), 1)
                dve.wait_ge(sem(name), cnt[name])

            def take(name):
                b, n = bank_of[name]
                dve.wait_ge(sem(f"bank_ready{b}"), n + 1)
                return banks[b]

            def free(ins, name):
                b, n = bank_of[name]
                ins.then_inc(sem(f"bank_read{b}"), 1)
                dve.wait_ge(sem(f"bank_read{b}"), n + 1)

            def invert_root():
                n = cnt.get("variance", 0)
                dve.wait_ge(sem("rooted"), n)
                step(dve.reciprocal(sm[:, 64:80], sm[:, 16:32]))

            stats = sm[:, 96:96 + 24].rearrange("p (t c s) -> p t c s", t=2, c=2)
            mv = sm[:, 120:124].rearrange("p (t s) -> p t s", t=2)
            junk = sm[:, 124:125]

            def piece_stats(src, t, c):
                return dve.bn_stats(stats[:, t, c, :], src[:, t, c * NCH:(c + 1) * NCH])

            def rms(src, beside=None, pieces=True):
                if pieces:
                    for t in range(TT):
                        for c in range(2):
                            m = piece_stats(src, t, c)
                    step(m)
                for t in range(TT):
                    m = dve.bn_aggr(mv[:, t, :], stats[:, t, :, :])
                step(m)
                for t in range(TT):
                    m = dve.scalar_tensor_tensor(sm[:, 32 + t:33 + t], mv[:, t, 0:1], mv[:, t, 0:1], mv[:, t, 1:2], ALU.mult, ALU.add)
                step(m)
                step(dve.tensor_scalar(sm[:, 0:2], sm[:, 32:34], EPS, None, ALU.add), "variance")
                if beside is not None:
                    beside()
                invert_root()

            def layer_norm(src, dst, g, b, eps, width, pieces=True):
                nb = width // NCH
                if pieces:
                    for t in range(TT):
                        for c in range(nb):
                            m = piece_stats(src, t, c)
                    step(m)
                for t in range(TT):
                    m = dve.bn_aggr(mv[:, t, :], stats[:, t, 0:nb, :])
                step(m)
                step(dve.tensor_scalar(sm[:, 0:2], mv[:, :, 1], eps, None, ALU.add), "variance")
                for t in range(TT):
                    m = dve.scalar_tensor_tensor(src[:, t, :], src[:, t, :], mv[:, t, 0:1], g, ALU.subtract, ALU.mult)
                step(m)
                invert_root()
                for t in range(TT):
                    m = dve.scalar_tensor_tensor(dst[:, t, :], src[:, t, :], sm[:, 64 + t:65 + t], b, ALU.mult, ALU.add)
                return m

            def scale_rows(dst, src, name="normed"):
                for t in range(TT):
                    m = dve.tensor_scalar(dst[:, t, :], src[:, t, :], sm[:, 64 + t:65 + t], None, ALU.mult)
                step(m, name)

            def post(g, src, pieces=True):
                def gate():
                    for t in range(TT):
                        m = dve.tensor_tensor(src[:, t, :], src[:, t, :], GP[:, g, :], ALU.mult)
                    step(m)
                rms(src, gate, pieces)
                for t in range(TT):
                    m = dve.scalar_tensor_tensor(X[:, t, :], src[:, t, :], sm[:, 64 + t:65 + t], X[:, t, :], ALU.mult, ALU.add)
                step(m, "x_updated")

            dve.memset(gates[:, :, :], 0.0)
            step(dve.memset(sm[:, :], 1.0), "scratch_set")
            dve.wait_ge(sem("cols_turned"), 1)
            for i, n in enumerate((P, 80, P, TAPS * KC - P)):
                m = dve.tensor_copy(PCOL[:, i, 0:n], banks[7][:, i * P:i * P + n])
            step(m, "cols_read")
            dve.wait_ge(sem("x_loaded"), 16)
            rms(X)
            scale_rows(XN, X)
            dve.wait_ge(sem("ctx_loaded"), 16)
            rms(TOK)
            scale_rows(TOK, TOK)
            dve.wait_ge(sem("silu_c"), 1)
            step(dve.tensor_copy(CB[:, :, :], CT[:, :, 0:1].broadcast_to([P, KC, P])), "c_spread")

            row_jobs = [0]

            def mod_job(name):
                l, c = int(name[3]), int(name[5:])
                o = take(name)
                if c in (4, 5, 10, 11):
                    rows = RB
                    if name == GAP5[1]:
                        rows = RB2
                        dve.wait_ge(sem("last_rows_in"), 32)
                    else:
                        row_jobs[0] += 1
                        dve.wait_ge(sem("rows_in"), 32 * row_jobs[0])
                    dst = GP[:, int(c > 5), (c % 2) * NCH:(c % 2 + 1) * NCH]
                    free(dve.tensor_tensor(dst, o[:, :], rows[:, 0, :], ALU.add), name)
                    step(dve.tensor_tensor(dst, dst, rows[:, 1, :], ALU.mult), "rows_used")
                    return
                d = SG[:, :, :].rearrange("p a n -> p (a n)").rearrange("p (j n) -> p j n", j=4)
                step(dve.tensor_tensor(d, o[:, :].rearrange("p (j n) -> p j n", j=4),
                                       ident[:, :].rearrange("p (a n) -> p a n", a=1).broadcast_to([P, 4, P]), ALU.mult))
                m = MODX[:, l, 4 * c:4 * c + 4]
                free(dve.tensor_reduce(m, d, axis=AX.X, op=ALU.add), name)
                step(dve.tensor_tensor(m, m, PCOL[:, 0, 64 * l + 4 * c:64 * l + 4 * c + 4], ALU.add))

            def gains(i, l, which, sc):
                g = PCOL[:, 0, 64 * l + 48 + 8 * which:64 * l + 56 + 8 * which]
                return dve.scalar_tensor_tensor(SCL[:, i, :], sc, 1.0, g, ALU.add, ALU.mult)

            o = take("mod0T")
            v = o[:, 0:32].rearrange("p (j c) -> p c j", c=2)
            dve.tensor_tensor(MODX[:, 0, 0:16], v[:, 0, :], PCOL[:, 0, 0:16], ALU.add)
            free(dve.tensor_tensor(MODC[:, :], v[:, 1, :], PCOL[:, 0, 0:16], ALU.add), "mod0T")
            gains(0, 0, 0, MODX[:, 0, 8:16])
            step(gains(1, 0, 0, MODC[:, 8:16]), "mod_cols")
            dve.wait_ge(sem("consts_in"), 16 * 14)
            for i, n in enumerate("qk"):
                for t in range(TT):
                    o = take(f"d{n}{t}")
                    v = XN[:, t, i * NCH:(i + 1) * NCH]
                    if i == 0 and t == 0:
                        dve.wait_ge(sem("turned"), 4)
                    c = rope[:, t:t + 1, 0, :].broadcast_to([P, 8, 64])
                    dve.tensor_tensor(v.rearrange("p (g d) -> p g d", g=8), o[:, :].rearrange("p (g d) -> p g d", g=8), c, ALU.mult)
                    ov = o[:, :].rearrange("p (g a f d) -> p g a f d", g=8, a=2, f=2)
                    tv = TOK[:, t, i * NCH:(i + 1) * NCH].rearrange("p (g a f d) -> p g a f d", g=8, a=2, f=2)
                    sv = rope[:, t, 1, :].rearrange("p (b a f d) -> p b a f d", b=1, a=2, f=2)
                    if i == 0 and t == 0:
                        dve.wait_ge(sem("turned"), 8)
                    for f in range(2):
                        m = dve.tensor_tensor(tv[:, :, :, f, :], ov[:, :, :, 1 - f, :], sv[:, :, :, f, :].broadcast_to([P, 8, 2, 16]), ALU.mult)
                    free(m, f"d{n}{t}")
                    m = dve.tensor_tensor(v, v, TOK[:, t, i * NCH:(i + 1) * NCH], ALU.add)
                step(m, "rotated")
            s = g_at["gates"][0]
            dve.wait_ge(sem("gate_pad"), 1)
            dve.wait_ge(sem("masks_made"), 1)
            dve.wait_ge(sem(f"chunk_in{s}"), 16 * (g_at["gates"][1] + 1))
            for d in range(2):
                for w in range(2):
                    m = dve.tensor_copy(WG[:, :, w, 32 * d:32 * d + 8], ring[:, s, :, 16 * d + 8 * w:16 * d + 8 * w + 8])
            step(m, "gate_weights")
            for i, n in enumerate(("mk0", "mk1", "mkc0", "mkc1", "mq0", "mq1")):
                j = int(n[-1])
                o = take(n)
                if i >= 2:
                    dve.wait_ge(sem("conv3_read"), i - 1)
                cv = CV[:, i % 2, :].rearrange("p (j t) -> p j t", j=2)
                ov = o[:, :].rearrange("p (j t) -> p j t", j=2)
                col = lambda tap, q: PCOL[:, 1, 16 + 8 * tap + (4 if n[1] == "k" else 0) + 2 * j + q:
                                          17 + 8 * tap + (4 if n[1] == "k" else 0) + 2 * j + q]
                for q in range(2):
                    m = dve.tensor_scalar(cv[:, q, :], ov[:, q, :], col(1, q), None, ALU.mult)
                step(m)
                for q in range(2):
                    m = dve.scalar_tensor_tensor(cv[:, q, 1:T], ov[:, q, 0:T - 1], col(0, q), cv[:, q, 1:T], ALU.mult, ALU.add)
                step(m)
                for q in range(2):
                    m = dve.scalar_tensor_tensor(cv[:, q, 0:T - 1], ov[:, q, 1:T], col(2, q), cv[:, q, 0:T - 1], ALU.mult, ALU.add)
                free(m, n)
                step(dve.memset(junk, 0.0), "conv3")
            dve.wait_ge(sem("gate_logs"), 1)
            step(dve.tensor_scalar(gf, gf, 0.0, None, ALU.min))
            step(dve.tensor_tensor(gf, gf, gt_, ALU.subtract))
            fw, bw = slice(0, 8), slice(32, 40)

            def scans(dst, src, data0, op0, op1):
                c, s = slice(0, T), slice(T, 2 * T)
                init = 0.0 if op0 == ALU.mult else -3e38
                dve.tensor_tensor_scan(dst[fw, :], data0[fw, :], src[fw, :], init, op0, op1)
                step(dve.tensor_tensor_scan(dst[bw, T - 1::-1], data0[bw, T - 1::-1], src[bw, T - 1::-1], init, op0, op1))
                step(dve.tensor_tensor_scan(dst[bw, 2 * T - 1:T - 1:-1], data0[bw, 2 * T - 1:T - 1:-1],
                                            src[bw, 2 * T - 1:T - 1:-1], dst[bw, 0:1], op0, op1))

            step(dve.memset(gB, 0.0))
            scans(gB, gf, onesr, ALU.mult, ALU.add)
            step(dve.tensor_tensor(gG, gi, gB, ALU.subtract))
            step(dve.memset(gt_, 0.0))
            scans(gt_, gG, gG, ALU.max, ALU.max)
            for t in range(TT):
                m = dve.tensor_scalar(nM[:, (1 - t) * P:(2 - t) * P], gt_[:, T + t * P:T + (t + 1) * P], -1.0, None, ALU.mult)
            step(m)
            step(dve.scalar_tensor_tensor(gE, gB[:, T:2 * T], -1.0, gt_[:, T:2 * T], ALU.mult, ALU.subtract))
            step(dve.tensor_scalar(gE, gE, 80.0, None, ALU.min), "gate_sums")
            for i in range(2):
                m = dve.tensor_tensor(lamv[:, 2 * i, :], lamv[:, 2 * i, :], lamv[:, 2 * i + 1, :], ALU.mult)
            step(m)
            for i in range(2):
                m = dve.reduce_sum(sm[:, 40 + i:41 + i], lamv[:, 2 * i, :], axis=AX.X)
            step(m, "lambdas")
            dve.wait_ge(sem("lambda_exp"), 1)
            step(dve.tensor_tensor(sm[:, 42:43], sm[:, 40:41], sm[:, 41:42], ALU.subtract))
            step(dve.tensor_scalar(sm[:, 43:44], sm[:, 42:43], LAM_INIT, -1.0, ALU.add, ALU.mult))
            o = take("gT")
            free(dve.tensor_copy(GCt[:, :, :], o[:, 0:6 * GR].rearrange("p (a n) -> p a n", a=6)), "gT")
            wait_output(dve, "mo1")
            for d in range(2):
                m = dve.tensor_copy(SEL[0:GR, d * MH:(d + 1) * MH, :],
                                    ident[0:GR, 32 * d:32 * d + MH].rearrange("p (h a) -> p h a", a=1).broadcast_to([GR, MH, P]))
            step(m)
            step(dve.memset(junk, 0.0), "gate_cols")
            def diff_bias(u):
                c = 2 * (u % 2)
                for i in range(2):
                    dve.wait_ge(sem("diff_scored"), 2 * u + i + 1)
                    m = dve.reduce_max(sm[:, 44 + i:45 + i], banks[4 + i][:, :], axis=AX.X)
                step(m)
                step(dve.tensor_scalar(sm[:, 48 + c:50 + c], sm[:, 44:46], -(DQ ** -0.5), None, ALU.mult), "diff_bias")

            def diff_prob(u):
                c = 2 * (u % 2)
                dve.wait_ge(sem("diff_exp"), 2 * u + 2)
                step(dve.reciprocal(sm[:, 56:58], sm[:, 52 + c:54 + c]))
                step(dve.tensor_tensor(sm[:, 57:58], sm[:, 57:58], sm[:, 43:44], ALU.mult))
                step(dve.tensor_scalar(EX[:, u % 2, 1, :], EX[:, u % 2, 1, :], sm[:, 57:58], None, ALU.mult))
                if u >= 2:
                    dve.wait_ge(sem("diff_turned"), u - 1)
                step(dve.scalar_tensor_tensor(PR[:, u % 2, :], EX[:, u % 2, 0, :], sm[:, 56:57], EX[:, u % 2, 1, :], ALU.mult, ALU.add),
                     "diff_prob")

            def diff_out(u):
                h, t = divmod(u, TT)
                dve.wait_ge(sem("diff_summed"), u + 1)
                step(dve.tensor_copy(TOK[:, t, NCH + h * DV:NCH + (h + 1) * DV], banks[7][:, 0:DV]), "diff_out")

            diff_bias(0)
            for u in range(2 * DH):
                diff_prob(u)
                if u + 1 < 2 * DH:
                    diff_bias(u + 1)
                if u:
                    diff_out(u - 1)
                    for f in fills_at(u - 1):
                        mod_job(f)
            diff_out(2 * DH - 1)
            dve.wait_ge(sem(f"bank_read{bank_of['mo1'][0]}"), bank_of["mo1"][1] + 1)
            step(dve.memset(junk, 0.0), "mlstm_operands")
            for h in range(MH):
                dve.wait_ge(sem("mlstm_scored"), h + 1)
                for d, msk in enumerate((mskf, mskb)):
                    at = 32 * d + h
                    lo = d * T
                    if h:
                        dve.wait_ge(sem("mlstm_exp"), 2 * (h - 1) + d + 1)
                    if d == 0:
                        parts = ((2, slice(0, 256), slice(0, 2), slice(lo, lo + 256)), (3, slice(256, 384), slice(2, 3), slice(lo, lo + 128)))
                    else:
                        parts = ((2, slice(0, 128), slice(0, 1), slice(lo + 128, lo + 256)), (3, slice(128, 384), slice(1, 3), slice(lo, lo + 256)))
                    for s, a, q, b in parts:
                        m = dve.scalar_tensor_tensor(AR[:, d, a], banks[6][:, b], GCt[:, s, at:at + 1],
                                                     msk[:, q, :].rearrange("p a n -> p (a n)"), ALU.add, ALU.min)
                    step(m, "mlstm_args")
                WD = WDs[h % 2]
                for d in range(2):
                    dve.wait_ge(sem("mlstm_exp"), 2 * h + d + 1)
                    dve.scalar_tensor_tensor(WD[:, d, 0:512], banks[4][:, :], MD ** -0.5, WD[:, d, 0:512], ALU.mult, ALU.mult)
                    step(dve.scalar_tensor_tensor(WD[:, d, 512:896], banks[5][:, d * P:d * P + 384], MD ** -0.5, WD[:, d, 512:896],
                                                  ALU.mult, ALU.mult), "mlstm_weighted")
                for f in fills_at(2 * DH + h - 1):
                    mod_job(f)
            for f in fills_at(SLOTS - 1):
                mod_job(f)
            step(gains(2, 0, 1, MODX[:, 0, 32:40]))
            dve.wait_ge(sem("mlstm_out"), MH)
            DN = sm[:, 128:128 + 32].rearrange("p (a h) -> p a h", a=4)
            for a in range(4):
                m = dve.scalar_tensor_tensor(DN[:, a, :], HR[:, :, a, MD], -1.0, HR[:, :, a, MD], ALU.mult, ALU.max)
            step(m)
            for a in range(4):
                d, t = divmod(a, TT)
                m = dve.tensor_tensor(DN[:, a, :], DN[:, a, :], GCt[:, 4 + t, 32 * d:32 * d + MH], ALU.max)
            step(m)
            step(dve.reciprocal(sm[:, 128:160], sm[:, 128:160]))
            for a in range(4):
                m = dve.tensor_tensor(HR[:, :, a, 0:MD], HR[:, :, a, 0:MD],
                                      DN[:, a, :].rearrange("p (h a) -> p h a", a=1).broadcast_to([P, MH, MD]), ALU.mult)
            step(m)
            for t in range(TT):
                m = dve.tensor_tensor(TOK[:, t, 0:NCH].rearrange("p (h d) -> p h d", h=MH), HR[:, :, t, 0:MD], HR[:, :, 2 + t, 0:MD], ALU.add)
            step(m)
            for t in range(TT):
                m = dve.tensor_tensor(XN[:, t, :], TOK[:, t, :], TOK[:, t, :], ALU.mult)
            step(m)
            hs = sm[:, 160:184].rearrange("p (t n) -> p t n", t=TT)
            for t in range(TT):
                dve.tensor_reduce(hs[:, t, 0:8], XN[:, t, 0:NCH].rearrange("p (h d) -> p h d", h=8), axis=AX.X, op=ALU.add)
                m = dve.tensor_reduce(hs[:, t, 8:12], XN[:, t, NCH:D].rearrange("p (h d) -> p h d", h=4), axis=AX.X, op=ALU.add)
            step(m)
            step(dve.tensor_scalar(sm[:, 0:16].rearrange("p (t n) -> p t n", t=TT), hs[:, :, 0:8], 1.0 / MD, EPS, ALU.mult, ALU.add))
            step(dve.tensor_scalar(sm[:, 184:192].rearrange("p (t n) -> p t n", t=TT), hs[:, :, 8:12], 1.0 / DV, EPS, ALU.mult, ALU.add), "variance")
            invert_root()
            step(dve.tensor_copy(sm[:, 192:208], sm[:, 64:80]))
            step(dve.tensor_copy(sm[:, 0:8], sm[:, 184:192]), "variance")
            invert_root()
            for t in range(TT):
                a = sm[:, 192 + 8 * t:200 + 8 * t].rearrange("p (h a) -> p h a", a=1).broadcast_to([P, 8, MD])
                b = sm[:, 64 + 4 * t:68 + 4 * t].rearrange("p (h a) -> p h a", a=1).broadcast_to([P, 4, DV])
                dve.tensor_tensor(TOK[:, t, 0:NCH].rearrange("p (h d) -> p h d", h=8), TOK[:, t, 0:NCH].rearrange("p (h d) -> p h d", h=8), a, ALU.mult)
                m = dve.tensor_tensor(TOK[:, t, NCH:D].rearrange("p (h d) -> p h d", h=4), TOK[:, t, NCH:D].rearrange("p (h d) -> p h d", h=4), b, ALU.mult)
            step(m)
            for t in range(TT):
                m = dve.tensor_tensor(TOK[:, t, :], TOK[:, t, :], RS[:, 0, :], ALU.mult)
            step(m)
            for t in range(TT):
                dve.tensor_tensor(TOK[:, t, 0:NCH], TOK[:, t, 0:NCH], osig[:, t, :], ALU.mult)
                m = dve.tensor_scalar(TOK[:, t, NCH:D], TOK[:, t, NCH:D], 1.0 - LAM_INIT, None, ALU.mult)
            step(m, "mixed")
            for f in GAP1:
                mod_job(f)

            for n in range(2):
                for t in range(TT):
                    b, k = bank_of[f"wo{n}{t}"]
                    dve.wait_ge(sem(f"bank_read{b}"), k + 1)
                    m = piece_stats(XN, t, n)
            step(m)
            post(0, XN, pieces=False)
            rms(X)
            scale_rows(XN, X)
            for f in GAP2:
                mod_job(f)

            for i in range(U_FFN):
                dve.wait_ge(sem("silued"), i + 1)
                if i >= 2:
                    dve.wait_ge(sem("turned_h"), i - 1)
                dve.tensor_tensor(H[:, i % 2, :], SG[:, i % 2, :], banks[i % 2][:, FSTEP:NCH], ALU.mult).then_inc(sem("hidden"), 1)
            for t in range(TT):
                for n in range(2):
                    dve.wait_ge(sem("sums_taken"), TT * t + n + 1)
                    m = piece_stats(XN, t, n)
            step(m)
            post(1, XN, pieces=False)
            rms(X)
            scale_rows(XN, X)
            for f in GAP3:
                mod_job(f)
            step(gains(3, 1, 0, MODX[:, 1, 8:16]), "conv_gains")
            dve.wait_ge(sem("margins"), 2)
            for c in range(2):
                for j in range(2):
                    b, k = bank_of[f"pg{c}{j}"]
                    dve.wait_ge(sem(f"bank_read{b}"), k + 1)
                    o = take(f"pa{c}{j}")
                    i = 2 * c + j
                    for q in range(2):
                        k = 4 * c + 2 * j + q
                        m = dve.scalar_tensor_tensor(hT[:, k, TAPS // 2:TAPS // 2 + T], o[:, q * T:(q + 1) * T], PCOL[:, 1, 48 + k:49 + k],
                                                     SGC[:, i % 2, q * T:(q + 1) * T], ALU.add, ALU.mult)
                    free(m, f"pa{c}{j}")
                    step(dve.memset(junk, 0.0), "glu")
            dve.wait_ge(sem("operand_ready"), 5)
            late_at = [(0, 7), (0, 13), (0, 18), (0, 24)]
            taken = 0
            for half, width in enumerate((4, 3)):
                for tap in range(TAPS):
                    for q in range(width):
                        k = 4 * half + q
                        r = tap * KC + k
                        taken += 1
                        w = PCOL[:, 2 + r // P, r % P:r % P + 1]
                        if q == 0 and (half, tap) in late_at:
                            mod_job(LATE[late_at.index((half, tap))])
                        if tap == 0:
                            dve.tensor_scalar(T2[:, k, :], hT[:, k, 0:T], w, PCOL[:, 1, 40 + k:41 + k], ALU.mult, ALU.add
                                              ).then_inc(sem("tap"), 1)
                        else:
                            dve.wait_ge(sem("tap"), taken - width)
                            dve.scalar_tensor_tensor(T2[:, k, :], hT[:, k, tap:tap + T], w, T2[:, k, :], ALU.mult, ALU.add
                                                     ).then_inc(sem("tap"), 1)
                dve.wait_ge(sem("tap"), taken)
                step(dve.memset(junk, 0.0), "convolved")
            dve.wait_ge(sem("turned_read"), 4 * 7)
            dve.wait_ge(sem("params_in"), 16 * 5)
            step(layer_norm(XN, XN, RS[:, 1, :], RS[:, 2, :], EPS, D), "conv_normed")
            for f in GAP4:
                mod_job(f)
            step(gains(4, 1, 1, MODX[:, 1, 32:40]))
            for n in range(2):
                for t in range(TT):
                    o = take(f"pw2{n}{t}")
                    free(dve.tensor_tensor(XN[:, t, n * NCH:(n + 1) * NCH], o[:, :], RS[:, 3, n * NCH:(n + 1) * NCH], ALU.add), f"pw2{n}{t}")
                    m = piece_stats(XN, t, n)
            step(m)
            post(0, XN, pieces=False)
            rms(X)
            cnt["normed"] += 1
            scale_rows(XN, X)

            def ranks(dst, v):
                g, n = v.shape[1], v.shape[2]
                a = v.rearrange("p g (a j) -> p g a j", a=1).broadcast_to([P, g, n, n])
                b = v.rearrange("p g (e a) -> p g e a", a=1).broadcast_to([P, g, n, n])
                s0 = rk[:, 0, 0:g * n * n].rearrange("p (g e j) -> p g e j", g=g, e=n)
                s1 = rk[:, 1, 0:g * n * n].rearrange("p (g e j) -> p g e j", g=g, e=n)
                dve.tensor_tensor(s0, a, b, ALU.is_gt)
                step(dve.tensor_tensor(s1, a, b, ALU.is_equal))
                tri = tri8[:, 0:n, 0:n].rearrange("p (a e) j -> p a e j", a=1).broadcast_to([P, g, n, n])
                step(dve.tensor_tensor(s1, s1, tri, ALU.mult))
                step(dve.tensor_tensor(s0, s0, s1, ALU.add))
                step(dve.tensor_reduce(dst, s0, axis=AX.X, op=ALU.add))

            def clear_results():
                dve.memset(place[:, :, :], -1.0)
                dve.memset(YS, 0.0)
                step(dve.memset(PTM[:, :, :], 0.0))

            dve.memset(TOK[:, :, :], 0.0)
            clear_results()
            for f in GAP5:
                mod_job(f)
            o = take("rt1")
            free(dve.tensor_copy(gates[:, :, 0:NE1], o[:, 0:TT * NE1].rearrange("p (t e) -> p t e", t=TT)), "rt1")
            R1 = sm[:, 208:224].rearrange("p (t e) -> p t e", t=TT)
            ranks(R1, gates[:, :, 0:NE1])
            step(dve.tensor_scalar(sm[:, 208:224], sm[:, 208:224], 2.0, None, ALU.is_lt))
            step(dve.reduce_max(sm[:, 62:64], gates[:, :, 0:NE1], axis=AX.X))
            step(dve.tensor_scalar(sm[:, 60:62], sm[:, 62:64], -1.0, None, ALU.mult), "router_max")
            dve.wait_ge(sem("router_act"), 1)
            step(dve.tensor_tensor(gates[:, :, 0:NE1], gates[:, :, 0:NE1], R1, ALU.mult))
            step(dve.reduce_sum(sm[:, 62:64], gates[:, :, 0:NE1], axis=AX.X))
            step(dve.reciprocal(sm[:, 62:64], sm[:, 62:64]))
            for t in range(TT):
                m = dve.tensor_scalar(gates[:, t, 0:NE1], gates[:, t, 0:NE1], sm[:, 62 + t:63 + t], None, ALU.mult)
            step(m)

            def sort_tokens(m, mask):
                nb = m.bins
                step(dve.tensor_copy(chosen[:, :, 0:nb], mask), "bins_chosen")
                o = take(f"pos{m.name}")
                v = place[:, :, 0:nb]
                step(dve.scalar_tensor_tensor(v, o[:, 0:2 * nb].rearrange("p (t b) -> p t b", t=TT), 1.0, mask, ALU.add, ALU.mult))
                step(dve.tensor_scalar(v, v, -1.0, None, ALU.add))
                step(dve.reduce_max(sm[:, 300:301], o[:, 2 * nb:3 * nb], axis=AX.X))
                free(dve.memset(junk, 0.0), f"pos{m.name}")
                i = MOES.index(m)
                step(dve.tensor_scalar(flag[:, i:i + 1], sm[:, 300:301], float(SL), None, ALU.is_gt), "flag_ready")

            def moe(m):
                n = m.steps

                def pick(p, b, f):
                    dve.tensor_scalar(bplace[:, :], place[:, :, bass.ds(b, 1)].rearrange("p t a -> p (t a)"), 0.0, None, ALU.add)
                    dve.tensor_scalar(bgates[:, :, 0:m.experts], gates[:, :, bass.ds(b * m.experts, m.experts)], 1.0, None,
                                      ALU.mult).then_inc(sem("picked"), 1)
                    dve.wait_ge(sem("picked"), f + 1)
                    for t in range(TT):
                        i = dve.tensor_scalar(PM[:, p, t * SL:(t + 1) * SL], slots[:, 0, :], bplace[:, t:t + 1], None, ALU.is_equal)
                    i.then_inc(sem("placed"), 1)

                def add(f):
                    for g in range(4):
                        t, h = divmod(g, 2)
                        v = TOK[:, t, h * NCH:(h + 1) * NCH]
                        dve.wait_ge(sem("scattered"), 4 * f + (g + 1))
                        dve.tensor_tensor(v, banks[6 + h][:, :], v, ALU.add).then_inc(sem("added"), 1)

                def body(it):
                    for u in range(2):
                        g0 = it * (2 * n) + (m.u0 + u * n)
                        f = it * 2 + (m.f0 + u)
                        dve.wait_ge(sem("fetch_read"), 3 * f + 3)
                        for i in range(n):
                            q = (u * n + i) % 2
                            e = i // m.halves
                            dve.wait_ge(sem("silued"), g0 + (i + 1))
                            dve.wait_ge(sem("turned_h"), g0 + (i - 1))
                            dve.scalar_tensor_tensor(H[:, q, :], SG[:, q, :], sgates[:, u, e:e + 1], banks[q][:, FSTEP:NCH],
                                                     ALU.mult, ALU.mult).then_inc(sem("hidden"), 1)
                            if i == 0:
                                pick(1 - u, it * 2 + (u + 1), f + 1)
                            if i == 1:
                                add(f)

                pick(0, 0, m.f0)
                with dve.Fori(0, m.bins // 2) as it:
                    body(it)
                add(m.f0 + m.bins)

                def pick_bin(b):
                    dve.memset(junk, 0.0)
                    dve.tensor_scalar(bplace[:, :], place[:, :, bass.ds(b, 1)].rearrange("p t a -> p (t a)"), 0.0, None, ALU.add)
                    return dve.tensor_scalar(bgates[:, :, 0:m.experts], gates[:, :, bass.ds(b * m.experts, m.experts)], 1.0, None, ALU.mult)

                def one_hot(b):
                    dve.memset(YS, 0.0)
                    for t in range(TT):
                        i = dve.tensor_scalar(PM[:, 0, t * SL:(t + 1) * SL], slots[:, 1, :], bplace[:, t:t + 1], None, ALU.is_equal)
                    return i

                def product(b, c, h):
                    dve.memset(junk, 0.0)
                    g = sgates[:, 0, 0:1] if m is MOE1 else sgates[:, 0, bass.ds(c, 1)]
                    dve.tensor_scalar(sm[:, 302:303], g, 1.0, None, ALU.mult)
                    return dve.tensor_tensor(H[:, 0, :], SG[:, 0, :], banks[4][:, FSTEP:NCH], ALU.mult)

                def add_down(b, c, h):
                    for w in range(2):
                        v = YS[:, w * NCH:(w + 1) * NCH]
                        i = dve.scalar_tensor_tensor(v, banks[6 + w][:, :], sm[:, 302:303], v, ALU.mult, ALU.add)
                    return i

                def add_tokens(b):
                    for g in range(4):
                        t, w = divmod(g, 2)
                        v = TOK[:, t, w * NCH:(w + 1) * NCH]
                        i = dve.tensor_tensor(v, banks[g][:, :], v, ALU.add)
                    return i

                dve.wait_ge(sem("added"), 4 * (m.f0 + m.bins + 1) + 2)
                dve.memset(junk, 0.0).then_inc(sem(f"baton{m.name}"), 1)
                second_pass(dve, m, [(0, pick_bin), (1, one_hot)], [(2, product), (6, add_down)], [(1, add_tokens)], end=True)

            sort_tokens(MOE1, R1)
            for _ in range(2):
                step(dve.memset(junk, 0.0), "added")
            moe(MOE1)
            post(1, TOK)
            dve.wait_ge(sem("gelu_done"), 1)

            def memory_attention(units):
                def bias(h):
                    u = units + h
                    c = 2 * (u % 2)
                    dve.wait_ge(sem("mem_scored"), u + 1)
                    step(dve.reduce_max(sm[:, 44:46], banks[4 + h % 2][:, :].rearrange("p (t m) -> p t m", t=TT), axis=AX.X))
                    step(dve.tensor_scalar(sm[:, 48 + c:50 + c], sm[:, 44:46], -(P ** -0.5), None, ALU.mult), "mem_bias")

                bias(0)
                for h in range(XH):
                    u = units + h
                    c = 2 * (u % 2)
                    dve.wait_ge(sem("mem_exp"), 2 * u + 2)
                    step(dve.reciprocal(sm[:, 56:58], sm[:, 52 + c:54 + c]))
                    for t in range(TT):
                        m = dve.tensor_scalar(EM[:, h % 2, t, :], EM[:, h % 2, t, :], sm[:, 56 + t:57 + t], None, ALU.mult)
                    step(m, "mem_prob")
                    if h + 1 < XH:
                        bias(h + 1)

            memory_attention(0)
            b, k = bank_of["sguT"]
            dve.wait_ge(sem(f"bank_read{b}"), k + 1)
            step(dve.memset(sguT[64:P, :, 0:64], 0.0))
            dve.wait_ge(sem("params_in"), 16 * 8)
            V = UV[:, :, 1, :]
            step(layer_norm(V, V, RS[:, 0, 0:NCH], RS[:, 0, NCH:D], LN_EPS, NCH), "sgu_ready")
            for t in range(TT):
                o = take(f"sg{t}")
                for h in range(XH):
                    m = dve.scalar_tensor_tensor(TOK[:, t, h * P:(h + 1) * P], o[:, h * P:(h + 1) * P], PCOL[:, 1, 76 + h:77 + h],
                                                 UV[:, t, 0, h * P:(h + 1) * P], ALU.add, ALU.mult)
                free(m, f"sg{t}")
            step(dve.memset(junk, 0.0), "gated_tokens")

            def projected(name, rows):
                for n in range(2):
                    for t in range(TT):
                        o = take(f"wo{name}{n}{t}")
                        v = slice(n * NCH, (n + 1) * NCH)
                        free(dve.scalar_tensor_tensor(XN[:, t, v], X[:, t, v], ALPHA, o[:, :], ALU.mult, ALU.add), f"wo{name}{n}{t}")
                        m = piece_stats(XN, t, n)
                step(m)
                dve.wait_ge(sem("params_in"), 16 * rows)
                step(layer_norm(XN, X, RS[:, 1, :], RS[:, 2, :], LN_EPS, D, pieces=False), "x_updated")

            def group_router(name):
                b, k = bank_of[f"rt{name}"]
                dve.wait_ge(sem(f"bank_read{b}"), k + 1)
                sel = sm[:, 208:240].rearrange("p (t e) -> p t e", t=TT)
                m2 = sm[:, 240:272].rearrange("p (t e) -> p t e", t=TT)
                gs = sm[:, 272:280].rearrange("p (t g) -> p t g", t=TT)
                gr = sm[:, 280:288].rearrange("p (t g) -> p t g", t=TT)
                for t in range(TT):
                    m = dve.tensor_tensor(sel[:, t, :], gates[:, t, 0:NE2], rbias[:, :], ALU.add)
                step(m)
                ranks(sm[:, 240:272].rearrange("p (g e) -> p g e", e=GS), sm[:, 208:240].rearrange("p (g e) -> p g e", e=GS))
                step(dve.tensor_scalar(sm[:, 240:272], sm[:, 240:272], 2.0, None, ALU.is_lt))
                step(dve.tensor_tensor(sel, sel, m2, ALU.mult))
                step(dve.tensor_reduce(sm[:, 272:280], sm[:, 208:240].rearrange("p (g e) -> p g e", e=GS), axis=AX.X, op=ALU.add))
                ranks(gr, gs)
                step(dve.tensor_scalar(sm[:, 280:288], sm[:, 280:288], 1.0, None, ALU.is_lt))
                step(dve.tensor_tensor(sm[:, 240:272].rearrange("p (g e) -> p g e", e=GS), sm[:, 240:272].rearrange("p (g e) -> p g e", e=GS),
                                       sm[:, 280:288].rearrange("p (g a) -> p g a", a=1).broadcast_to([P, 2 * NG, GS]), ALU.mult))
                step(dve.tensor_tensor(gates[:, :, 0:NE2], gates[:, :, 0:NE2], m2, ALU.mult))
                step(dve.reduce_sum(sm[:, 62:64], gates[:, :, 0:NE2], axis=AX.X))
                step(dve.reciprocal(sm[:, 62:64], sm[:, 62:64]))
                for t in range(TT):
                    m = dve.tensor_scalar(gates[:, t, 0:NE2], gates[:, t, 0:NE2], sm[:, 62 + t:63 + t], None, ALU.mult)
                step(m)

            for l, name in ((0, "A"), (1, "B")):
                projected(name, 8 if l == 0 else 11)
                dve.tensor_scalar(TOK[:, :, :], X[:, :, :], ALPHA, None, ALU.mult)
                clear_results()
                group_router(name)
                m = MOEA if l == 0 else MOEB
                sort_tokens(m, sm[:, 280:288].rearrange("p (t g) -> p t g", t=TT))
                moe(m)
                dve.wait_ge(sem("params_in"), 16 * (11 if l == 0 else 13))
                step(layer_norm(TOK, X, RS[:, 3, :], RS[:, 0, :], LN_EPS, D), "x_updated")
                if l == 0:
                    dve.wait_ge(sem("margins"), 3)
                    dve.wait_ge(sem("conv_gates"), 1)
                    for j in range(2):
                        o = take(f"zb2{j}")
                        free(dve.tensor_tensor(hT2[:, 2 * j:2 * j + 2, 2:T + 2], cgT[:, 2 * j:2 * j + 2, :],
                                               o[:, :].rearrange("p (j t) -> p j t", j=2), ALU.mult), f"zb2{j}")
                    for k in range(4):
                        col = lambda tap: PCOL[:, 1, 64 + 4 * tap + k:65 + 4 * tap + k]
                        step(dve.tensor_scalar(cvB[:, 0, :], hT2[:, k, 0:T], col(0), None, ALU.mult))
                        for tap in (1, 2):
                            step(dve.scalar_tensor_tensor(cvB[:, 0, :], hT2[:, k, tap:tap + T], col(tap), cvB[:, 0, :], ALU.mult, ALU.add))
                        step(dve.tensor_tensor(T2[:, k, :], cvB[:, 0, :], bgT[:, k, :], ALU.mult))
                    memory_attention(XH)
                    dve.wait_ge(sem("mem_out"), 2 * XH)
                    dve.wait_ge(sem("cat_ready"), 1)
                    dve.memset(junk, 0.0).then_inc(sem("cat_ready"), 1)


def rope_table():
    width, axis = 64, 32
    rows = T // width
    r = np.repeat(np.arange(rows, dtype=np.float32), width)
    c = np.tile(np.arange(width, dtype=np.float32), rows)
    inv = (np.float32(10000.0) ** (-np.arange(0, axis, 2, dtype=np.float32) / np.float32(axis))).astype(np.float32)
    parts = []
    for f, sign in ((np.cos, 1), (np.sin, -1)):
        cols = []
        for pos in (r, c):
            a = f(pos[:, None] * inv).astype(np.float32)
            cols += [sign * a, a]
        parts.append(np.concatenate(cols, axis=1))
    return np.stack(parts, axis=1).astype(np.float32)


def kernel(**inputs):
    import concourse.bacc as _bacc
    from concourse.bass_utils import run_bass_kernel_spmd as _run

    nc = _bacc.Bacc("TRN2", target_bir_lowering=False, num_devices=1)
    arrays, args = {}, {}
    for name, a in inputs.items():
        arrays[f"in_{name}"] = np.ascontiguousarray(a)
    arrays["in_rope"] = rope_table()
    for name, a in arrays.items():
        args[name[3:]] = nc.dram_tensor(name, a.shape, mybir.dt.from_np(a.dtype), kind="ExternalInput").ap()
    out = nc.dram_tensor("out_0", (1, T, D), F32, kind="ExternalOutput").ap()
    two_blocks(nc, args, out)
    r = _run(nc, [arrays], core_ids=[0])
    return r.results[0]["out_0"]
```
